# Optimizing a Trainium2 kernel written in Bass

```python
import math
import jax, jax.numpy as jnp
from jax import lax
import numpy as np

D_MODEL = 1024
BATCH = 1
SEQ = 256
DEPTH = 1

HEAD_DIM = 64
HEADS_DIFF = 4
HEADS_MOBA = 8
N_HEADS_TOTAL = HEADS_DIFF + HEADS_MOBA
DIFF_WIDTH = HEADS_DIFF * 2 * HEAD_DIM
MOBA_WIDTH = HEADS_MOBA * HEAD_DIM
MIX_WIDTH = DIFF_WIDTH + MOBA_WIDTH
IN_PROJ_WIDTH = 3 * MIX_WIDTH
DIFF_Q_BLOCK = 128
MOBA_BLOCK = 256
MOBA_TOPK = 3
MOBA_Q_CHUNK = 16
NUM_BUCKETS = 32
MAX_DISTANCE = 2048
N_GROUPS = 4
EXPERTS_PER_GROUP = 8
N_EXPERTS = N_GROUPS * EXPERTS_PER_GROUP
EXPERTS_PER_TOKEN = 2
EXPERT_HIDDEN = 256
DISPATCH_CHUNK = 256
RMS_EPS = 1e-6
NEG_INF = -1e30


def rms_norm(x, g):
    xf = x.astype(jnp.float32)
    y = xf * lax.rsqrt(jnp.mean(xf * xf, axis=-1, keepdims=True) + RMS_EPS)
    return (y * g.astype(jnp.float32)).astype(x.dtype)

def t5_bucket(dist):
    n = jnp.maximum(dist, 0)
    max_exact = NUM_BUCKETS // 2
    nf = jnp.maximum(n, 1).astype(jnp.float32)
    large = max_exact + (jnp.log(nf / max_exact) / math.log(MAX_DISTANCE / max_exact)
                         * (NUM_BUCKETS - max_exact)).astype(jnp.int32)
    large = jnp.minimum(large, NUM_BUCKETS - 1)
    return jnp.where(n < max_exact, n, large)

def diff_attention(q, k, v, q_g, k_g, lq1, lk1, lq2, lk2, sub_g, bias_table, lambda_init):
    B, S, H = q.shape[:3]
    q = rms_norm(q, q_g).transpose(0, 2, 3, 1, 4)
    k = rms_norm(k, k_g).transpose(0, 2, 3, 1, 4)
    v = v.transpose(0, 2, 1, 3)
    f32 = jnp.float32
    lam = (jnp.exp(jnp.sum(lq1.astype(f32) * lk1.astype(f32)))
           - jnp.exp(jnp.sum(lq2.astype(f32) * lk2.astype(f32))) + lambda_init)
    scale = HEAD_DIM ** -0.5
    kpos = jnp.arange(S)

    def block(i):
        s0 = i * DIFF_Q_BLOCK
        qb = lax.dynamic_slice_in_dim(q, s0, DIFF_Q_BLOCK, axis=3)
        logits = jnp.einsum('bhmqd,bhmkd->bhmqk', qb, k, preferred_element_type=f32) * scale
        dist = (s0 + jnp.arange(DIFF_Q_BLOCK))[:, None] - kpos[None, :]
        bias = bias_table[t5_bucket(dist)].astype(f32).transpose(2, 0, 1)
        logits = jnp.where(dist >= 0, logits + bias[None, :, None], NEG_INF)
        p = jax.nn.softmax(logits, axis=-1)
        w = p[:, :, 0] - lam * p[:, :, 1]
        return jnp.einsum('bhqk,bhkc->bhqc', w.astype(v.dtype), v)

    out = lax.map(block, jnp.arange(S // DIFF_Q_BLOCK))
    out = out.transpose(1, 0, 3, 2, 4).reshape(B, S, H, 2 * HEAD_DIM)
    out = rms_norm(out, sub_g) * (1.0 - lambda_init)
    return out.reshape(B, S, H * 2 * HEAD_DIM)

def moba_attention(q, k, v, q_g, k_g, bias_table):
    B, S, H, d = q.shape
    f32 = jnp.float32
    q = rms_norm(q, q_g).transpose(0, 2, 1, 3)
    k = rms_norm(k, k_g).transpose(0, 2, 1, 3)
    v = v.transpose(0, 2, 1, 3)
    n_kb = -(-S // MOBA_BLOCK)
    pad = n_kb * MOBA_BLOCK - S
    k_blocks = jnp.pad(k, ((0, 0), (0, 0), (0, pad), (0, 0))).reshape(B, H, n_kb, MOBA_BLOCK, d)
    v_blocks = jnp.pad(v, ((0, 0), (0, 0), (0, pad), (0, 0))).reshape(B, H, n_kb, MOBA_BLOCK, d)
    k_mean = jnp.mean(k_blocks.astype(f32), axis=3)
    top = min(MOBA_TOPK, n_kb)
    scale = HEAD_DIM ** -0.5
    bi = jnp.arange(B)[:, None, None, None]
    hi = jnp.arange(H)[None, :, None, None]
    blk_off = jnp.arange(MOBA_BLOCK)

    def chunk(i):
        s0 = i * MOBA_Q_CHUNK
        qc = lax.dynamic_slice_in_dim(q, s0, MOBA_Q_CHUNK, axis=2)
        qpos = s0 + jnp.arange(MOBA_Q_CHUNK)
        own = s0 // MOBA_BLOCK
        gate = jnp.einsum('bhqd,bhnd->bhqn', qc.astype(f32), k_mean)
        gate = jnp.where(jnp.arange(n_kb) < own, gate, NEG_INF)
        _, sel = lax.top_k(gate, top)
        sel_valid = jnp.arange(top)[:, None] < own
        k_sel = k_blocks[bi, hi, sel]
        v_sel = v_blocks[bi, hi, sel]
        sel_logits = jnp.einsum('bhqd,bhqtkd->bhqtk', qc, k_sel, preferred_element_type=f32) * scale
        sel_pos = sel[..., None] * MOBA_BLOCK + blk_off
        sel_bias = bias_table[t5_bucket(qpos[:, None, None] - sel_pos), hi[..., None]].astype(f32)
        sel_logits = jnp.where(sel_valid, sel_logits + sel_bias, NEG_INF)
        k_own = lax.dynamic_index_in_dim(k_blocks, own, axis=2, keepdims=False)
        v_own = lax.dynamic_index_in_dim(v_blocks, own, axis=2, keepdims=False)
        dist_own = qpos[:, None] - (own * MOBA_BLOCK + blk_off)[None, :]
        own_bias = bias_table[t5_bucket(dist_own)].astype(f32).transpose(2, 0, 1)[None]
        own_logits = jnp.einsum('bhqd,bhkd->bhqk', qc, k_own, preferred_element_type=f32) * scale
        own_logits = jnp.where(dist_own >= 0, own_logits + own_bias, NEG_INF)
        logits = jnp.concatenate([sel_logits.reshape(B, H, MOBA_Q_CHUNK, top * MOBA_BLOCK), own_logits], axis=-1)
        p = jax.nn.softmax(logits, axis=-1).astype(v.dtype)
        p_sel = p[..., :top * MOBA_BLOCK].reshape(B, H, MOBA_Q_CHUNK, top, MOBA_BLOCK)
        p_own = p[..., top * MOBA_BLOCK:]
        return (jnp.einsum('bhqtk,bhqtkd->bhqd', p_sel, v_sel)
                + jnp.einsum('bhqk,bhkd->bhqd', p_own, v_own))

    out = lax.map(chunk, jnp.arange(S // MOBA_Q_CHUNK))
    return out.transpose(1, 0, 3, 2, 4).reshape(B, S, H * d)

def hier_moe(h, router_group, router_expert, w_gate, w_up, w_down):
    B, S, D = h.shape
    N = B * S
    t = h.reshape(N, D)
    f32 = jnp.float32
    g_logits = (t @ router_group).astype(f32)
    g_prob = jax.nn.softmax(g_logits, axis=-1)
    g = jnp.argmax(g_logits, axis=-1)
    p_group = jnp.take_along_axis(g_prob, g[:, None], axis=-1)
    e_logits_all = jnp.einsum('nd,gde->nge', t, router_expert).astype(f32)
    e_logits = jnp.take_along_axis(e_logits_all, g[:, None, None], axis=1)[:, 0]
    top_v, top_e = lax.top_k(e_logits, EXPERTS_PER_TOKEN)
    weight = p_group * jax.nn.softmax(top_v, axis=-1)
    expert_id = g[:, None] * EXPERTS_PER_GROUP + top_e
    A = N * EXPERTS_PER_TOKEN
    C = DISPATCH_CHUNK
    eid = expert_id.reshape(A)
    tok = jnp.repeat(jnp.arange(N, dtype=jnp.int32), EXPERTS_PER_TOKEN)
    w_flat = weight.reshape(A)
    order = jnp.argsort(eid)
    eid_s, tok_s, w_s = eid[order], tok[order], w_flat[order]
    counts = jax.ops.segment_sum(jnp.ones((A,), jnp.int32), eid, num_segments=N_EXPERTS)
    start = jnp.cumsum(counts) - counts
    pad_counts = ((counts + C - 1) // C) * C
    pad_end = jnp.cumsum(pad_counts)
    pad_start = pad_end - pad_counts
    dest = pad_start[eid_s] + (jnp.arange(A, dtype=jnp.int32) - start[eid_s])
    P = A + N_EXPERTS * C
    n_chunks = P // C
    slot_tok = jnp.zeros((P,), jnp.int32).at[dest].set(tok_s)
    slot_w = jnp.zeros((P,), f32).at[dest].set(w_s)
    chunk_e = jnp.minimum(jnp.searchsorted(pad_end, jnp.arange(n_chunks) * C, side='right'), N_EXPERTS - 1)

    def run(args):
        e, toks = args
        xc = t[toks]
        hid = jax.nn.silu(xc @ w_gate[e]) * (xc @ w_up[e])
        return hid @ w_down[e]

    out = lax.map(run, (chunk_e, slot_tok.reshape(n_chunks, C))).reshape(P, D)
    y = jnp.zeros((N, D), t.dtype).at[slot_tok].add((out * slot_w[:, None]).astype(t.dtype))
    return y.reshape(B, S, D)

def first_inputs(seed: int = 0) -> dict:
    key = jax.random.key(seed)
    ks = jax.random.split(key, 20)
    f32 = jnp.float32

    def nrm(k, shape, scale):
        return jax.random.normal(k, shape, f32) * scale

    def gain(k, shape):
        return 1.0 + 0.05 * jax.random.normal(k, shape, f32)

    return {
        'x': nrm(ks[0], (BATCH, SEQ, D_MODEL), 1.0),
        'norm1_g': gain(ks[1], (DEPTH, D_MODEL)),
        'w_in': nrm(ks[2], (DEPTH, D_MODEL, IN_PROJ_WIDTH), D_MODEL ** -0.5),
        'diff_q_g': gain(ks[3], (DEPTH, HEAD_DIM)),
        'diff_k_g': gain(ks[4], (DEPTH, HEAD_DIM)),
        'lambda_q1': nrm(ks[5], (DEPTH, HEAD_DIM), 0.1),
        'lambda_k1': nrm(ks[6], (DEPTH, HEAD_DIM), 0.1),
        'lambda_q2': nrm(ks[7], (DEPTH, HEAD_DIM), 0.1),
        'lambda_k2': nrm(ks[8], (DEPTH, HEAD_DIM), 0.1),
        'diff_sub_g': gain(ks[9], (DEPTH, 2 * HEAD_DIM)),
        'moba_q_g': gain(ks[10], (DEPTH, HEAD_DIM)),
        'moba_k_g': gain(ks[11], (DEPTH, HEAD_DIM)),
        'rel_bias': nrm(ks[12], (NUM_BUCKETS, N_HEADS_TOTAL), 0.5),
        'w_out': nrm(ks[13], (DEPTH, MIX_WIDTH, D_MODEL), MIX_WIDTH ** -0.5),
        'norm2_g': gain(ks[14], (DEPTH, D_MODEL)),
        'router_group': nrm(ks[15], (DEPTH, D_MODEL, N_GROUPS), D_MODEL ** -0.5),
        'router_expert': nrm(ks[16], (DEPTH, N_GROUPS, D_MODEL, EXPERTS_PER_GROUP), D_MODEL ** -0.5),
        'w_gate': nrm(ks[17], (DEPTH, N_EXPERTS, D_MODEL, EXPERT_HIDDEN), D_MODEL ** -0.5),
        'w_up': nrm(ks[18], (DEPTH, N_EXPERTS, D_MODEL, EXPERT_HIDDEN), D_MODEL ** -0.5),
        'w_down': nrm(ks[19], (DEPTH, N_EXPERTS, EXPERT_HIDDEN, D_MODEL), EXPERT_HIDDEN ** -0.5),
    }

def first_block(x, norm1_g, w_in, diff_q_g, diff_k_g, lambda_q1, lambda_k1, lambda_q2, lambda_k2,
              diff_sub_g, moba_q_g, moba_k_g, rel_bias, w_out, norm2_g, router_group,
              router_expert, w_gate, w_up, w_down):
    B, S, _ = x.shape
    bias_diff = rel_bias[:, :HEADS_DIFF]
    bias_moba = rel_bias[:, HEADS_DIFF:]
    splits = [DIFF_WIDTH, 2 * DIFF_WIDTH, 3 * DIFF_WIDTH,
              3 * DIFF_WIDTH + MOBA_WIDTH, 3 * DIFF_WIDTH + 2 * MOBA_WIDTH]
    for layer in range(DEPTH):
        lambda_init = 0.8 - 0.6 * math.exp(-0.3 * layer)
        h = rms_norm(x, norm1_g[layer])
        proj = h @ w_in[layer]
        q_d, k_d, v_d, q_m, k_m, v_m = jnp.split(proj, splits, axis=-1)
        y_d = diff_attention(q_d.reshape(B, S, HEADS_DIFF, 2, HEAD_DIM),
                             k_d.reshape(B, S, HEADS_DIFF, 2, HEAD_DIM),
                             v_d.reshape(B, S, HEADS_DIFF, 2 * HEAD_DIM),
                             diff_q_g[layer], diff_k_g[layer], lambda_q1[layer], lambda_k1[layer],
                             lambda_q2[layer], lambda_k2[layer], diff_sub_g[layer], bias_diff, lambda_init)
        y_m = moba_attention(q_m.reshape(B, S, HEADS_MOBA, HEAD_DIM),
                             k_m.reshape(B, S, HEADS_MOBA, HEAD_DIM),
                             v_m.reshape(B, S, HEADS_MOBA, HEAD_DIM),
                             moba_q_g[layer], moba_k_g[layer], bias_moba)
        x = x + jnp.concatenate([y_d, y_m], axis=-1) @ w_out[layer]
        x = x + hier_moe(rms_norm(x, norm2_g[layer]), router_group[layer], router_expert[layer],
                         w_gate[layer], w_up[layer], w_down[layer])
    return x


DEPTH_2 = 2

N_A = DEPTH_2 // 2
N_B = DEPTH_2 - N_A

EXPAND = 2
D_INNER = EXPAND * D_MODEL
SSM_HEAD_DIM = 64
SSM_HEADS = D_INNER // SSM_HEAD_DIM
HEADS_PER_GROUP = SSM_HEADS // N_GROUPS
D_STATE = 128
CONV_K = 4
CONV_DIM = D_INNER + 2 * N_GROUPS * D_STATE
IN_PROJ_DIM = 2 * D_INNER + 2 * N_GROUPS * D_STATE + SSM_HEADS
CHUNK = 128
DT_MIN = 0.001
DT_MAX = 0.1

SB_HEAD_DIM = 64
SB_HEADS = D_MODEL // SB_HEAD_DIM
SB_WIDTH = SB_HEADS * SB_HEAD_DIM
SB_BLOCK = 128

PLE_DIM = 256

NORM_EPS = 1e-6


def rms(x):
    xf = x.astype(jnp.float32)
    return (xf * lax.rsqrt(jnp.mean(xf * xf, axis=-1, keepdims=True) + NORM_EPS)).astype(x.dtype)

def rmsnorm(x, g):
    return rms(x) * g.astype(x.dtype)

def causal_depthwise_conv(u, w, b):
    k = w.shape[0]
    s = u.shape[1]
    up = jnp.pad(u, ((0, 0), (k - 1, 0), (0, 0)))
    out = b
    for j in range(k):
        out = out + w[j] * up[:, j:j + s]
    return out

def ssd_chunked_scan(xs, dt, A, Bm, Cm):
    bsz, s, _, _ = xs.shape
    nc = s // CHUNK
    G, HG, P, N, L = N_GROUPS, HEADS_PER_GROUP, SSM_HEAD_DIM, D_STATE, CHUNK
    xc = xs.astype(jnp.float32).reshape(bsz, nc, L, G, HG, P).transpose(1, 0, 2, 3, 4, 5)
    dtc = dt.reshape(bsz, nc, L, G, HG).transpose(1, 0, 2, 3, 4)
    Bc = Bm.astype(jnp.float32).reshape(bsz, nc, L, G, N).transpose(1, 0, 2, 3, 4)
    Cc = Cm.astype(jnp.float32).reshape(bsz, nc, L, G, N).transpose(1, 0, 2, 3, 4)
    Ag = A.reshape(G, HG)
    causal = jnp.tril(jnp.ones((L, L), dtype=bool))

    def step(state, inp):
        x_k, dt_k, B_k, C_k = inp
        acum = jnp.cumsum(dt_k * Ag, axis=1)
        seg = acum[:, :, None] - acum[:, None, :]
        decay = jnp.exp(jnp.where(causal[None, :, :, None, None], seg, -jnp.inf))
        xdt = x_k * dt_k[..., None]
        cb = jnp.einsum('blgn,bsgn->blsg', C_k, B_k)
        y_intra = jnp.einsum('blsgh,bsghp->blghp', cb[..., None] * decay, xdt)
        y_inter = jnp.einsum('blgn,bghpn->blghp', C_k, state) * jnp.exp(acum)[..., None]
        to_end = jnp.exp(acum[:, -1:] - acum)
        new_state = state * jnp.exp(acum[:, -1])[..., None, None] + jnp.einsum(
            'bsgn,bsghp->bghpn', B_k, xdt * to_end[..., None])
        return new_state, y_intra + y_inter

    state0 = jnp.zeros((bsz, G, HG, P, N), jnp.float32)
    _, y = lax.scan(step, state0, (xc, dtc, Bc, Cc))
    y = y.transpose(1, 0, 2, 3, 4, 5).reshape(bsz, s, SSM_HEADS, P)
    return y.astype(xs.dtype)

def mamba2_mixer(h, norm_g, w_in, conv_w, conv_b, dt_bias, A_log, d_skip, y_g, w_out):
    bsz, s, _ = h.shape
    u = rmsnorm(h, norm_g)
    zxbcdt = u @ w_in
    z = zxbcdt[..., :D_INNER]
    xbc = zxbcdt[..., D_INNER:D_INNER + CONV_DIM]
    dt = zxbcdt[..., D_INNER + CONV_DIM:]
    xbc = jax.nn.silu(causal_depthwise_conv(xbc, conv_w, conv_b))
    xs = xbc[..., :D_INNER].reshape(bsz, s, SSM_HEADS, SSM_HEAD_DIM)
    Bm = xbc[..., D_INNER:D_INNER + N_GROUPS * D_STATE].reshape(bsz, s, N_GROUPS, D_STATE)
    Cm = xbc[..., D_INNER + N_GROUPS * D_STATE:].reshape(bsz, s, N_GROUPS, D_STATE)
    dt = jax.nn.softplus(dt.astype(jnp.float32) + dt_bias.astype(jnp.float32))
    A = -jnp.exp(A_log.astype(jnp.float32))
    y = ssd_chunked_scan(xs, dt, A, Bm, Cm)
    y = y + d_skip.astype(y.dtype)[:, None] * xs
    y = y.reshape(bsz, s, D_INNER) * jax.nn.silu(z)
    y = rms(y.reshape(bsz, s, N_GROUPS, D_INNER // N_GROUPS)).reshape(bsz, s, D_INNER) * y_g
    return y @ w_out

def shared_kv(h, norm_g, w_kv, k_g):
    bsz, s, _ = h.shape
    kv = rmsnorm(h, norm_g) @ w_kv
    k = rmsnorm(kv[..., :SB_WIDTH].reshape(bsz, s, SB_HEADS, SB_HEAD_DIM), k_g)
    v = kv[..., SB_WIDTH:].reshape(bsz, s, SB_HEADS, SB_HEAD_DIM)
    return k.transpose(0, 2, 1, 3), v.transpose(0, 2, 1, 3)

def stick_breaking_mixer(h, k, v, norm_g, w_in, q_g, w_out):
    bsz, s, _ = h.shape
    qg = rmsnorm(h, norm_g) @ w_in
    gate = qg[..., SB_WIDTH:]
    q = rmsnorm(qg[..., :SB_WIDTH].reshape(bsz, s, SB_HEADS, SB_HEAD_DIM), q_g)
    q = (q * (1.0 / math.sqrt(SB_HEAD_DIM))).transpose(0, 2, 1, 3)
    outs = []
    for blk in range(s // SB_BLOCK):
        q0 = blk * SB_BLOCK
        kend = q0 + SB_BLOCK
        z = jnp.einsum('bhtd,bhsd->bhts', q[:, :, q0:kend], k[:, :, :kend]).astype(jnp.float32)
        t_idx = q0 + jnp.arange(SB_BLOCK)[:, None]
        s_idx = jnp.arange(kend)[None, :]
        strict = s_idx < t_idx
        log_keep = jnp.where(strict, jax.nn.log_sigmoid(-z), 0.0)
        suffix = lax.cumsum(log_keep, axis=3, reverse=True) - log_keep
        weights = jnp.where(strict, jnp.exp(jax.nn.log_sigmoid(z) + suffix), 0.0)
        outs.append(jnp.einsum('bhts,bhsd->bhtd', weights.astype(v.dtype), v[:, :, :kend]))
    o = jnp.concatenate(outs, axis=2).transpose(0, 2, 1, 3).reshape(bsz, s, SB_WIDTH)
    return (o * jax.nn.silu(gate)) @ w_out

def per_layer_embedding(h, p_i, norm_g, w_gate, w_proj):
    return h + (p_i @ w_proj) * jax.nn.sigmoid(rmsnorm(h, norm_g) @ w_gate)

def second_inputs(seed: int = 0) -> dict:
    key = jax.random.key(seed)
    ks = jax.random.split(key, 24)

    def nrm(k, shape, scale):
        return jax.random.normal(k, shape, jnp.float32) * scale

    def gain(k, shape):
        return 1.0 + 0.05 * jax.random.normal(k, shape, jnp.float32)

    u = jax.random.uniform(ks[6], (N_A, SSM_HEADS), jnp.float32)
    dt = jnp.exp(u * (math.log(DT_MAX) - math.log(DT_MIN)) + math.log(DT_MIN))
    dt_bias = dt + jnp.log(-jnp.expm1(-dt))
    A_log = jnp.log(jax.random.uniform(ks[7], (N_A, SSM_HEADS), jnp.float32, minval=1.0, maxval=16.0))
    return {
        "x": nrm(ks[0], (BATCH, SEQ, D_MODEL), 1.0),
        "p": nrm(ks[1], (DEPTH_2, BATCH, SEQ, PLE_DIM), 1.0),
        "m_norm": gain(ks[2], (N_A, D_MODEL)),
        "m_in": nrm(ks[3], (N_A, D_MODEL, IN_PROJ_DIM), D_MODEL ** -0.5),
        "m_conv_w": nrm(ks[4], (N_A, CONV_K, CONV_DIM), CONV_K ** -0.5),
        "m_conv_b": nrm(ks[5], (N_A, CONV_DIM), 0.01),
        "m_dt_bias": dt_bias,
        "m_A_log": A_log,
        "m_D": gain(ks[8], (N_A, SSM_HEADS)),
        "m_ynorm": gain(ks[9], (N_A, D_INNER)),
        "m_out": nrm(ks[10], (N_A, D_INNER, D_MODEL), D_INNER ** -0.5),
        "kv_norm": gain(ks[11], (D_MODEL,)),
        "w_kv": nrm(ks[12], (D_MODEL, 2 * SB_WIDTH), D_MODEL ** -0.5),
        "k_norm": gain(ks[13], (SB_HEAD_DIM,)),
        "s_norm": gain(ks[14], (N_B, D_MODEL)),
        "s_in": nrm(ks[15], (N_B, D_MODEL, 2 * SB_WIDTH), D_MODEL ** -0.5),
        "q_norm": gain(ks[16], (N_B, SB_HEAD_DIM)),
        "s_out": nrm(ks[17], (N_B, SB_WIDTH, D_MODEL), SB_WIDTH ** -0.5),
        "ple_norm": gain(ks[18], (DEPTH_2, D_MODEL)),
        "ple_gate": nrm(ks[19], (DEPTH_2, D_MODEL, D_MODEL), D_MODEL ** -0.5),
        "ple_proj": nrm(ks[20], (DEPTH_2, PLE_DIM, D_MODEL), PLE_DIM ** -0.5),
    }

def second_block(x, p, m_norm, m_in, m_conv_w, m_conv_b, m_dt_bias, m_A_log, m_D, m_ynorm, m_out,
              kv_norm, w_kv, k_norm, s_norm, s_in, q_norm, s_out, ple_norm, ple_gate, ple_proj):
    h = x
    k = v = None
    for i in range(DEPTH_2):
        if i < N_A:
            h = h + mamba2_mixer(h, m_norm[i], m_in[i], m_conv_w[i], m_conv_b[i], m_dt_bias[i],
                                 m_A_log[i], m_D[i], m_ynorm[i], m_out[i])
        else:
            if i == N_A:
                k, v = shared_kv(h, kv_norm, w_kv, k_norm)
            j = i - N_A
            h = h + stick_breaking_mixer(h, k, v, s_norm[j], s_in[j], q_norm[j], s_out[j])
        h = per_layer_embedding(h, p[i], ple_norm[i], ple_gate[i], ple_proj[i])
    return h


def setup_inputs(seed=0):
    out = dict(first_inputs(seed))
    for name, value in second_inputs(seed + 1).items():
        if name != "x":
            out[name + "_2"] = value
    return out


def reference(
    x, norm1_g, w_in, diff_q_g, diff_k_g, lambda_q1, lambda_k1, lambda_q2, lambda_k2,
    diff_sub_g, moba_q_g, moba_k_g, rel_bias, w_out, norm2_g, router_group, router_expert,
    w_gate, w_up, w_down, p_2, m_norm_2, m_in_2, m_conv_w_2, m_conv_b_2, m_dt_bias_2, m_A_log_2,
    m_D_2, m_ynorm_2, m_out_2, kv_norm_2, w_kv_2, k_norm_2, s_norm_2, s_in_2, q_norm_2, s_out_2,
    ple_norm_2, ple_gate_2, ple_proj_2,
):
    x = first_block(
        x, norm1_g, w_in, diff_q_g, diff_k_g, lambda_q1, lambda_k1, lambda_q2, lambda_k2,
        diff_sub_g, moba_q_g, moba_k_g, rel_bias, w_out, norm2_g, router_group, router_expert,
        w_gate, w_up, w_down,
    )
    return second_block(
        x, p_2, m_norm_2, m_in_2, m_conv_w_2, m_conv_b_2, m_dt_bias_2, m_A_log_2, m_D_2,
        m_ynorm_2, m_out_2, kv_norm_2, w_kv_2, k_norm_2, s_norm_2, s_in_2, q_norm_2, s_out_2,
        ple_norm_2, ple_gate_2, ple_proj_2,
    )


_drawn_inputs = setup_inputs


def setup_inputs(seed=0):
    import zlib

    import numpy as np

    out = dict(_drawn_inputs(seed))
    spreads = {}
    factors = {'lambda_q1': 8.0,
     'moba_q_g': 3.306,
     'moba_k_g': 3.092,
     'm_conv_b_2': 6.623,
     'm_D_2': 2.779,
     'kv_norm_2': 4.254,
     'k_norm_2': 8.0,
     's_norm_2': 4.474,
     'q_norm_2': 8.0,
     'ple_norm_2': 6.426}
    for name, (base, spread) in spreads.items():
        noise = np.random.default_rng([zlib.crc32(name.encode()), seed]).standard_normal(out[name].shape)
        drawn = base * np.exp(spread * noise) if base else spread * noise
        out[name] = __import__('jax').numpy.asarray(drawn.astype(out[name].dtype))
    for name, factor in factors.items():
        out[name] = (out[name] * factor).astype(out[name].dtype)
    return out
```

```python
import math
from contextlib import ExitStack

import numpy as np

import concourse.bass as bass
from concourse import mybir

F32 = mybir.dt.float32
I32 = mybir.dt.int32
ALU = mybir.AluOpType
ACT = mybir.ActivationFunctionType
AX = mybir.AxisListType

P = 128
D = 1024
S = 256
TT = S // P
KT = D // P
HD = 64
DIFF_HEADS, MOBA_HEADS = 4, 8
UNITS = DIFF_HEADS + MOBA_HEADS
MAPS = 2 * DIFF_HEADS + MOBA_HEADS
BUCKETS, MAX_DISTANCE = 32, 2048
EXPERTS, GROUPS, PER_GROUP, HIDDEN = 32, 4, 8, 256
SLOTS = 32
QUAD = 4
QUADS = EXPERTS // QUAD
D_INNER, SSM_HEADS, CONV_K = 2048, 32, 4
CONV_TILES = 24
SB_HEADS = 16
EPS = 1e-6
NEG = -1e30
LAMBDA_INIT = 0.8 - 0.6 * math.exp(-0.3 * 0)

RING = 12
UNIT = 2048
UNITS_A = 16
UNITS_B = 58


def bucket_onehot():
    out = np.zeros((BUCKETS + 1, 384), np.float32)
    exact = BUCKETS // 2
    for i in range(384):
        n = S - 1 - i
        if n < 0:
            out[BUCKETS, i] = NEG
            continue
        b = n if n < exact else min(BUCKETS - 1, exact + int(
            math.log(n / exact) / math.log(MAX_DISTANCE / exact) * (BUCKETS - exact)))
        out[b, i] = 1.0
    return out


CONSTS = ["ident", "tri_le", "tri_lt", "flip", "sufneg", "negones", "ones", "segmask", "strictmask", "fold", "iota", "iota_low", "passes", "neghalf"]


def constants():
    a, b = np.arange(P)[:, None], np.arange(P)[None, :]
    parts = {
        "ident": a == b, "tri_le": a <= b, "tri_lt": a < b, "flip": a + b == P - 1,
        "sufneg": -1.0 * (a >= b), "negones": -np.ones((P, P)), "ones": np.ones((P, P)),
        "segmask": np.where(a <= b, 0.0, NEG),
        "strictmask": np.where(a < b, 0.0, NEG),
        "fold": (a % SLOTS) == np.arange(SLOTS)[None, :],
        "iota": np.broadcast_to(np.arange(32.0), (P, 32)),
        "iota_low": np.broadcast_to(np.arange(32.0) - 99.0, (P, 32)),
        "passes": np.broadcast_to(SLOTS * np.arange(8.0), (P, 8)),
        "neghalf": np.full((P, 8), -0.5),
    }
    at, col = {}, 0
    for name in CONSTS:
        at[name] = (col, parts[name].shape[1])
        col += parts[name].shape[1]
    return np.concatenate([np.asarray(parts[n], np.float32) for n in CONSTS], 1), at


def two_blocks(nc, d, out):
    _, const_at = constants()
    n_const = sum(w for _, w in const_at.values())
    ctx = ExitStack()
    with ctx:
        def sb(name, shape, dt=F32):
            return ctx.enter_context(nc.sbuf_tensor(name, shape, dt))

        def sem(name):
            return ctx.enter_context(nc.semaphore(name))

        ring = sb("ring", [P, RING, UNIT])
        consts = sb("consts", [P, n_const])
        x = sb("x_residual", [P, TT, D])
        hn = sb("hn", [P, TT, D])
        hT = sb("hT", [P, KT, S])
        gcol = sb("gcol", [P, 96])
        ccol = sb("ccol", [P, 96])
        g2 = sb("g2", [P, KT])
        gq = sb("gq", [P, 3])
        ga = sb("ga", [P, KT])
        headp = sb("headp", [P, 3, SSM_HEADS])
        nlam = sb("nlam", [P, 1])
        ss = sb("ss", [P, TT])
        rs = sb("rs", [P, TT])
        pbuf = sb("pbuf", [P, TT, 256])
        counts_i = sb("counts_i", [P, 2], I32)
        arena = sb("arena", [P, 19776])
        banks = [ctx.enter_context(nc.psum_tensor(f"bank{i}", [P, 512], F32)) for i in range(8)]

        def C(name):
            at, n = const_at[name]
            return consts[:, at:at + n]

        class Arena:
            def __init__(self):
                self.at = 0

            def __call__(self, *dims):
                n = math.prod(dims)
                v = arena[:, self.at:self.at + n]
                self.at += n
                assert self.at <= 19776
                if len(dims) == 2:
                    v = v.rearrange("p (a b) -> p a b", a=dims[0])
                if len(dims) == 3:
                    v = v.rearrange("p (a b c) -> p a b c", a=dims[0], b=dims[1])
                return v

        def over(ap, *dims):
            n = ap.shape[1]
            return ap.unsqueeze(2).to_broadcast([P, n, dims[0]])

        def repeat(ap, n):
            return ap.unsqueeze(1).to_broadcast([P, n, ap.shape[1]])

        def cols(ap, n):
            return ap.rearrange("p (a b) -> p a b", a=n)

        GAIN = {"norm1": 0, "m_norm": 8, "kv": 16, "s_norm": 24, "ple0": 32, "ple1": 40,
                "ynorm": 48, "conv_b": 64, "dq": 88, "dk": 89, "mq": 90, "mk": 91, "sq": 92,
                "sk": 93, "sub": 94}

        A = Arena()
        qk_a = A(2, TT, 512)
        sq_a = A(TT, 512)
        v_a = A(TT, D)
        qT_a, kT_a = A(KT, S), A(KT, S)
        hank = A(UNITS, 256)
        probs = A(4, 384)
        wT = A(2, 384)
        nmax, psum_, prec = A(MAPS, TT), A(MAPS, TT), A(MAPS, TT)
        ssd, rsd = A(UNITS, TT), A(UNITS, TT)
        hss, hrs = A(TT, 8), A(TT, 8)
        lamv = A(4, 64)
        lame = A(2)
        rows_a, rows_c = A(P), A(P)
        u_sb, tab, onehot = A(384), A(UNITS), A(384)
        y_a = hn

        M = Arena()
        sel = M(TT, EXPERTS * SLOTS)
        selw = M(TT, EXPERTS * SLOTS)
        selwT = M(QUADS, S)
        xg = M(KT, P)
        selwT_q = M(S)
        hpre = M(2, 512)
        sg = M(QUAD, 64)
        hid = M(QUAD, 64)
        dn = M(D)
        rl = M(TT, 36)
        gmx, gex, gsum, gidx = M(TT), M(TT, GROUPS), M(TT), M(TT)
        geq, gc = M(TT, GROUPS), M(TT, GROUPS)
        el, el2, eq, cand = (M(TT, EXPERTS) for _ in range(4))
        oh1, oh2, wsel, msel, rk = (M(TT, EXPERTS) for _ in range(5))
        m1, m2, i1, w1, w2 = (M(TT) for _ in range(5))
        cmax, cpass = M(1), M(8)

        B = Arena()
        xc = B(CONV_TILES, S)
        z = B(TT, D_INNER)
        ym = B(TT, D_INNER)
        seg = B(2, 1024)
        xdt = B(2, 512)
        xdte = B(512)
        cb = B(TT, 512)
        btok = B(512)
        dtb, dtA = B(TT, SSM_HEADS), B(TT, SSM_HEADS)
        dta, dtu, dtw, dtl, dtq, dtv = (cols(seg[:, 0, 64 * i:64 * i + 64], TT) for i in range(6))
        acum, toend, ea = B(TT, SSM_HEADS), B(SSM_HEADS), B(SSM_HEADS)
        negA = B(SSM_HEADS)
        ssy, rsy = B(8), B(8)
        state = hn[:, :, :].rearrange("p a b -> p (a b)")
        yT = xc[:, 0:16, :]

        E_ = Arena()
        pT = E_(TT, S)
        sig = E_(2, 512)
        pret = E_(2, 512)

        K = Arena()
        qk_b = K(2, TT, 512)
        sq_b = K(TT, 512)
        v_b = K(TT, D)
        gate_b = K(TT, D)
        qT_b, kT_b = K(KT, S), K(KT, S)
        hT2 = K(KT, S)
        mask3 = K(384)
        absz, expz, lnz, spz, wz = (K(2, 384) for _ in range(5))
        hss_b, hrs_b = K(TT, 8), K(TT, 8)
        o_b = hn

        wr = sb("wr", [P, KT, 36])
        wdt = sb("wdt", [P, KT, SSM_HEADS])

        bias_dram = nc.dram_tensor("bias_rows", (UNITS, 384), F32, kind="Internal").ap()

        x_loaded, const_loaded, rows_loaded, small_loaded = map(sem, (
            "x_loaded", "const_loaded", "rows_loaded", "small_loaded"))
        tab_loaded, ones_set, u_ps, u_ready, u_stored, hank_loaded = map(sem, (
            "tab_loaded", "ones_set", "u_ps", "u_ready", "u_stored", "hank_loaded"))
        full_a = [sem(f"full_a{i}") for i in range(RING)]
        full_e = [sem(f"full_e{i}") for i in range(RING)]
        full_b = [sem(f"full_b{i}") for i in range(RING)]
        used_a, used_e, used_b = map(sem, ("used_a", "used_e", "used_b"))
        act_step, dve_step, pool_step = map(sem, ("act_step", "dve_step", "pool_step"))
        gains_ps, gains_ready, lam_sum, lam_exp = map(sem, (
            "gains_ps", "gains_ready", "lam_sum", "lam_exp"))
        ss_ready, hn_ready, turn_ps, turned, x_ready = map(sem, (
            "ss_ready", "hn_ready", "turn_ps", "turned", "x_ready"))
        proj_act, proj_dve, qkT_ps, qkT_ready = map(sem, ("proj_act", "proj_dve", "qkT_ps", "qkT_ready"))
        logits_ps, nmax_ready, probs_ready, w_ready, wT_ps, wT_ready, pv_ps, sqd_ready, y_ready = map(
            sem, ("logits_ps", "nmax_ready", "probs_ready", "w_ready", "wT_ps", "wT_ready", "pv_ps",
                  "sqd_ready", "y_ready"))
        router_ps, gsub_ready, gexp_ready, msel_ready, rank_ps, npass_ready, edif_ready, eexp_ready = map(
            sem, ("router_ps", "gsub_ready", "gexp_ready", "msel_ready", "rank_ps", "npass_ready",
                  "edif_ready", "eexp_ready"))
        pass_step, sel_ready, selT_ps, selT_ready = map(sem, (
            "pass_step", "sel_ready", "selT_ps", "selT_ready"))
        gather_ps, xg_ready, h_ready, fold_ps, silu_ready, hid_ready, dn0_ps = map(sem, (
            "gather_ps", "xg_ready", "h_ready", "fold_ps", "silu_ready", "hid_ready", "dn0_ps"))
        dn0_ready, dn1_ready, selq_ready, scatter_ps = map(sem, (
            "dn0_ready", "dn1_ready", "selq_ready", "scatter_ps"))
        dt_ps, dta_ready, dtu_ready, dtw_ready, dtl_ready, a_ready, dtA_ready, cum_ps = map(sem, (
            "dt_ps", "dta_ready", "dtu_ready", "dtw_ready", "dtl_ready", "a_ready", "dtA_ready", "cum_ps"))
        acum_ready, decay_ready, conv_done, xc_ready, z_ready = map(sem, (
            "acum_ready", "decay_ready", "conv_done", "xc_ready", "z_ready"))
        bt_ps, bt_ready, cb_ps, cb_ready, xT_ps, xt_ready, xdt_ready, xdte_ready = map(sem, (
            "bt_ps", "bt_ready", "cb_ps", "cb_ready", "xT_ps", "xt_ready", "xdt_ready", "xdte_ready"))
        rows_ps, seg_ready, dec_ready, m_ready, intra_ps, state_ready, ysum_ready, yz_ready = map(sem, (
            "rows_ps", "seg_ready", "dec_ready", "m_ready", "intra_ps", "state_ready", "ysum_ready",
            "yz_ready"))
        ssy_ready, yn_ready, yT_ps, yT_ready, xd_ready = map(sem, (
            "ssy_ready", "yn_ready", "yT_ps", "yT_ready", "xd_ready"))
        p_loaded, pT_ps, pT_ready, sig_ready = map(sem, ("p_loaded", "pT_ps", "pT_ready", "sig_ready"))
        projb_act, projb_dve, qkTb_ps, qkTb_ready = map(sem, (
            "projb_act", "projb_dve", "qkTb_ps", "qkTb_ready"))
        zz_ps, ln_ready, sp_ready, suf_ps, we_ready, wm_ready, ob_ps, o_ready = map(sem, (
            "zz_ps", "ln_ready", "sp_ready", "suf_ps", "we_ready", "wm_ready", "ob_ps",
            "o_ready"))
        out_stored = sem("out_stored")
        rs_ready, hss_ready, hrs_ready, hssb_ready, hrsb_ready, rsd_ready, rsy_ready = map(sem, (
            "rs_ready", "hss_ready", "hrs_ready", "hssb_ready", "hrsb_ready", "rsd_ready", "rsy_ready"))

        def wide(w, c, half):
            return w[512 * half:512 * half + 512, 512 * c:512 * c + 512].rearrange("(k p) n -> p k n", p=P)

        w_in, w_out = d["w_in"][0], d["w_out"][0]
        units_a = [wide(w_in, c, h) for c in range(6) for h in range(2)]
        units_a += [wide(w_out, c, h) for c in range(2) for h in range(2)]
        m_in, m_out = d["m_in_2"][0], d["m_out_2"][0]
        XBC_ORDER = [4, 5, 0, 1, 2, 3]
        m_xbc = m_in[:, D_INNER:]
        units_b = [wide(m_xbc, c, h) for c in XBC_ORDER for h in range(2)]
        units_b += [wide(m_in, c, h) for c in range(4) for h in range(2)]
        units_b += [wide(m_out, c, h) for c in range(2) for h in range(4)]
        ple = [[d["ple_proj_2"][i].rearrange("(k p) n -> p k n", p=P)]
               + [wide(d["ple_gate_2"][i], c, h) for c in range(2) for h in range(2)] for i in range(2)]
        AT_Z, AT_MOUT, AT_PLE0 = 12, 20, 28
        units_b += ple[0]
        AT_KV = len(units_b)
        units_b += [wide(d["w_kv_2"], c, h) for c in range(4) for h in range(2)]
        units_b += [wide(d["s_in_2"][0], c, h) for c in range(4) for h in range(2)]
        AT_SOUT = len(units_b)
        units_b += [wide(d["s_out_2"][0], c, h) for c in range(2) for h in range(2)]
        AT_PLE1 = len(units_b)
        units_b += ple[1]
        assert len(units_a) == UNITS_A and len(units_b) == UNITS_B

        gate_v = d["w_gate"][0].rearrange("e (p k) n -> e p (k n)", k=KT)
        up_v = d["w_up"][0].rearrange("e (p k) n -> e p (k n)", k=KT)
        down_v = d["w_down"][0].rearrange("e (p f) n -> e p (f n)", f=2)
        QUAD_UNITS = [(v, e) for e in range(QUAD) for v in (gate_v, up_v)] + [(down_v, e) for e in range(QUAD)]

        def e_slot(j):
            return (UNITS_A + j) % RING

        def b_slot(n):
            return (UNITS_A + n) % RING

        def b_full(n):
            return full_b[b_slot(n)], 16 * (n // RING + 1)

        def maps_of(u):
            return [2 * u, 2 * u + 1] if u < DIFF_HEADS else [u + DIFF_HEADS]

        def unit_of(m):
            return m // 2 if m < 2 * DIFF_HEADS else m - DIFF_HEADS

        block = ctx.enter_context(nc.Block())

        @block.sync
        def _(sp):
            xin = d["x"][0].rearrange("(t p) n -> t p n", p=P)
            for t in range(TT):
                sp.dma_start(x[:, t, :], xin[t]).then_inc(x_loaded, 16)
            sp.dma_start(consts[:, :], d["consts"]).then_inc(const_loaded, 16)
            for n in range(UNITS_A):
                if n >= RING:
                    sp.wait_ge(used_a, n - RING + 1)
                sp.dma_start(cols(ring[:, n % RING, :], 4), units_a[n]).then_inc(full_a[n % RING], 16)
            for j, (v, e) in enumerate(QUAD_UNITS):
                sp.wait_ge(used_a, UNITS_A - RING + j + 1)
                sp.dma_start(ring[:, e_slot(j), :], v[e]).then_inc(full_e[e_slot(j)], 16)
            sp.wait_ge(npass_ready, 1)
            npass = sp.value_load(counts_i[0:1, 0:1], min_val=1, max_val=S // SLOTS)
            first_free = sp.value_load(counts_i[0:1, 1:2], min_val=QUADS * RING - RING + 1,
                                       max_val=S // SLOTS * QUADS * RING)
            with sp.Fori(1, npass * QUADS) as q:
                for j, (v, e) in enumerate(QUAD_UNITS):
                    sp.wait_ge(used_e, q * RING + (j + 1 - RING))
                    src = v[bass.ds((q % QUADS) * QUAD + e, 1)].rearrange("e p n -> (e p) n")
                    sp.dma_start(ring[:, e_slot(j), :], src).then_inc(full_e[e_slot(j)], 16)
            for n in range(UNITS_B):
                if n < RING:
                    sp.wait_ge(used_e, first_free + n)
                else:
                    sp.wait_ge(used_b, n - RING + 1)
                dst = cols(ring[:, b_slot(n), :], 2 if n in (AT_PLE0, AT_PLE1) else 4)
                sp.dma_start(dst, units_b[n]).then_inc(full_b[b_slot(n)], 16)
            sp.wait_ge(x_ready, 24)
            sp.dma_start(out[0].rearrange("(t p) n -> p t n", p=P), x[:, :, :]).then_inc(out_stored, 16)
            sp.wait_ge(out_stored, 16)

        @block.scalar
        def _(act):
            chain = [0]

            def link(ins):
                chain[0] += 1
                ins.then_inc(act_step, 1)
                act.wait_ge(act_step, chain[0])

            def rows(at, src, n):
                act.dma_start(rows_a[at:at + n, :], src).then_inc(rows_loaded, 16)

            for name, n in (("norm1", "norm1_g"), ("m_norm", "m_norm_2"), ("s_norm", "s_norm_2"),
                            ("ynorm", "m_ynorm_2"), ("conv_b", "m_conv_b_2")):
                v = d[n].rearrange("o (k p) -> (o k) p", p=P)
                rows(GAIN[name], v, v.shape[0])
            rows(GAIN["kv"], d["kv_norm_2"].rearrange("(k p) -> k p", p=P), KT)
            rows(GAIN["ple0"], d["ple_norm_2"].rearrange("o (k p) -> (o k) p", p=P), 2 * KT)
            for name, n in (("dq", "diff_q_g"), ("dk", "diff_k_g"), ("mq", "moba_q_g"), ("mk", "moba_k_g"),
                            ("sq", "q_norm_2"), ("sk", "k_norm_2")):
                v = d[n] if len(d[n].shape) == 2 else d[n].rearrange("(o n) -> o n", o=1)
                for half in range(2):
                    act.dma_start(rows_a[GAIN[name]:GAIN[name] + 1, HD * half:HD * half + HD], v)\
                       .then_inc(rows_loaded, 16)
            rows(GAIN["sub"], d["diff_sub_g"], 1)
            act.dma_start(rows_c[0:96, :], d["m_conv_w_2"].rearrange("o j (k p) -> (o j k) p", p=P))\
               .then_inc(rows_loaded, 16)
            act.dma_start(tab[0:BUCKETS, :], d["rel_bias"]).then_inc(tab_loaded, 16)
            act.dma_start(onehot[0:BUCKETS + 1, :], d["onehot"]).then_inc(tab_loaded, 16)
            for i, n in enumerate(("lambda_q1", "lambda_k1", "lambda_q2", "lambda_k2")):
                act.dma_start(lamv[:, i, :], d[n].to_broadcast([P, HD])).then_inc(small_loaded, 16)
            for i, n in enumerate(("m_dt_bias_2", "m_A_log_2", "m_D_2")):
                act.dma_start(headp[:, i, :], d[n].to_broadcast([P, SSM_HEADS])).then_inc(small_loaded, 16)
            act.dma_start(g2[:, :], d["norm2_g"].rearrange("o (p k) -> (o p) k", k=KT)).then_inc(small_loaded, 16)
            act.dma_start(wr[:, :, 0:GROUPS], d["router_group"][0].rearrange("(p k) n -> p k n", k=KT))\
               .then_inc(small_loaded, 16)
            for g in range(GROUPS):
                act.dma_start(wr[:, :, GROUPS + PER_GROUP * g:GROUPS + PER_GROUP * (g + 1)],
                              d["router_expert"][0, g].rearrange("(p k) n -> p k n", k=KT))\
                   .then_inc(small_loaded, 16)
            act.dma_start(wdt[:, :, :], d["m_in_2"][0][:, 5120:5152].rearrange("(k p) n -> p k n", p=P))\
               .then_inc(small_loaded, 16)

            def squares(i, junk):
                for t in range(TT):
                    if i == 0:
                        act.wait_ge(x_loaded, 16 * TT)
                    else:
                        act.wait_ge(x_ready, 4 * i)
                        act.wait_ge(rs_ready, i)
                    act.activation(junk[:, t, :], x[:, t, :], ACT.Square, accum_out=ss[:, t:t + 1])\
                       .then_inc(ss_ready, 1)

            squares(0, hn)
            act.wait_ge(lam_sum, 1)
            act.activation(lame[:, :], lame[:, :], ACT.Exp).then_inc(lam_exp, 1)
            act.wait_ge(u_ready, 1)
            act.dma_start(bias_dram, u_sb[0:UNITS, :]).then_inc(u_stored, 16)
            act.wait_ge(u_stored, 16)
            act.dma_start(hank, bass.AP(bias_dram.tensor, 0, [[1, P], [384, UNITS], [1, 256]]))\
               .then_inc(hank_loaded, 16)

            def project(kinds, used, at, c_act, c_dve, t_ps, t_ready, sq, v, gate, turned_to):
                j = 0
                n_v = n_g = 0
                pend = None

                def copy_turned(jj, dst, gain):
                    for t in range(TT):
                        act.wait_ge(t_ps, 2 * jj + t + 1)
                        src, to = cols(banks[4 + t][:, :], 4), dst[:, :, P * t:P * t + P]
                        if gain is None:
                            act.activation(to, src, ACT.Copy).then_inc(t_ready, 1)
                        else:
                            act.activation(to, src, ACT.Identity, scale=gain).then_inc(t_ready, 1)

                for c, kind in enumerate(kinds):
                    act.wait_ge(used, at + 2 * c + 2)
                    for t in range(TT):
                        bank = banks[2 * (c % 2) + t]
                        if kind == "qk":
                            if j >= 1 and t == 0:
                                act.wait_ge(c_dve, 2 * j)
                            act.activation(sq[:, t, :], bank[:, :], ACT.Square).then_inc(c_act, 1)
                        elif kind == "v":
                            act.activation(v[:, t, 512 * n_v:512 * n_v + 512], bank[:, :], ACT.Copy)\
                               .then_inc(c_act, 1)
                        else:
                            act.activation(gate[:, t, 512 * n_g:512 * n_g + 512], bank[:, :], ACT.Silu)\
                               .then_inc(c_act, 1)
                    n_v += kind == "v"
                    n_g += kind == "gate"
                    if pend is not None:
                        copy_turned(*pend)
                        pend = None
                    if kind == "qk":
                        pend = (j, *turned_to[j])
                        j += 1
                if pend is not None:
                    copy_turned(*pend)

            act.wait_ge(gains_ready, 3)
            project(["qk", "qk", "v", "qk", "qk", "v"], used_a, 0, proj_act, proj_dve, qkT_ps, qkT_ready,
                    sq_a, v_a, None, [(qT_a[:, 0:4, :], gq[:, 0:1]), (kT_a[:, 0:4, :], None),
                                      (qT_a[:, 4:8, :], gq[:, 1:2]), (kT_a[:, 4:8, :], None)])

            def exps(u):
                for m in maps_of(u):
                    act.wait_ge(nmax_ready, m + 1)
                    if m >= 4:
                        act.wait_ge(wT_ps, unit_of(m - 4) + 1)
                    bank = banks[m % 3]
                    act.activation(probs[:, m % 4, 0:128], bank[:, 0:128], ACT.Exp, bias=nmax[:, m, 0:1],
                                   accum_out=psum_[:, m, 0:1])
                    act.activation(probs[:, m % 4, 128:384], bank[:, 128:384], ACT.Exp, bias=nmax[:, m, 1:2],
                                   accum_out=psum_[:, m, 1:2]).then_inc(probs_ready, 1)

            exps(0)
            for u in range(UNITS + 1):
                if u + 1 < UNITS:
                    exps(u + 1)
                if u < UNITS:
                    act.wait_ge(wT_ps, u + 1)
                    if u >= 2:
                        act.wait_ge(pv_ps, u - 1)
                    act.activation(wT[:, u % 2, :], banks[3 + u % 2][:, 0:384], ACT.Copy).then_inc(wT_ready, 1)
                if 1 <= u <= DIFF_HEADS:
                    act.wait_ge(pv_ps, u)
                    for t in range(TT):
                        ins = act.activation(sq_a[:, t, 0:128], banks[5 + (u - 1) % 2][:, 128 * t:128 * t + 128],
                                             ACT.Square, accum_out=ssd[:, u - 1, t:t + 1])
                    ins.then_inc(sqd_ready, 1)

            squares(1, hn)
            act.wait_ge(gsub_ready, 1)
            act.activation(gex, gex, ACT.Exp).then_inc(gexp_ready, 1)
            act.wait_ge(edif_ready, 1)
            act.activation(m2, m2, ACT.Exp).then_inc(eexp_ready, 1)

            act.wait_ge(npass_ready, 1)
            npass = act.value_load(counts_i[0:1, 0:1], min_val=1, max_val=S // SLOTS)
            act.sem_inc(h_ready, 4)
            act.sem_inc(dn0_ready, 1)
            with act.Fori(0, npass) as r:
                for n in range(4):
                    act.wait_ge(selT_ps, r * 4 + (n + 1))
                    if n == 0:
                        act.wait_ge(selq_ready, r * QUADS + 1)
                    t, half = n // 2, n % 2
                    act.activation(selwT[:, 4 * half:4 * half + 4, P * t:P * t + P],
                                   cols(banks[6 + n % 2][:, :], 4), ACT.Copy).then_inc(selT_ready, 1)
                with act.Fori(0, QUADS) as g:
                    q = r * QUADS + g
                    for e in range(QUAD):
                        act.wait_ge(used_e, q * RING + (2 * e + 2))
                        act.wait_ge(fold_ps, q * QUAD + (e + 3))
                        act.activation(hpre[:, e % 2, :], banks[6 + e % 2][:, :], ACT.Copy).then_inc(h_ready, 1)
                        if e >= 1:
                            act.wait_ge(fold_ps, q * QUAD + (e + QUAD))
                            act.activation(sg[:, e - 1, :], banks[4 + (e - 1) % 2][:, 0:64], ACT.Silu)\
                               .then_inc(silu_ready, 1)
                    act.wait_ge(fold_ps, q * QUAD + 2 * QUAD)
                    act.activation(sg[:, 3, :], banks[5][:, 0:64], ACT.Silu).then_inc(silu_ready, 1)
                    act.wait_ge(dn0_ps, q + 1)
                    act.wait_ge(scatter_ps, q + 1)
                    act.activation(dn[:, 0:512], banks[6][:, :], ACT.Copy).then_inc(dn0_ready, 1)

            squares(2, hn)
            act.wait_ge(x_ready, 8)
            act.activation(negA, headp[:, 1, :], ACT.Exp).then_inc(a_ready, 1)
            act.wait_ge(dta_ready, 1)
            act.activation(dtu, dta, ACT.Exp, scale=-1.0).then_inc(dtu_ready, 1)
            act.wait_ge(dtw_ready, 1)
            act.activation(dtl, dtw, ACT.Ln).then_inc(dtl_ready, 1)
            act.wait_ge(acum_ready, 1)
            link(act.activation(toend, toend, ACT.Exp))
            act.activation(ea, acum[:, 1, :], ACT.Exp).then_inc(decay_ready, 1)
            for ci, c in enumerate(XBC_ORDER):
                act.wait_ge(conv_done, ci + 1)
                v = xc[:, 4 * c:4 * c + 4, :]
                act.activation(v, v, ACT.Silu).then_inc(xc_ready, 1)
            for c in range(4):
                act.wait_ge(used_b, AT_Z + 2 * c + 2)
                for t in range(TT):
                    act.activation(z[:, t, 512 * c:512 * c + 512], banks[2 * (c % 2) + t][:, :], ACT.Silu)\
                       .then_inc(z_ready, 1)
            act.wait_ge(bt_ps, 1)
            act.activation(btok, banks[4][:, :], ACT.Copy).then_inc(bt_ready, 1)
            for c in range(TT):
                act.wait_ge(cb_ps, c + 1)
                act.activation(cb[:, c, :], banks[6 + c][:, :], ACT.Copy).then_inc(cb_ready, 1)

            def mamba_tail(k):
                c, g = k // 4, k % 4
                act.wait_ge(yz_ready, k + 1)
                if k >= 1:
                    act.wait_ge(ssy_ready, k)
                act.activation(btok, ym[:, c, 512 * g:512 * g + 512], ACT.Square,
                               accum_out=ssy[:, k:k + 1]).then_inc(ssy_ready, 1)

            for k in range(8):
                c, g = k // 4, k % 4
                act.wait_ge(xT_ps, k + 1)
                act.activation(ym[:, c, 512 * g:512 * g + 512], banks[k % 2][:, :], ACT.Copy)\
                   .then_inc(xt_ready, 1)
                for b in range(2):
                    act.wait_ge(seg_ready, 2 * k + b + 1)
                    v = seg[:, k % 2, 512 * b:512 * b + 512]
                    act.activation(v, v, ACT.Exp).then_inc(dec_ready, 1)
                if c == 0:
                    act.wait_ge(intra_ps, k + 1)
                    act.activation(state[:, 512 * g:512 * g + 512], banks[5][:, :], ACT.Copy)\
                       .then_inc(state_ready, 1)
            for k in range(8):
                mamba_tail(k)

            def ple_act(i, at):
                act.wait_ge(pT_ps, i + 1)
                act.activation(pT, cols(banks[6][:, :], 2), ACT.Copy).then_inc(pT_ready, 1)
                squares(3 + 2 * i, hn)
                for c in range(2):
                    act.wait_ge(used_b, at + 3 + 2 * c)
                    for t in range(TT):
                        if c == 1:
                            act.wait_ge(x_ready, 12 + 8 * i + t + 1)
                        act.activation(sig[:, t, :], banks[2 * c + t][:, :], ACT.Sigmoid).then_inc(sig_ready, 1)

            act.dma_start(pbuf[:, :, :], d["p_2"][0, 0].rearrange("(t p) n -> p t n", p=P)).then_inc(p_loaded, 16)
            ple_act(0, AT_PLE0)
            act.dma_start(pbuf[:, :, :], d["p_2"][1, 0].rearrange("(t p) n -> p t n", p=P)).then_inc(p_loaded, 16)

            squares(4, hn)
            act.wait_ge(x_ready, 16)
            project(["qk", "qk", "v", "v", "qk", "qk", "gate", "gate"], used_b, AT_KV, projb_act, projb_dve,
                    qkTb_ps, qkTb_ready, sq_b, v_b, gate_b,
                    [(kT_b[:, 0:4, :], None), (kT_b[:, 4:8, :], None),
                     (qT_b[:, 0:4, :], gq[:, 2:3]), (qT_b[:, 4:8, :], gq[:, 2:3])])
            act.preload_act_table_set("natural_log_exp_and_others")

            def weights(h):
                act.wait_ge(wm_ready, h + 1)
                act.activation(wz[:, h % 2, :], wz[:, h % 2, :], ACT.Exp).then_inc(we_ready, 1)

            for h in range(SB_HEADS):
                act.wait_ge(zz_ps, h + 1)
                link(act.activation(absz[:, h % 2, :], banks[h % 4][:, 0:384], ACT.Abs))
                if h >= 2:
                    act.wait_ge(sp_ready, h - 1)
                link(act.activation(expz[:, h % 2, :], absz[:, h % 2, :], ACT.Exp, scale=-1.0))
                act.activation(lnz[:, h % 2, :], expz[:, h % 2, :], ACT.Ln, bias=1.0).then_inc(ln_ready, 1)
                if h >= 1:
                    weights(h - 1)
            weights(SB_HEADS - 1)
            ple_act(1, AT_PLE1)

        @block.gpsimd
        def _(pool):
            def y_z(k):
                c, g = k // 4, k % 4
                y = ym[:, c, 512 * g:512 * g + 512]
                pool.wait_ge(ysum_ready, k + 1)
                pool.wait_ge(z_ready, 8)
                pool.tensor_tensor(y, y, z[:, c, 512 * g:512 * g + 512], ALU.mult).then_inc(yz_ready, 1)

            chain = [0]

            def rsqrt(dst, src, eps, ready, step, done):
                pool.wait_ge(ready, step)
                chain[0] += 1
                pool.tensor_scalar(dst, src, eps, None, ALU.add).then_inc(pool_step, 1)
                pool.wait_ge(pool_step, chain[0])
                pool.tensor_tensor(dst, dst, C("neghalf")[:, 0:src.shape[1]], ALU.pow).then_inc(done, 1)

            def norm(i):
                if i:
                    pool.wait_ge(hn_ready, 2 * i)
                rsqrt(rs[:, :], ss[:, :], EPS * D, ss_ready, 2 * i + 2, rs_ready)

            def project(hs, hr, hsum, hroot):
                for j in range(4):
                    for t in range(TT):
                        rsqrt(hr[:, t, :], hs[:, t, :], EPS * HD, hsum, 2 * j + t + 1, hroot)

            pool.wait_ge(const_loaded, 16)
            norm(0)
            project(hss, hrs, hss_ready, hrs_ready)
            for u in range(DIFF_HEADS):
                rsqrt(rsd[:, u, :], ssd[:, u, :], EPS * 128, sqd_ready, u + 1, rsd_ready)
            norm(1)
            norm(2)
            for k in range(8):
                c, g = k // 4, k % 4
                y = ym[:, c, 512 * g:512 * g + 512]
                pool.wait_ge(xt_ready, k + 1)
                if k == 0:
                    pool.wait_ge(small_loaded, 16 * 14)
                    pool.wait_ge(cb_ready, 2)
                    pool.wait_ge(decay_ready, 1)
                pool.tensor_tensor(cols(y, 8), cols(y, 8), over(headp[:, 2, 8 * g:8 * g + 8], HD), ALU.mult)\
                    .then_inc(xd_ready, 1)
                if c == 0:
                    pool.wait_ge(xdt_ready, k + 1)
                    if k >= 1:
                        pool.wait_ge(intra_ps, k)
                    pool.tensor_tensor(cols(xdte, 8), cols(xdt[:, k % 2, :], 8),
                                       over(toend[:, 8 * g:8 * g + 8], HD), ALU.mult).then_inc(xdte_ready, 1)
                for b in range(2):
                    pool.wait_ge(dec_ready, 2 * k + b + 1)
                    v = cols(seg[:, k % 2, 512 * b:512 * b + 512], 4)
                    pool.tensor_tensor(v, v, repeat(cb[:, c, P * g:P * g + P], 4), ALU.mult).then_inc(m_ready, 1)
                if k >= 1:
                    y_z(k - 1)
            y_z(7)
            for k in range(8):
                rsqrt(rsy[:, k:k + 1], ssy[:, k:k + 1], EPS * 512, ssy_ready, k + 1, rsy_ready)
            norm(3)
            norm(4)
            project(hss_b, hrs_b, hssb_ready, hrsb_ready)
            norm(5)

        @block.vector
        def _(dve):
            chain = [0]

            def link(ins):
                chain[0] += 1
                ins.then_inc(dve_step, 1)
                dve.wait_ge(dve_step, chain[0])

            dve.memset(tab[BUCKETS:BUCKETS + 1, :], 1.0).then_inc(ones_set, 1)
            for i, (dst, n) in enumerate(((gcol, 95), (ccol, 96))):
                dve.wait_ge(gains_ps, i + 1)
                dve.tensor_copy(dst[:, 0:n], banks[4 + i][:, 0:n]).then_inc(gains_ready, 1)

            def norm(i, permuted=False):
                for t in range(TT):
                    dve.wait_ge(rs_ready, i + 1)
                    src, dst = x[:, t, :], hn[:, t, :]
                    if permuted:
                        src, dst = src.rearrange("p (j k) -> p k j", k=KT), cols(dst, KT)
                    dve.tensor_scalar(dst, src, rs[:, t:t + 1], math.sqrt(D), ALU.mult, ALU.mult)\
                       .then_inc(hn_ready, 1)

            def turn(i, gain, second=None):
                for n in range(4):
                    t, half = n // 2, n % 2
                    dve.wait_ge(turn_ps, 4 * i + n + 1)
                    src = cols(banks[6 + n % 2][:, :], 4)
                    if second is not None:
                        dve.tensor_tensor(hT2[:, 4 * half:4 * half + 4, P * t:P * t + P], src,
                                          over(second[:, 4 * half:4 * half + 4], P), ALU.mult)
                    dve.tensor_tensor(hT[:, 4 * half:4 * half + 4, P * t:P * t + P], src,
                                      over(gain[:, 4 * half:4 * half + 4], P), ALU.mult).then_inc(turned, 1)

            def G(name, n=KT):
                return gcol[:, GAIN[name]:GAIN[name] + n]

            norm(0)
            dve.wait_ge(gains_ready, 2)
            turn(0, G("norm1"))
            for i, a in enumerate(("dq", "mq", "sq")):
                at = GAIN[a]
                link(dve.tensor_scalar(gq[:, i:i + 1], gcol[:, at:at + 1], gcol[:, at + 1:at + 2], 8.0,
                                       ALU.mult, ALU.mult))
            link(dve.memset(ga[:, :], 1.0))
            dve.tensor_scalar(ga[:, 0:4], G("sub", 1).to_broadcast([P, 4]), 1.0 - LAMBDA_INIT, None, ALU.mult)\
               .then_inc(gains_ready, 1)
            dve.wait_ge(gains_ready, 3)
            dve.wait_ge(small_loaded, 16 * 14)
            for i in range(2):
                link(dve.tensor_tensor(lamv[:, 2 * i, :], lamv[:, 2 * i, :], lamv[:, 2 * i + 1, :], ALU.mult))
                ins = dve.tensor_reduce(lame[:, i:i + 1], lamv[:, 2 * i, :], AX.X, ALU.add)
                if i == 0:
                    link(ins)
            ins.then_inc(lam_sum, 1)
            dve.wait_ge(lam_exp, 1)
            link(dve.tensor_scalar(nlam[:, :], lame[:, 1:2], lame[:, 0:1], -LAMBDA_INIT, ALU.subtract, ALU.add))
            dve.wait_ge(u_ps, 1)
            dve.tensor_copy(u_sb[0:UNITS, :], banks[7][0:UNITS, 0:384]).then_inc(u_ready, 1)

            def project(kinds, c_act, c_dve, t_ps, sq, qk, hs, hr, hsum, hroot):
                j = 0
                for c, kind in enumerate(kinds):
                    if kind != "qk":
                        continue
                    if j >= 2:
                        dve.wait_ge(t_ps, 2 * (j - 1))
                    for t in range(TT):
                        dve.wait_ge(c_act, 2 * c + t + 1)
                        dve.tensor_reduce(hs[:, t, :], cols(sq[:, t, :], 8), AX.X, ALU.add).then_inc(hsum, 1)
                    for t in range(TT):
                        dve.wait_ge(hroot, 2 * j + t + 1)
                        dve.tensor_tensor(cols(qk[:, j % 2, t, :], 8), cols(banks[2 * (c % 2) + t][:, :], 8),
                                          over(hr[:, t, :], HD), ALU.mult).then_inc(c_dve, 1)
                    j += 1

            project(["qk", "qk", "v", "qk", "qk", "v"], proj_act, proj_dve, qkT_ps,
                    sq_a, qk_a, hss, hrs, hss_ready, hrs_ready)

            def maxima(u):
                for m in maps_of(u):
                    dve.wait_ge(logits_ps, m + 1)
                    bank = banks[m % 3]
                    dve.tensor_reduce(nmax[:, m, 0:1], bank[:, 0:128], AX.X, ALU.max, negate=True)
                    dve.tensor_reduce(nmax[:, m, 1:2], bank[:, 128:384], AX.X, ALU.max, negate=True)\
                       .then_inc(nmax_ready, 1)

            def combine(u):
                ms = maps_of(u)
                dve.wait_ge(probs_ready, ms[-1] + 1)
                for m in ms[:-1]:
                    link(dve.reciprocal(prec[:, m, :], psum_[:, m, :]))
                last = dve.reciprocal(prec[:, ms[-1], :], psum_[:, ms[-1], :])
                if u >= DIFF_HEADS:
                    last.then_inc(w_ready, 1)
                    return
                link(last)
                a, b = ms
                link(dve.tensor_scalar(prec[:, b, :], prec[:, b, :], nlam[:, 0:1], None, ALU.mult))
                parts = ((0, 128), (128, 384))
                for t, (lo, hi) in enumerate(parts):
                    ins = dve.tensor_scalar(probs[:, b % 4, lo:hi], probs[:, b % 4, lo:hi],
                                            prec[:, b, t:t + 1], None, ALU.mult)
                link(ins)
                for t, (lo, hi) in enumerate(parts):
                    pa = probs[:, a % 4, lo:hi]
                    ins = dve.scalar_tensor_tensor(pa, pa, prec[:, a, t:t + 1], probs[:, b % 4, lo:hi],
                                                   ALU.mult, ALU.add)
                ins.then_inc(w_ready, 1)

            def outputs(u):
                bank = banks[5 + u % 2]
                if u < DIFF_HEADS:
                    dve.wait_ge(rsd_ready, u + 1)
                    for t in range(TT):
                        ins = dve.tensor_scalar(y_a[:, t, 128 * u:128 * u + 128], bank[:, 128 * t:128 * t + 128],
                                                rsd[:, u, t:t + 1], math.sqrt(128.0), ALU.mult, ALU.mult)
                else:
                    dve.wait_ge(pv_ps, u + 1)
                    dve.wait_ge(w_ready, u + 1)
                    h, m = u - DIFF_HEADS, u + DIFF_HEADS
                    for t in range(TT):
                        ins = dve.tensor_scalar(y_a[:, t, 512 + HD * h:512 + HD * h + HD],
                                                bank[:, 128 * t:128 * t + HD], prec[:, m, t:t + 1], None, ALU.mult)
                ins.then_inc(y_ready, 1)

            maxima(0)
            for u in range(UNITS + 1):
                if u < UNITS:
                    combine(u)
                if u + 1 < UNITS:
                    maxima(u + 1)
                if u >= 1:
                    outputs(u - 1)
            turn(1, ga)

            def add_product(c, bank0, used, at):
                dve.wait_ge(used, at)
                for t in range(TT):
                    xv = x[:, t, 512 * c:512 * c + 512]
                    dve.tensor_tensor(xv, banks[bank0 + t][:, :], xv, ALU.add).then_inc(x_ready, 1)

            for c in range(2):
                add_product(c, 2 * c, used_a, 12 + 2 * c + 2)
            dve.wait_ge(x_ready, 4)
            norm(1, permuted=True)
            turn(2, g2)

            dve.wait_ge(router_ps, 1)
            link(dve.tensor_copy(rl, cols(banks[4][:, 0:72], 2)))
            iota32 = C("iota")
            gl = rl[:, :, 0:GROUPS]
            link(dve.tensor_reduce(gmx, gl, AX.X, ALU.max))
            link(dve.tensor_tensor(geq, gl, over(gmx, 4), ALU.is_equal))
            dve.tensor_tensor(gex, gl, over(gmx, 4), ALU.subtract).then_inc(gsub_ready, 1)
            link(dve.tensor_tensor(gc, geq, repeat(C("iota_low")[:, 0:4], TT), ALU.mult))
            link(dve.tensor_reduce(gidx, gc, AX.X, ALU.min))
            link(dve.tensor_tensor(geq, repeat(C("iota_low")[:, 0:4], TT), over(gidx, 4), ALU.is_equal))
            link(dve.tensor_scalar(gc, geq, -NEG, NEG, ALU.mult, ALU.add))
            for t in range(TT):
                ins = dve.tensor_tensor(cols(el[:, t, :], GROUPS), cols(rl[:, t, GROUPS:36], GROUPS),
                                        over(gc[:, t, :], PER_GROUP), ALU.add)
            link(ins)

            def pick(vals, mx, oh):
                link(dve.tensor_reduce(mx, vals, AX.X, ALU.max))
                link(dve.tensor_tensor(eq, vals, over(mx, EXPERTS), ALU.is_equal))
                link(dve.tensor_tensor(cand, eq, repeat(C("iota_low"), TT), ALU.mult))
                link(dve.tensor_reduce(i1, cand, AX.X, ALU.min))
                link(dve.tensor_tensor(oh, repeat(C("iota_low"), TT), over(i1, EXPERTS), ALU.is_equal))

            pick(el, m1, oh1)
            link(dve.scalar_tensor_tensor(el2, oh1, 2 * NEG, el, ALU.mult, ALU.add))
            pick(el2, m2, oh2)
            dve.tensor_tensor(m2, m2, m1, ALU.subtract).then_inc(edif_ready, 1)
            dve.wait_ge(edif_ready, 1)
            dve.tensor_tensor(msel, oh1, oh2, ALU.add).then_inc(msel_ready, 1)
            dve.wait_ge(gexp_ready, 1)
            link(dve.tensor_reduce(gsum, gex, AX.X, ALU.add))
            dve.wait_ge(eexp_ready, 1)
            link(dve.tensor_scalar(w1, m2, 1.0, None, ALU.add))
            link(dve.tensor_tensor(w1, w1, gsum, ALU.mult))
            link(dve.reciprocal(w1, w1))
            link(dve.tensor_tensor(w2, w1, m2, ALU.mult))
            link(dve.tensor_tensor(oh1, oh1, over(w1, EXPERTS), ALU.mult))
            link(dve.tensor_tensor(oh2, oh2, over(w2, EXPERTS), ALU.mult))
            link(dve.tensor_tensor(wsel, oh1, oh2, ALU.add))
            dve.wait_ge(rank_ps, 1)
            link(dve.scalar_tensor_tensor(rk, cols(banks[5][:, 0:64], 2), 1.0, msel, ALU.add, ALU.mult))
            link(dve.tensor_scalar(rk, rk, -1.0, None, ALU.add))
            link(dve.tensor_reduce(cmax, banks[5][:, 64:96], AX.X, ALU.max))
            link(dve.tensor_scalar(cpass, C("passes"), cmax[:, 0:1], None, ALU.is_lt))
            link(dve.tensor_reduce(cmax, cpass, AX.X, ALU.add))
            link(dve.tensor_scalar(cpass[:, 0:1], cmax, float(QUADS * RING), 1.0 - RING, ALU.mult, ALU.add))
            dve.tensor_copy(counts_i[:, 0:1], cmax)
            dve.tensor_copy(counts_i[:, 1:2], cpass[:, 0:1]).then_inc(npass_ready, 1)
            dve.wait_ge(npass_ready, 1)
            npass = dve.value_load(counts_i[0:1, 0:1], min_val=1, max_val=S // SLOTS)

            dve.sem_inc(xg_ready, 2)
            dve.sem_inc(hid_ready, 4)
            dve.sem_inc(dn1_ready, 1)
            dve.sem_inc(selq_ready, 1)
            with dve.Fori(0, npass) as r:
                dve.wait_ge(scatter_ps, r * QUADS + 1)
                for t in range(TT):
                    ins = dve.tensor_tensor(cols(sel[:, t, :], EXPERTS), repeat(iota32, EXPERTS),
                                            over(rk[:, t, :], SLOTS), ALU.is_equal)
                ins.then_inc(pass_step, 1)
                dve.wait_ge(pass_step, r * 2 + 1)
                dve.tensor_scalar(rk, rk, -float(SLOTS), None, ALU.add).then_inc(pass_step, 1)
                dve.wait_ge(pass_step, r * 2 + 2)
                for t in range(TT):
                    dve.tensor_tensor(cols(selw[:, t, :], EXPERTS), cols(sel[:, t, :], EXPERTS),
                                      over(wsel[:, t, :], SLOTS), ALU.mult).then_inc(sel_ready, 1)
                with dve.Fori(0, QUADS) as g:
                    q = r * QUADS + g
                    for b in range(2):
                        dve.wait_ge(gather_ps, q * 2 + (b + 1))
                        dve.tensor_tensor(xg[:, 4 * b:4 * b + 4, :], cols(banks[4 + b][:, :], 4),
                                          over(g2[:, 4 * b:4 * b + 4], P), ALU.mult).then_inc(xg_ready, 1)
                    dve.wait_ge(selT_ready, r * 4 + 4)
                    dve.wait_ge(scatter_ps, q + 1)
                    dve.tensor_copy(selwT_q, selwT[:, bass.ds(g, 1), :].rearrange("p a b -> p (a b)"))\
                       .then_inc(selq_ready, 1)
                    for e in range(QUAD):
                        dve.wait_ge(silu_ready, q * QUAD + (e + 1))
                        dve.tensor_tensor(hid[:, e, :], banks[4 + e % 2][:, 64:128], sg[:, e, :], ALU.mult)\
                           .then_inc(hid_ready, 1)
                    dve.wait_ge(used_e, q * RING + RING)
                    dve.tensor_copy(dn[:, 512:1024], banks[7][:, :]).then_inc(dn1_ready, 1)
            dve.wait_ge(scatter_ps, npass * QUADS + 1)
            for t in range(TT):
                for half in range(2):
                    dve.tensor_copy(x[:, t, 512 * half:512 * half + 512], banks[2 * t + half][:, :])\
                       .then_inc(x_ready, 1)
            dve.wait_ge(x_ready, 8)

            def turned_y(k):
                c, g = k // 4, k % 4
                dve.wait_ge(yT_ps, k + 1)
                dve.tensor_tensor(yT[:, 4 * g:4 * g + 4, P * c:P * c + P], cols(banks[6 + k % 2][:, :], 4),
                                  over(gcol[:, 48 + 4 * g:52 + 4 * g], P), ALU.mult).then_inc(yT_ready, 1)

            norm(2)
            turn(3, G("m_norm"))
            dve.wait_ge(dt_ps, 1)
            link(dve.tensor_tensor(dtb, cols(banks[4][:, 0:64], 2), repeat(headp[:, 0, :], TT), ALU.add))
            dve.scalar_tensor_tensor(dta, dtb, -1.0, dtb, ALU.mult, ALU.max).then_inc(dta_ready, 1)
            dve.wait_ge(dtu_ready, 1)
            dve.tensor_scalar(dtw, dtu, 1.0, None, ALU.add).then_inc(dtw_ready, 1)
            dve.wait_ge(dtw_ready, 1)
            link(dve.tensor_scalar(dtv, dtw, -1.0, None, ALU.add))
            link(dve.tensor_scalar(dtq, dtv, 0.0, None, ALU.is_equal))
            link(dve.tensor_tensor(dtv, dtv, dtq, ALU.add))
            link(dve.reciprocal(dtv, dtv))
            link(dve.tensor_tensor(dtv, dtv, dtu, ALU.mult))
            link(dve.tensor_tensor(dtq, dtq, dtu, ALU.mult))
            dve.wait_ge(dtl_ready, 1)
            link(dve.tensor_tensor(dtv, dtv, dtl, ALU.mult))
            link(dve.tensor_tensor(dtv, dtv, dtq, ALU.add))
            link(dve.scalar_tensor_tensor(dtb, dtb, 0.0, dtv, ALU.max, ALU.add))
            dve.wait_ge(a_ready, 1)
            dve.scalar_tensor_tensor(dtA, dtb, -1.0, repeat(negA, TT), ALU.mult, ALU.mult).then_inc(dtA_ready, 1)

            def conv(ci):
                dve.wait_ge(used_b, 2 * ci + 2)
                c = XBC_ORDER[ci]
                ins = None
                for tap in range(CONV_K - 1, -1, -1):
                    lag = CONV_K - 1 - tap
                    for k in range(4):
                        tile = 4 * c + k
                        src = banks[2 * (ci % 2) + k // 2][:, 256 * (k % 2):256 * (k % 2) + 256 - lag]
                        w = ccol[:, 24 * tap + tile:24 * tap + tile + 1]
                        if lag == 0:
                            ins = dve.tensor_scalar(xc[:, tile, :], src, w, gcol[:, 64 + tile:65 + tile],
                                                    ALU.mult, ALU.add)
                        else:
                            v = xc[:, tile, lag:]
                            ins = dve.scalar_tensor_tensor(v, src, w, v, ALU.mult, ALU.add)
                    if tap:
                        link(ins)
                ins.then_inc(conv_done, 1)

            conv(0)
            conv(1)
            dve.wait_ge(cum_ps, 1)
            link(dve.tensor_copy(acum, cols(banks[5][:, 0:64], 2)))
            dve.tensor_tensor(toend, banks[5][:, 64:96], acum[:, 0, :], ALU.subtract).then_inc(acum_ready, 1)
            for ci in range(2, 6):
                conv(ci)

            def y_out(k):
                c, g = k // 4, k % 4
                y = ym[:, c, 512 * g:512 * g + 512]
                dve.wait_ge(intra_ps, k + 1)
                dve.wait_ge(xd_ready, k + 1)
                if c == 0:
                    dve.tensor_tensor(y, banks[4][:, :], y, ALU.add).then_inc(ysum_ready, 1)
                    return
                link(dve.tensor_tensor(y, banks[4][:, :], y, ALU.add))
                link(dve.tensor_tensor(cols(xdte, 8), cols(banks[5][:, :], 8),
                                       over(ea[:, 8 * g:8 * g + 8], HD), ALU.mult))
                dve.tensor_tensor(y, y, xdte, ALU.add).then_inc(ysum_ready, 1)

            for k in range(8):
                c, g = k // 4, k % 4
                dve.wait_ge(xT_ps, k + 1)
                dve.wait_ge(xt_ready, k + 1)
                if k >= 2:
                    dve.wait_ge(intra_ps, k - 1)
                    if c == 0 or k - 2 < 4:
                        dve.wait_ge(xdte_ready, min(k - 1, 4))
                dve.tensor_tensor(cols(xdt[:, k % 2, :], 8), cols(banks[k % 2][:, :], 8),
                                  over(dtb[:, c, 8 * g:8 * g + 8], HD), ALU.mult).then_inc(xdt_ready, 1)
                for b in range(2):
                    dve.wait_ge(rows_ps, 2 * k + b + 1)
                    for i in range(4):
                        h = 8 * g + 4 * b + i
                        ins = dve.scalar_tensor_tensor(
                            seg[:, k % 2, 512 * b + P * i:512 * b + P * i + P], banks[2 + b][:, P * i:P * i + P],
                            acum[:, c, h:h + 1], C("segmask"), ALU.subtract, ALU.add)
                    ins.then_inc(seg_ready, 1)
                if k >= 1:
                    y_out(k - 1)
            y_out(7)
            for k in range(8):
                c, g = k // 4, k % 4
                y = ym[:, c, 512 * g:512 * g + 512]
                dve.wait_ge(rsy_ready, k + 1)
                dve.tensor_scalar(y, y, rsy[:, k:k + 1], math.sqrt(512.0), ALU.mult, ALU.mult).then_inc(yn_ready, 1)
                if k >= 1:
                    turned_y(k - 1)
            turned_y(7)
            for c in range(2):
                add_product(c, 2 * c, used_b, AT_MOUT + 4 * (c + 1))
            dve.wait_ge(x_ready, 12)

            def ple_dve(i, at):
                norm(3 + 2 * i)
                turn(4 + 3 * i, G(f"ple{i}"))
                for c in range(2):
                    for t in range(TT):
                        dve.wait_ge(sig_ready, 4 * i + 2 * c + t + 1)
                        link(dve.tensor_tensor(pret[:, t, :], banks[4 + 2 * c + t][:, :], sig[:, t, :], ALU.mult))
                        xv = x[:, t, 512 * c:512 * c + 512]
                        dve.tensor_tensor(xv, xv, pret[:, t, :], ALU.add).then_inc(x_ready, 1)
                dve.wait_ge(x_ready, 16 + 8 * i)

            ple_dve(0, AT_PLE0)

            norm(4)
            turn(5, G("kv"), second=G("s_norm"))
            project(["qk", "qk", "v", "v", "qk", "qk", "gate", "gate"], projb_act, projb_dve,
                    qkTb_ps, sq_b, qk_b, hss_b, hrs_b, hssb_ready, hrsb_ready)

            def softplus(h):
                dve.wait_ge(ln_ready, h + 1)
                if h >= 2:
                    dve.wait_ge(suf_ps, h - 1)
                link(dve.scalar_tensor_tensor(spz[:, h % 2, :], banks[h % 4][:, 0:384], 0.0, lnz[:, h % 2, :],
                                              ALU.max, ALU.add))
                v = spz[:, h % 2, :].rearrange("p (a b) -> p a b", a=3)[:, 0:3:2, :]
                dve.tensor_tensor(v, v, repeat(C("tri_lt"), 2), ALU.mult).then_inc(sp_ready, 1)

            def mask(h):
                dve.wait_ge(suf_ps, h + 1)
                if h >= 2:
                    dve.wait_ge(ob_ps, h - 1)
                dve.tensor_tensor(wz[:, h % 2, :], banks[h % 4][:, 0:384], mask3, ALU.add).then_inc(wm_ready, 1)

            def take(h):
                dve.wait_ge(ob_ps, h + 1)
                dve.wait_ge(projb_act, 16)
                for t in range(TT):
                    ins = dve.tensor_tensor(o_b[:, t, HD * h:HD * h + HD], banks[4 + h % 2][:, HD * t:HD * t + HD],
                                            gate_b[:, t, HD * h:HD * h + HD], ALU.mult)
                ins.then_inc(o_ready, 1)

            link(dve.memset(mask3, 0.0))
            for at in (0, 256):
                link(dve.tensor_copy(mask3[:, at:at + P], C("strictmask")))
            for h in range(SB_HEADS):
                softplus(h)
                if h >= 1:
                    mask(h - 1)
                if h >= 2:
                    take(h - 2)
            mask(SB_HEADS - 1)
            take(SB_HEADS - 2)
            take(SB_HEADS - 1)
            link(dve.memset(ga[:, 0:4], 1.0))
            turn(6, ga)
            for c in range(2):
                add_product(c, 2 * c, used_b, AT_SOUT + 2 * (c + 1))
            dve.wait_ge(x_ready, 20)
            ple_dve(1, AT_PLE1)

        @block.tensor
        def _(pe):
            ident = C("ident")

            def turn(i, waits):
                for n in range(4):
                    t, half = n // 2, n % 2
                    if half == 0:
                        pe.wait_ge(*waits[t])
                    if n >= 2 or i >= 1:
                        pe.wait_ge(turned, 4 * i + n - 1)
                    for k in range(4):
                        kt = 4 * half + k
                        ins = pe.transpose(banks[6 + n % 2][:, P * k:P * k + P], hn[:, t, P * kt:P * kt + P], ident)
                    ins.then_inc(turn_ps, 1)

            def product(lhs, chunk, bank0, full, used, units):
                n_kt = 4 * len(units)
                for i, (slot, value) in enumerate(units):
                    pe.wait_ge(full[slot], value)
                    w = cols(ring[:, slot, :], 4)
                    for t in range(TT):
                        for k in range(4):
                            kt = 4 * i + k
                            ins = pe.matmul(banks[bank0 + t][:, :], lhs[:, kt, P * t:P * t + P], w[:, k, :],
                                            start=kt == 0, stop=kt == n_kt - 1)
                    ins.then_inc(used, 1)

            def a_units(at, n):
                return [(u % RING, 16 * (u // RING + 1)) for u in range(at, at + n)]

            def b_units(at, n):
                return [(b_slot(u), 16 * (u // RING + 1)) for u in range(at, at + n)]

            pe.wait_ge(const_loaded, 16)
            pe.wait_ge(rows_loaded, 16 * 21)
            pe.transpose(banks[4][:, 0:95], rows_a[0:95, :], ident[0:95, 0:95]).then_inc(gains_ps, 1)
            pe.transpose(banks[5][:, 0:96], rows_c[0:96, :], ident[0:96, 0:96]).then_inc(gains_ps, 1)
            turn(0, [(hn_ready, 1), (hn_ready, 2)])
            pe.wait_ge(tab_loaded, 32)
            pe.wait_ge(ones_set, 1)
            pe.wait_ge(turned, 4)
            pe.matmul(banks[7][0:UNITS, 0:384], tab[0:BUCKETS + 1, :], onehot[0:BUCKETS + 1, :],
                      start=True, stop=True).then_inc(u_ps, 1)

            def project(kinds, lhs_of, at, mk, full, used, c_act, c_dve, t_ps, t_ready, qk):
                j = 0
                pend = None
                n_qk = [sum(k == "qk" for k in kinds[:c + 1]) for c in range(len(kinds))]

                def turn_qk(jj):
                    for t in range(TT):
                        pe.wait_ge(c_dve, 2 * jj + t + 1)
                        if jj >= 1:
                            pe.wait_ge(t_ready, 2 * (jj - 1) + t + 1)
                        for p in range(4):
                            ins = pe.transpose(banks[4 + t][:, P * p:P * p + P], qk[:, jj % 2, t, P * p:P * p + P],
                                               ident)
                        ins.then_inc(t_ps, 1)

                for c, kind in enumerate(kinds):
                    if c >= 2:
                        pe.wait_ge(c_act, 2 * (c - 1))
                        if n_qk[c - 2]:
                            pe.wait_ge(c_dve, 2 * n_qk[c - 2])
                    product(lhs_of(c), c, 2 * (c % 2), full, used, mk(at + 2 * c, 2))
                    if pend is not None:
                        turn_qk(pend)
                        pend = None
                    if kind == "qk":
                        pend = j
                        j += 1
                if pend is not None:
                    turn_qk(pend)

            pe.wait_ge(gains_ready, 3)
            project(["qk", "qk", "v", "qk", "qk", "v"], lambda c: hT, 0, a_units, full_a, used_a,
                    proj_act, proj_dve, qkT_ps, qkT_ready, qk_a)

            pe.wait_ge(hank_loaded, 16)
            pe.wait_ge(proj_act, 12)
            pe.wait_ge(proj_dve, 8)
            pe.wait_ge(qkT_ready, 8)

            def logits(u):
                for m in maps_of(u):
                    if m >= 3:
                        pe.wait_ge(probs_ready, m - 2)
                    r0, pair, bank = HD * (m % 2), m // 2, banks[m % 3]
                    for t, lo, hi in ((0, 0, 128), (1, 128, 384)):
                        n = hi - lo
                        pe.matmul(bank[:, lo:hi], qT_a[r0:r0 + HD, pair, P * t:P * t + P],
                                  kT_a[r0:r0 + HD, pair, 0:n], start=True, stop=False)
                        ins = pe.matmul(bank[:, lo:hi], C("flip"), hank[:, u, 256 - n:256], start=False, stop=True)
                    ins.then_inc(logits_ps, 1)

            logits(0)
            for u in range(UNITS + 1):
                if u + 1 < UNITS:
                    logits(u + 1)
                if u < UNITS:
                    pe.wait_ge(w_ready, u + 1)
                    pe.wait_ge(probs_ready, maps_of(u)[0] + 1)
                    if u >= 2:
                        pe.wait_ge(wT_ready, u - 1)
                    m, bank = maps_of(u)[0], banks[3 + u % 2]
                    for i in range(3):
                        ins = pe.transpose(bank[:, P * i:P * i + P], probs[:, m % 4, P * i:P * i + P], ident)
                    ins.then_inc(wT_ps, 1)
                if u >= 1:
                    v = u - 1
                    pe.wait_ge(wT_ready, v + 1)
                    if v >= 2:
                        pe.wait_ge(y_ready, v - 1)
                    bank, w = banks[5 + v % 2], wT[:, v % 2, :]
                    at, n = (128 * v, 128) if v < DIFF_HEADS else (512 + HD * (v - DIFF_HEADS), HD)
                    pe.matmul(bank[:, 0:n], w[:, 0:128], v_a[:, 0, at:at + n], start=True, stop=True)
                    pe.matmul(bank[:, 128:128 + n], w[:, 128:256], v_a[:, 0, at:at + n], start=True, stop=False)
                    pe.matmul(bank[:, 128:128 + n], w[:, 256:384], v_a[:, 1, at:at + n], start=False, stop=True)\
                      .then_inc(pv_ps, 1)
            turn(1, [(y_ready, UNITS)] * 2)
            pe.wait_ge(turned, 8)
            for c in range(2):
                product(hT, c, 2 * c, full_a, used_a, a_units(12 + 2 * c, 2))

            pe.wait_ge(x_ready, 4)
            for t in range(TT):
                for half in range(2):
                    pe.matmul(banks[2 * t + half][:, :], ident, x[:, t, 512 * half:512 * half + 512],
                              start=True, stop=True)
            turn(2, [(hn_ready, 3), (hn_ready, 4)])
            pe.wait_ge(turned, 12)
            pe.wait_ge(small_loaded, 16 * 14)
            for t in range(TT):
                for kt in range(KT):
                    ins = pe.matmul(banks[4][:, 36 * t:36 * t + 36], hT[:, kt, P * t:P * t + P], wr[:, kt, :],
                                    start=kt == 0, stop=kt == KT - 1)
            ins.then_inc(router_ps, 1)
            pe.wait_ge(msel_ready, 1)
            b = banks[5]
            pe.matmul(b[:, 0:32], C("tri_lt"), msel[:, 0, :], start=True, stop=True)
            pe.matmul(b[:, 32:64], C("ones"), msel[:, 0, :], start=True, stop=False)
            pe.matmul(b[:, 32:64], C("tri_lt"), msel[:, 1, :], start=False, stop=True)
            pe.matmul(b[:, 64:96], C("ones"), msel[:, 0, :], start=True, stop=False)
            pe.matmul(b[:, 64:96], C("ones"), msel[:, 1, :], start=False, stop=True).then_inc(rank_ps, 1)

            pe.wait_ge(npass_ready, 1)
            npass = pe.value_load(counts_i[0:1, 0:1], min_val=1, max_val=S // SLOTS)
            pe.sem_inc(fold_ps, 4)
            pe.sem_inc(scatter_ps, 1)
            with pe.Fori(0, npass) as r:
                for n in range(4):
                    t, half = n // 2, n % 2
                    if n < 2:
                        pe.wait_ge(sel_ready, r * 2 + (2 if n else 1))
                    if n == 0:
                        pe.wait_ge(sel_ready, r * 2 + 2)
                    if n >= 2:
                        pe.wait_ge(selT_ready, r * 4 + (n - 1))
                    for k in range(4):
                        qd = 4 * half + k
                        ins = pe.transpose(banks[6 + n % 2][:, P * k:P * k + P], selw[:, t, P * qd:P * qd + P], ident)
                    ins.then_inc(selT_ps, 1)
                with pe.Fori(0, QUADS) as g:
                    q = r * QUADS + g
                    pe.wait_ge(hid_ready, q * QUAD + 4)
                    for b in range(2):
                        for k in range(4):
                            kt = 4 * b + k
                            for t in range(TT):
                                ins = pe.matmul(banks[4 + b][:, P * k:P * k + P], hn[:, t, P * kt:P * kt + P],
                                                sel[:, t, bass.ds(g * P, P)], start=t == 0, stop=t == 1)
                        ins.then_inc(gather_ps, 1)
                    pe.wait_ge(xg_ready, q * 2 + 4)
                    pe.wait_ge(selT_ready, r * 4 + 4)
                    pe.wait_ge(dn0_ready, q + 1)
                    pe.wait_ge(dn1_ready, q + 1)

                    def fold(e):
                        pe.wait_ge(h_ready, q * QUAD + (e + 5))
                        if e >= 2:
                            pe.wait_ge(hid_ready, q * QUAD + (e + 3))
                        for i in range(4):
                            at = 256 * (i // 2) + i % 2
                            ins = pe.matmul(banks[4 + e % 2][:, SLOTS * i:SLOTS * i + SLOTS],
                                            hpre[:, e % 2, at:256 * (i // 2) + 256:2], C("fold"),
                                            start=True, stop=True)
                        ins.then_inc(fold_ps, 1)

                    for e in range(QUAD):
                        if e >= 2:
                            pe.wait_ge(h_ready, q * QUAD + (e + 3))
                        for i in range(2):
                            slot = e_slot(2 * e + i)
                            pe.wait_ge(full_e[slot], q * 16 + 16)
                            w = cols(ring[:, slot, :], KT)
                            for kt in range(KT):
                                c0 = SLOTS * (kt % 4)
                                ins = pe.matmul(banks[6 + e % 2][c0:c0 + SLOTS, 256 * i:256 * i + 256],
                                                xg[:, kt, SLOTS * e:SLOTS * e + SLOTS], w[:, kt, :],
                                                start=kt < 4, stop=kt >= 4)
                            ins.then_inc(used_e, 1)
                        if e >= 1:
                            fold(e - 1)
                    fold(3)
                    for e in range(QUAD):
                        pe.wait_ge(full_e[e_slot(8 + e)], q * 16 + 16)
                    pe.wait_ge(hid_ready, q * QUAD + 8)
                    for half in range(2):
                        for f in range(2):
                            for e in range(QUAD):
                                w = cols(ring[:, e_slot(8 + e), :], 2)
                                ins = pe.matmul(banks[6 + half][SLOTS * e:SLOTS * e + SLOTS, :],
                                                hid[:, e, SLOTS * f:SLOTS * f + SLOTS],
                                                w[:, f, 512 * half:512 * half + 512],
                                                start=f == 0, stop=f == 1)
                                if half == 1 and f == 1:
                                    ins.then_inc(used_e, 1)
                                elif half == 0 and f == 1 and e == 3:
                                    ins.then_inc(dn0_ps, 1)
                    pe.wait_ge(selq_ready, q + 2)
                    for half in range(2):
                        pe.wait_ge((dn0_ready, dn1_ready)[half], q + 2)
                        for t in range(TT):
                            ins = pe.matmul(banks[2 * t + half][:, :], selwT_q[:, P * t:P * t + P],
                                            dn[:, 512 * half:512 * half + 512], start=False, stop=False,
                                            skip_group_check=True)
                    ins.then_inc(scatter_ps, 1)

            turn(3, [(hn_ready, 5), (hn_ready, 6)])
            pe.wait_ge(turned, 16)
            for t in range(TT):
                for kt in range(KT):
                    ins = pe.matmul(banks[4][:, 32 * t:32 * t + 32], hT[:, kt, P * t:P * t + P], wdt[:, kt, :],
                                    start=kt == 0, stop=kt == KT - 1)
            ins.then_inc(dt_ps, 1)
            for ci in range(6):
                if ci >= 2:
                    pe.wait_ge(conv_done, ci - 1)
                slots = b_units(2 * ci, 2)
                for slot, value in slots:
                    pe.wait_ge(full_b[slot], value)
                for k in range(4):
                    for kt in range(KT):
                        w = cols(ring[:, slots[kt // 4][0], :], 4)
                        ins = pe.matmul(banks[2 * (ci % 2) + k // 2][:, 256 * (k % 2):256 * (k % 2) + 256],
                                        w[:, kt % 4, P * k:P * k + P], hT[:, kt, :], start=kt == 0, stop=kt == KT - 1)
                ins.then_inc(used_b, 2)
                if ci == 1:
                    pe.wait_ge(dtA_ready, 1)
                    b = banks[5]
                    for c in range(TT):
                        pe.matmul(b[:, 32 * c:32 * c + 32], C("tri_le"), dtA[:, c, :], start=True, stop=True)
                    pe.matmul(b[:, 64:96], C("ones"), dtA[:, 0, :], start=True, stop=True).then_inc(cum_ps, 1)
            for c in range(4):
                if c < 2:
                    pe.wait_ge(conv_done, 5 + c)
                else:
                    pe.wait_ge(z_ready, 2 * (c - 1))
                product(hT, c, 2 * (c % 2), full_b, used_b, b_units(AT_Z + 2 * c, 2))
            pe.wait_ge(xc_ready, 6)
            for g in range(4):
                ins = pe.transpose(banks[4][:, P * g:P * g + P], xc[:, 16 + g, 0:P], ident)
            ins.then_inc(bt_ps, 1)
            for c in range(TT):
                for g in range(4):
                    ins = pe.matmul(banks[6 + c][:, P * g:P * g + P], xc[:, 16 + g, P * c:P * c + P],
                                    xc[:, 20 + g, P * c:P * c + P], start=True, stop=True)
                ins.then_inc(cb_ps, 1)
            pe.wait_ge(z_ready, 8)
            pe.wait_ge(acum_ready, 1)

            def step_in(k):
                c, g = k // 4, k % 4
                if k >= 2:
                    pe.wait_ge(xdt_ready, k - 1)
                    pe.wait_ge(xt_ready, k - 1)
                for i in range(4):
                    ins = pe.transpose(banks[k % 2][:, P * i:P * i + P], xc[:, 4 * g + i, P * c:P * c + P], ident)
                ins.then_inc(xT_ps, 1)
                for b in range(2):
                    if k >= 1:
                        pe.wait_ge(seg_ready, 2 * k - 1 + b)
                    for i in range(4):
                        h = 8 * g + 4 * b + i
                        ins = pe.matmul(banks[2 + b][:, P * i:P * i + P], dtA[:, c, h:h + 1].to_broadcast([P, P]),
                                        C("tri_le"), start=True, stop=True)
                    ins.then_inc(rows_ps, 1)

            def step_out(k):
                c, g = k // 4, k % 4
                pe.wait_ge(xdt_ready, k + 1)
                pe.wait_ge(m_ready, 2 * k + 2)
                if k == 0:
                    pe.wait_ge(bt_ready, 1)
                if k >= 1:
                    pe.wait_ge(ysum_ready, k)
                    pe.wait_ge(state_ready, min(k, 4))
                if c == 0:
                    pe.wait_ge(xdte_ready, k + 1)
                    pe.matmul(banks[5][:, :], btok[:, P * g:P * g + P], xdte, start=True, stop=True)
                else:
                    pe.matmul(banks[5][:, :], xc[:, 20 + g, P:2 * P], state[:, 512 * g:512 * g + 512],
                              start=True, stop=True)
                for i in range(8):
                    ins = pe.matmul(banks[4][:, HD * i:HD * i + HD], seg[:, k % 2, P * i:P * i + P],
                                    xdt[:, k % 2, HD * i:HD * i + HD], start=True, stop=True)
                ins.then_inc(intra_ps, 1)

            step_in(0)
            for k in range(8):
                if k + 1 < 8:
                    step_in(k + 1)
                step_out(k)
            for k in range(8):
                c, g = k // 4, k % 4
                pe.wait_ge(yn_ready, k + 1)
                if k >= 2:
                    pe.wait_ge(yT_ready, k - 1)
                for i in range(4):
                    ins = pe.transpose(banks[6 + k % 2][:, P * i:P * i + P],
                                       ym[:, c, 512 * g + P * i:512 * g + P * i + P], ident)
                ins.then_inc(yT_ps, 1)
            pe.wait_ge(yT_ready, 8)
            pe.wait_ge(seg_ready, 16)
            for c in range(2):
                product(yT, c, 2 * c, full_b, used_b, b_units(AT_MOUT + 4 * c, 4))

            def ple_pe(i, at):
                pe.wait_ge(p_loaded, 16 * (i + 1))
                if i == 0:
                    pe.wait_ge(yT_ready, 8)
                for kp in range(2):
                    for t in range(TT):
                        ins = pe.transpose(banks[6][:, 256 * kp + P * t:256 * kp + P * t + P],
                                           pbuf[:, t, P * kp:P * kp + P], ident)
                ins.then_inc(pT_ps, 1)
                pe.wait_ge(pT_ready, i + 1)
                turn(4 + 3 * i, [(hn_ready, 7 + 4 * i), (hn_ready, 8 + 4 * i)])
                pe.wait_ge(turned, 20 + 12 * i)
                slot, value = b_units(at, 1)[0]
                pe.wait_ge(full_b[slot], value)
                w = cols(ring[:, slot, :], 2)
                for c in range(2):
                    for t in range(TT):
                        for kp in range(2):
                            ins = pe.matmul(banks[4 + 2 * c + t][:, :], pT[:, kp, P * t:P * t + P],
                                            w[:, kp, 512 * c:512 * c + 512], start=kp == 0, stop=kp == 1)
                ins.then_inc(used_b, 1)
                for c in range(2):
                    product(hT, c, 2 * c, full_b, used_b, b_units(at + 1 + 2 * c, 2))

            ple_pe(0, AT_PLE0)

            pe.wait_ge(x_ready, 16)
            turn(5, [(hn_ready, 9), (hn_ready, 10)])
            pe.wait_ge(turned, 24)
            project(["qk", "qk", "v", "v", "qk", "qk", "gate", "gate"], lambda c: hT if c < 4 else hT2, AT_KV,
                    b_units, full_b, used_b, projb_act, projb_dve, qkTb_ps, qkTb_ready, qk_b)
            pe.wait_ge(projb_act, 16)
            pe.wait_ge(qkTb_ready, 8)

            def scores(h):
                if h >= 4:
                    pe.wait_ge(wm_ready, h - 3)
                r0, pair, bank = HD * (h % 2), h // 2, banks[h % 4]
                pe.matmul(bank[:, 0:256], kT_b[r0:r0 + HD, pair, 0:P], qT_b[r0:r0 + HD, pair, :],
                          start=True, stop=False, skip_group_check=True)
                pe.matmul(bank[:, 256:384], kT_b[r0:r0 + HD, pair, P:2 * P], qT_b[r0:r0 + HD, pair, P:2 * P],
                          start=False, stop=False, skip_group_check=True).then_inc(zz_ps, 1)

            def suffix(h):
                pe.wait_ge(sp_ready, h + 1)
                bank, sp_ = banks[h % 4], spz[:, h % 2, :]
                pe.matmul(bank[:, 128:256], C("negones"), sp_[:, 256:384], start=False, stop=False,
                          skip_group_check=True)
                pe.matmul(bank[:, 0:384], C("sufneg"), sp_, start=False, stop=True, skip_group_check=True)\
                  .then_inc(suf_ps, 1)

            def outputs(h):
                pe.wait_ge(we_ready, h + 1)
                if h >= 2:
                    pe.wait_ge(o_ready, h - 1)
                bank, w, at = banks[4 + h % 2], wz[:, h % 2, :], HD * h
                pe.matmul(bank[:, 0:HD], w[:, 0:128], v_b[:, 0, at:at + HD], start=True, stop=True)
                pe.matmul(bank[:, HD:2 * HD], w[:, 128:256], v_b[:, 0, at:at + HD], start=True, stop=False)
                pe.matmul(bank[:, HD:2 * HD], w[:, 256:384], v_b[:, 1, at:at + HD], start=False, stop=True)\
                  .then_inc(ob_ps, 1)

            scores(0)
            scores(1)
            for h in range(SB_HEADS):
                if h + 2 < SB_HEADS:
                    scores(h + 2)
                suffix(h)
                if h >= 1:
                    outputs(h - 1)
            outputs(SB_HEADS - 1)
            turn(6, [(o_ready, SB_HEADS)] * 2)
            pe.wait_ge(turned, 28)
            for c in range(2):
                product(hT, c, 2 * c, full_b, used_b, b_units(AT_SOUT + 2 * c, 2))
            ple_pe(1, AT_PLE1)


INPUTS = ["x", "norm1_g", "w_in", "diff_q_g", "diff_k_g", "lambda_q1", "lambda_k1", "lambda_q2", "lambda_k2",
          "diff_sub_g", "moba_q_g", "moba_k_g", "rel_bias", "w_out", "norm2_g", "router_group",
          "router_expert", "w_gate", "w_up", "w_down", "p_2", "m_norm_2", "m_in_2", "m_conv_w_2",
          "m_conv_b_2", "m_dt_bias_2", "m_A_log_2", "m_D_2", "m_ynorm_2", "m_out_2", "kv_norm_2",
          "w_kv_2", "k_norm_2", "s_norm_2", "s_in_2", "q_norm_2", "s_out_2", "ple_norm_2",
          "ple_gate_2", "ple_proj_2"]


def kernel(**inputs):
    import concourse.bacc as bacc
    from concourse.bass_utils import run_bass_kernel_spmd

    nc = bacc.Bacc("TRN2", target_bir_lowering=False, num_devices=1)
    arrays = {f"in_{n}": np.ascontiguousarray(inputs[n]) for n in INPUTS}
    arrays["in_consts"] = constants()[0]
    arrays["in_onehot"] = bucket_onehot()
    d = {n[3:]: nc.dram_tensor(n, a.shape, F32, kind="ExternalInput").ap() for n, a in arrays.items()}
    out = nc.dram_tensor("out_dram", (1, S, D), F32, kind="ExternalOutput").ap()
    two_blocks(nc, d, out)
    r = run_bass_kernel_spmd(nc, [arrays], core_ids=[0])
    return r.results[0]["out_dram"]
```

```python
import math
from contextlib import ExitStack

import numpy as np

import concourse.bass as bass
from concourse import mybir

F32 = mybir.dt.float32
R32 = mybir.dt.float32r
I32 = mybir.dt.int32
ALU = mybir.AluOpType
ACT = mybir.ActivationFunctionType
AX = mybir.AxisListType

P = 128
D = 1024
S = 256
TT = S // P
KT = D // P
HD = 64
DIFF_HEADS, MOBA_HEADS = 4, 8
UNITS = DIFF_HEADS + MOBA_HEADS
MAPS = 2 * DIFF_HEADS + MOBA_HEADS
BUCKETS, MAX_DISTANCE = 32, 2048
EXPERTS, GROUPS, PER_GROUP, HIDDEN = 32, 4, 8, 256
SLOTS = 32
QUAD = 4
QUADS = EXPERTS // QUAD
D_INNER, SSM_HEADS, CONV_K = 2048, 32, 4
CONV_TILES = 24
SB_HEADS = 16
EPS = 1e-6
NEG = -1e30
LAMBDA_INIT = 0.8 - 0.6 * math.exp(-0.3 * 0)

RING = 12
UNIT = 2048
UNITS_A = 16
UNITS_B = 58
SHORT = 7
HI_SLOTS = (11, 0, 1, 2)
HT_HI_SLOT = 3
ARENA = 19776


def bucket_onehot():
    out = np.zeros((BUCKETS + 1, 384), np.float32)
    exact = BUCKETS // 2
    for i in range(384):
        n = S - 1 - i
        if n < 0:
            out[BUCKETS, i] = NEG
            continue
        b = n if n < exact else min(BUCKETS - 1, exact + int(
            math.log(n / exact) / math.log(MAX_DISTANCE / exact) * (BUCKETS - exact)))
        out[b, i] = 1.0
    return out


CONSTS = ["ident", "tri_le", "tri_lt", "flip", "sufneg", "negones", "ones", "segmask", "strictmask", "fold", "iota", "iota_low", "passes", "neghalf"]


def constants():
    a, b = np.arange(P)[:, None], np.arange(P)[None, :]
    parts = {
        "ident": a == b, "tri_le": a <= b, "tri_lt": a < b, "flip": a + b == P - 1,
        "sufneg": -1.0 * (a >= b), "negones": -np.ones((P, P)), "ones": np.ones((P, P)),
        "segmask": np.where(a <= b, 0.0, NEG),
        "strictmask": np.where(a < b, 0.0, NEG),
        "fold": (a % SLOTS) == np.arange(SLOTS)[None, :],
        "iota": np.broadcast_to(np.arange(32.0), (P, 32)),
        "iota_low": np.broadcast_to(np.arange(32.0) - 99.0, (P, 32)),
        "passes": np.broadcast_to(SLOTS * np.arange(8.0), (P, 8)),
        "neghalf": np.full((P, 8), -0.5),
    }
    at, col = {}, 0
    for name in CONSTS:
        at[name] = (col, parts[name].shape[1])
        col += parts[name].shape[1]
    return np.concatenate([np.asarray(parts[n], np.float32) for n in CONSTS], 1), at


def two_blocks(nc, d, out):
    _, const_at = constants()
    n_const = sum(w for _, w in const_at.values())
    ctx = ExitStack()
    with ctx:
        def sb(name, shape, dt=F32):
            return ctx.enter_context(nc.sbuf_tensor(name, shape, dt))

        def sem(name):
            return ctx.enter_context(nc.semaphore(name))

        base = -(-nc.sbuf_base // 64) * 64
        sb("slab", [P, 16 + RING * UNIT + ARENA + KT * S])

        def twin(name, shape, at):
            return (nc.alloc_sbuf_tensor_at(name, shape, F32, offset=base + 4 * at),
                    nc.alloc_sbuf_tensor_at(name + "_r", shape, R32, offset=base + 4 * at))

        ring, ring_r = twin("ring", [P, RING, UNIT], 0)
        arena, arena_r = twin("arena", [P, ARENA], RING * UNIT)
        hT, hT_lo = twin("hT", [P, KT, S], RING * UNIT + ARENA)
        hT_hi = ring_r[:, HT_HI_SLOT, :].rearrange("p (a b) -> p a b", a=KT)
        consts = sb("consts", [P, n_const])
        x = sb("x_residual", [P, TT, D])
        hn = sb("hn", [P, TT, D])
        gcol = sb("gcol", [P, 96])
        ccol = sb("ccol", [P, 96])
        g2 = sb("g2", [P, KT])
        gq = sb("gq", [P, 3])
        ga = sb("ga", [P, KT])
        headp = sb("headp", [P, 3, SSM_HEADS])
        nlam = sb("nlam", [P, 1])
        ss = sb("ss", [P, 6, 2, TT])
        rs = sb("rs", [P, 6, TT])
        pbuf = sb("pbuf", [P, TT, 256])
        counts_i = sb("counts_i", [P, 2], I32)
        banks = [ctx.enter_context(nc.psum_tensor(f"bank{i}", [P, 512], F32)) for i in range(8)]

        def C(name):
            at, n = const_at[name]
            return consts[:, at:at + n]

        class Arena:
            def __init__(self):
                self.at = 0

            def __call__(self, *dims):
                return self.twin(*dims)[0]

            def twin(self, *dims):
                n = math.prod(dims)
                self.at += n
                assert self.at <= ARENA
                return [self.view(a[:, self.at - n:self.at], dims) for a in (arena, arena_r)]

            @staticmethod
            def view(v, dims):
                if len(dims) == 2:
                    v = v.rearrange("p (a b) -> p a b", a=dims[0])
                if len(dims) == 3:
                    v = v.rearrange("p (a b c) -> p a b c", a=dims[0], b=dims[1])
                return v

        def over(ap, *dims):
            n = ap.shape[1]
            return ap.unsqueeze(2).to_broadcast([P, n, dims[0]])

        def repeat(ap, n):
            return ap.unsqueeze(1).to_broadcast([P, n, ap.shape[1]])

        def cols(ap, n):
            return ap.rearrange("p (a b) -> p a b", a=n)

        GAIN = {"norm1": 0, "m_norm": 8, "kv": 16, "s_norm": 24, "ple0": 32, "ple1": 40,
                "ynorm": 48, "conv_b": 64, "dq": 88, "dk": 89, "mq": 90, "mk": 91, "sq": 92,
                "sk": 93, "sub": 94}

        A = Arena()
        qk_a = A(2, TT, 512)
        sq_a = A(TT, 512)
        v_a = A(TT, D)
        qT_a, kT_a = A(KT, S), A(KT, S)
        hank = A(UNITS, 256)
        probs = A(4, 384)
        wT = A(2, 384)
        nmax, psum_, prec = A(MAPS, TT), A(MAPS, TT), A(MAPS, TT)
        ssd, rsd = A(UNITS, TT), A(UNITS, TT)
        hss, hrs = A(TT, 8), A(TT, 8)
        lamv = A(4, 64)
        lame = A(2)
        rows_a, rows_c = A(P), A(P)
        u_sb, tab, onehot = A(384), A(UNITS), A(384)
        y_a = hn

        M = Arena()
        sel = M(TT, EXPERTS * SLOTS)
        selw = M(TT, EXPERTS * SLOTS)
        selwT = M(QUADS, S)
        xg = M(KT, P)
        selwT_q = M(S)
        hpre = M(2, 512)
        sg = M(QUAD, 64)
        hid = M(QUAD, 64)
        dn = M(D)
        rl = M(TT, 36)
        gmx, gex, gsum, gidx = M(TT), M(TT, GROUPS), M(TT), M(TT)
        geq, gc = M(TT, GROUPS), M(TT, GROUPS)
        el, el2, eq, cand = (M(TT, EXPERTS) for _ in range(4))
        oh1, oh2, wsel, msel, rk = (M(TT, EXPERTS) for _ in range(5))
        m1, m2, i1, w1, w2 = (M(TT) for _ in range(5))
        cmax, cpass = M(1), M(8)

        B = Arena()
        xc, xc_r = B.twin(CONV_TILES, S)
        z, z_r = B.twin(TT, D_INNER)
        ym = B(TT, D_INNER)
        seg = B(2, 1024)
        xdt = B(2, 512)
        xdte = B(512)
        cb = B(TT, 512)
        btok = B(512)
        dtb, dtA = B(TT, SSM_HEADS), B(TT, SSM_HEADS)
        dta, dtu, dtw, dtl, dtq, dtv = (cols(seg[:, 0, 64 * i:64 * i + 64], TT) for i in range(6))
        acum, toend, ea = B(TT, SSM_HEADS), B(SSM_HEADS), B(SSM_HEADS)
        negA = B(SSM_HEADS)
        ssy, rsy = B(8), B(8)
        state = hn[:, :, :].rearrange("p a b -> p (a b)")
        yT, yT_lo = xc[:, 0:16, :], xc_r[:, 0:16, :]
        yT_hi = z_r.rearrange("p a b -> p (a b)").rearrange("p (a b) -> p a b", a=16)

        E_ = Arena()
        E_.at = 16896
        pT = E_(TT, S)
        sig = E_(2, 512)
        pret = E_(2, 512)

        K = Arena()
        qk_b = K(2, TT, 512)
        sq_b = K(TT, 512)
        v_b = K(TT, D)
        gate_b = K(TT, D)
        qT_b, kT_b = K(KT, S), K(KT, S)
        hT2, hT2_lo = K.twin(KT, S)
        _, hT2_hi = K.twin(KT, S)
        mask3 = K(384)
        absz, expz, lnz, spz, wz = (K(2, 384) for _ in range(5))
        hss_b, hrs_b = K(TT, 8), K(TT, 8)
        o_b = hn

        wr = sb("wr", [P, KT, 36])
        wdt = sb("wdt", [P, KT, SSM_HEADS])

        bias_dram = nc.dram_tensor("bias_rows", (UNITS, 384), F32, kind="Internal").ap()

        hi_a, lo_a, hi_w, lo_w, hi_turned, lo_turned, turned2, hi_turned2, lo_turned2, yT_hi_ready, yT_lo_ready, tap_ready = map(
            sem, ("hi_a", "lo_a", "hi_w", "lo_w", "hi_turned", "lo_turned", "turned2", "hi_turned2", "lo_turned2",
                  "yT_hi_ready", "yT_lo_ready", "tap_ready"))
        x_loaded, const_loaded, rows_loaded, small_loaded, lam_loaded = map(sem, (
            "x_loaded", "const_loaded", "rows_loaded", "small_loaded", "lam_loaded"))
        tab_loaded, ones_set, u_ps, u_ready, u_stored, hank_loaded = map(sem, (
            "tab_loaded", "ones_set", "u_ps", "u_ready", "u_stored", "hank_loaded"))
        full_a = [sem(f"full_a{i}") for i in range(RING)]
        full_b = [sem(f"full_b{i}") for i in range(SHORT)]
        used_a, used_e, used_b = map(sem, ("used_a", "used_e", "used_b"))
        act_step, dve_step, pool_step = map(sem, ("act_step", "dve_step", "pool_step"))
        gains_ps, gains_ready, lam_sum, lam_exp = map(sem, (
            "gains_ps", "gains_ready", "lam_sum", "lam_exp"))
        ss_ready, hn_ready, turn_ps, turned, x_ready = map(sem, (
            "ss_ready", "hn_ready", "turn_ps", "turned", "x_ready"))
        proj_act, proj_dve, qkT_ps, qkT_ready = map(sem, ("proj_act", "proj_dve", "qkT_ps", "qkT_ready"))
        logits_ps, nmax_ready, probs_ready, w_ready, wT_ps, wT_ready, pv_ps, sqd_ready, y_ready = map(
            sem, ("logits_ps", "nmax_ready", "probs_ready", "w_ready", "wT_ps", "wT_ready", "pv_ps",
                  "sqd_ready", "y_ready"))
        router_ps, gsub_ready, gexp_ready, msel_ready, rank_ps, npass_ready, edif_ready, eexp_ready = map(
            sem, ("router_ps", "gsub_ready", "gexp_ready", "msel_ready", "rank_ps", "npass_ready",
                  "edif_ready", "eexp_ready"))
        pass_step, sel_ready, selT_ps, selT_ready = map(sem, (
            "pass_step", "sel_ready", "selT_ps", "selT_ready"))
        gather_ps, xg_ready, h_ready, fold_ps, silu_ready, hid_ready, dn0_ps = map(sem, (
            "gather_ps", "xg_ready", "h_ready", "fold_ps", "silu_ready", "hid_ready", "dn0_ps"))
        dn0_ready, dn1_ready, selq_ready, scatter_ps = map(sem, (
            "dn0_ready", "dn1_ready", "selq_ready", "scatter_ps"))
        dt_ps, dta_ready, dtu_ready, dtw_ready, dtl_ready, a_ready, dtA_ready, cum_ps = map(sem, (
            "dt_ps", "dta_ready", "dtu_ready", "dtw_ready", "dtl_ready", "a_ready", "dtA_ready", "cum_ps"))
        acum_ready, decay_ready, conv_done, xc_ready, z_ready = map(sem, (
            "acum_ready", "decay_ready", "conv_done", "xc_ready", "z_ready"))
        bt_ps, bt_ready, cb_ps, cb_ready, xT_ps, xt_ready, xdt_ready, xdte_ready = map(sem, (
            "bt_ps", "bt_ready", "cb_ps", "cb_ready", "xT_ps", "xt_ready", "xdt_ready", "xdte_ready"))
        rows_ps, seg_ready, dec_ready, m_ready, intra_ps, state_ready, ysum_ready, yz_ready = map(sem, (
            "rows_ps", "seg_ready", "dec_ready", "m_ready", "intra_ps", "state_ready", "ysum_ready",
            "yz_ready"))
        ssy_ready, yn_ready, yT_ps, yT_ready, xd_ready = map(sem, (
            "ssy_ready", "yn_ready", "yT_ps", "yT_ready", "xd_ready"))
        p_loaded, pT_ps, pT_ready, sig_ready = map(sem, ("p_loaded", "pT_ps", "pT_ready", "sig_ready"))
        projb_act, projb_dve, qkTb_ps, qkTb_ready = map(sem, (
            "projb_act", "projb_dve", "qkTb_ps", "qkTb_ready"))
        zz_ps, ln_ready, sp_ready, suf_ps, we_ready, wm_ready, ob_ps, o_ready = map(sem, (
            "zz_ps", "ln_ready", "sp_ready", "suf_ps", "we_ready", "wm_ready", "ob_ps",
            "o_ready"))
        out_stored = sem("out_stored")
        rs_ready, hss_ready, hrs_ready, hssb_ready, hrsb_ready, rsd_ready, rsy_ready = map(sem, (
            "rs_ready", "hss_ready", "hrs_ready", "hssb_ready", "hrsb_ready", "rsd_ready", "rsy_ready"))

        def wide(w, c, half):
            return w[512 * half:512 * half + 512, 512 * c:512 * c + 512].rearrange("(k p) n -> p k n", p=P)

        w_in, w_out = d["w_in"][0], d["w_out"][0]
        units_a = [wide(w_in, c, h) for c in range(6) for h in range(2)]
        units_a += [wide(w_out, c, h) for c in range(2) for h in range(2)]
        m_in, m_out = d["m_in_2"][0], d["m_out_2"][0]
        XBC_ORDER = [4, 5, 0, 1, 2, 3]
        m_xbc = m_in[:, D_INNER:]
        units_b = [wide(m_xbc, c, h) for c in XBC_ORDER for h in range(2)]
        units_b += [wide(m_in, c, h) for c in range(4) for h in range(2)]
        units_b += [wide(m_out, c, h) for c in range(2) for h in range(4)]
        ple = [[wide(d["ple_gate_2"][i], c, h) for c in range(2) for h in range(2)] for i in range(2)]
        for i in range(2):
            ple[i].insert(1, d["ple_proj_2"][i].rearrange("(k p) n -> p k n", p=P))
        AT_Z, AT_MOUT, AT_PLE0 = 12, 20, 28
        units_b += ple[0]
        AT_KV = len(units_b)
        units_b += [wide(d["w_kv_2"], c, h) for c in range(4) for h in range(2)]
        units_b += [wide(d["s_in_2"][0], c, h) for c in range(4) for h in range(2)]
        AT_SOUT = len(units_b)
        units_b += [wide(d["s_out_2"][0], c, h) for c in range(2) for h in range(2)]
        AT_PLE1 = len(units_b)
        units_b += ple[1]
        assert len(units_a) == UNITS_A and len(units_b) == UNITS_B

        gate_v = d["w_gate"][0].rearrange("e (p k) n -> e p (k n)", k=KT)
        up_v = d["w_up"][0].rearrange("e (p k) n -> e p (k n)", k=KT)
        down_v = d["w_down"][0].rearrange("e (p f) n -> e p (f n)", f=2)
        QUAD_UNITS = [(v, e) for e in range(QUAD) for v in (gate_v, up_v)] + [(down_v, e) for e in range(QUAD)]

        def e_slot(j):
            return (UNITS_A + j) % RING

        def e_full(slot):
            return 16 * (1 + sum(a_slot(n) == slot for n in range(UNITS_A)))

        def a_slot(n):
            return 4 + (n % SHORT - UNITS_A % SHORT) % SHORT

        def b_slot(n):
            return (UNITS_A + n % SHORT) % RING

        def b_full(n):
            return full_b[n % SHORT], 16 * (n // SHORT + 1)

        SPLIT = [n for n in range(UNITS_B) if n not in (AT_PLE0 + 1, AT_PLE1 + 1)]
        H_KV, H_MOUT = SPLIT.index(AT_KV), SPLIT.index(AT_MOUT)
        H_PLE0, H_SOUT, H_PLE1 = SPLIT.index(AT_PLE0), SPLIT.index(AT_SOUT), SPLIT.index(AT_PLE1)

        class WeightsA:
            split, slot, used, hi_ready, lo_ready = range(UNITS_A), a_slot, used_a, hi_a, lo_a

            def full(n):
                return full_a[a_slot(n)], 16 * (n // SHORT + 1)

        class WeightsB:
            split, slot, used, hi_ready, lo_ready, full = SPLIT, b_slot, used_b, hi_w, lo_w, b_full

        def w_hi(h):
            return ring_r[:, HI_SLOTS[h % 4], :]

        def maps_of(u):
            return [2 * u, 2 * u + 1] if u < DIFF_HEADS else [u + DIFF_HEADS]

        def unit_of(m):
            return m // 2 if m < 2 * DIFF_HEADS else m - DIFF_HEADS

        SMALL_LOADS = 10
        ROW_LOADS = 15

        SPLIT_TURNS = [0, 1, 3, 4, 5, 6, 7]

        LOGIT_BANKS = [0, 1, 2, 7]

        YZ_ORDER = [0, 1, 2, 4, 3, 5, 6, 7]

        TAIL_ORDER = [4 * c + g for g in range(4) for c in range(TT)]

        block = ctx.enter_context(nc.Block())

        @block.sync
        def _(sp):
            xin = d["x"][0].rearrange("(t p) n -> t p n", p=P)
            for t in range(TT):
                sp.dma_start(x[:, t, :], xin[t]).then_inc(x_loaded, 16)
            sp.dma_start(cols(ring[:, a_slot(0), :], 4), units_a[0]).then_inc(full_a[a_slot(0)], 16)
            sp.dma_start(consts[:, :], d["consts"]).then_inc(const_loaded, 16)
            for name, n in (("dq", "diff_q_g"), ("dk", "diff_k_g"), ("mq", "moba_q_g"), ("mk", "moba_k_g"),
                            ("sq", "q_norm_2"), ("sk", "k_norm_2")):
                at = GAIN[name]
                sp.dma_start(cols(rows_a[at:at + 1, :], 2), bass.AP(d[n].tensor, 0, [[HD, 1], [0, 2], [1, HD]]))\
                  .then_inc(rows_loaded, 16)
            sp.dma_start(rows_a[GAIN["sub"]:GAIN["sub"] + 1, :], d["diff_sub_g"]).then_inc(rows_loaded, 16)
            for n in range(1, UNITS_A):
                if n == 2:
                    sp.dma_start(tab[0:BUCKETS, :], d["rel_bias"]).then_inc(tab_loaded, 16)
                    sp.dma_start(onehot[0:BUCKETS + 1, :], d["onehot"]).then_inc(tab_loaded, 16)
                    for i, m in enumerate(("lambda_q1", "lambda_k1", "lambda_q2", "lambda_k2")):
                        sp.dma_start(lamv[:, i, :], d[m].to_broadcast([P, HD])).then_inc(lam_loaded, 16)
                    sp.wait_ge(rows_loaded, 16 * ROW_LOADS)
                if n == 6:
                    sp.dma_start(pbuf[:, :, :], d["p_2"][0, 0].rearrange("(t p) n -> p t n", p=P)).then_inc(p_loaded, 16)
                    for i, m in enumerate(("m_dt_bias_2", "m_A_log_2", "m_D_2")):
                        sp.dma_start(headp[:, i, :], d[m].to_broadcast([P, SSM_HEADS])).then_inc(small_loaded, 16)
                    sp.dma_start(g2[:, :], d["norm2_g"].rearrange("o (p k) -> (o p) k", k=KT))\
                      .then_inc(small_loaded, 16)
                    sp.dma_start(wr[:, :, 0:GROUPS], d["router_group"][0].rearrange("(p k) n -> p k n", k=KT))\
                      .then_inc(small_loaded, 16)
                    for g in range(GROUPS):
                        sp.dma_start(wr[:, :, GROUPS + PER_GROUP * g:GROUPS + PER_GROUP * (g + 1)],
                                     d["router_expert"][0, g].rearrange("(p k) n -> p k n", k=KT))\
                          .then_inc(small_loaded, 16)
                    sp.dma_start(wdt[:, :, :], d["m_in_2"][0][:, 5120:5152].rearrange("(k p) n -> p k n", p=P))\
                      .then_inc(small_loaded, 16)
                if n == 8:
                    sp.wait_ge(u_ready, 1)
                    sp.dma_start(bias_dram, u_sb[0:UNITS, :]).then_inc(u_stored, 16)
                if n == 10:
                    sp.wait_ge(u_stored, 16)
                    sp.dma_start(hank, bass.AP(bias_dram.tensor, 0, [[1, P], [384, UNITS], [1, 256]]))\
                      .then_inc(hank_loaded, 16)
                if n >= SHORT:
                    sp.wait_ge(used_a, n - SHORT + 1)
                sp.dma_start(cols(ring[:, a_slot(n), :], 4), units_a[n]).then_inc(full_a[a_slot(n)], 16)
            for j, (v, e) in enumerate(QUAD_UNITS):
                sp.wait_ge(used_a, UNITS_A - SHORT + j + 1 if j < SHORT else min(UNITS_A, UNITS_A - 4 + j - SHORT + 1))
                sp.dma_start(ring[:, e_slot(j), :], v[e]).then_inc(full_a[e_slot(j)], 16)
            sp.wait_ge(npass_ready, 1)
            npass = sp.value_load(counts_i[0:1, 0:1], min_val=1, max_val=S // SLOTS)
            first_free = sp.value_load(counts_i[0:1, 1:2], min_val=QUADS * RING - RING + 1,
                                       max_val=S // SLOTS * QUADS * RING)
            with sp.Fori(1, npass * QUADS) as q:
                for j, (v, e) in enumerate(QUAD_UNITS):
                    sp.wait_ge(used_e, q * RING + (j + 1 - RING))
                    src = v[bass.ds((q % QUADS) * QUAD + e, 1)].rearrange("e p n -> (e p) n")
                    sp.dma_start(ring[:, e_slot(j), :], src).then_inc(full_a[e_slot(j)], 16)
            for n in range(UNITS_B):
                if n < SHORT:
                    sp.wait_ge(used_e, first_free + n)
                else:
                    sp.wait_ge(used_b, n - SHORT + 1)
                dst = cols(ring[:, b_slot(n), :], 2 if n in (AT_PLE0 + 1, AT_PLE1 + 1) else 4)
                sp.dma_start(dst, units_b[n]).then_inc(full_b[n % SHORT], 16)
            sp.wait_ge(x_ready, 24)
            sp.dma_start(out[0].rearrange("(t p) n -> p t n", p=P), x[:, :, :]).then_inc(out_stored, 16)
            sp.wait_ge(out_stored, 16)

        @block.scalar
        def _(act):
            chain = [0]

            def link(ins):
                chain[0] += 1
                ins.then_inc(act_step, 1)
                act.wait_ge(act_step, chain[0])

            for name, n in (("norm1", "norm1_g"), ("m_norm", "m_norm_2"), ("s_norm", "s_norm_2"),
                            ("ynorm", "m_ynorm_2"), ("conv_b", "m_conv_b_2"), ("ple0", "ple_norm_2")):
                v = d[n].rearrange("o (k p) -> (o k) p", p=P)
                act.dma_start(rows_a[GAIN[name]:GAIN[name] + v.shape[0], :], v).then_inc(rows_loaded, 16)
            act.dma_start(rows_a[GAIN["kv"]:GAIN["kv"] + KT, :], d["kv_norm_2"].rearrange("(k p) -> k p", p=P))\
               .then_inc(rows_loaded, 16)
            act.dma_start(rows_c[0:96, :], d["m_conv_w_2"].rearrange("o j (k p) -> (o j k) p", p=P))\
               .then_inc(rows_loaded, 16)

            def squares(i, halves=(0, 1)):
                for half in halves:
                    for t in range(TT):
                        if i == 0:
                            act.wait_ge(x_loaded, 16 * TT)
                        else:
                            act.wait_ge(x_ready, 4 * i - 4 + 2 * half + t + 1)
                        at = (slice(None), t, slice(512 * half, 512 * half + 512))
                        act.activation(hn[at], x[at], ACT.Square, accum_out=ss[:, i, half, t:t + 1])\
                           .then_inc(ss_ready, 1)

            def hi(*hs, of=WeightsB):
                for h in hs:
                    act.wait_ge(*of.full(of.split[h]))
                    if h >= 4:
                        act.wait_ge(of.used, of.split[h - 4] + 1)
                    act.activation(w_hi(h), ring[:, of.slot(of.split[h]), :], ACT.Copy).then_inc(of.hi_ready, 1)

            def turned_hi(i, halves=(0, 1)):
                for n in range(2 * halves[0], 2 * halves[-1] + 2):
                    half, t = n // 2, n % 2
                    at = (slice(None), slice(4 * half, 4 * half + 4), slice(P * t, P * t + P))
                    act.wait_ge(turned, 4 * i + n + 1)
                    act.activation(hT_hi[at], hT[at], ACT.Copy).then_inc(hi_turned, 1)

            hi(0, of=WeightsA)
            squares(0)
            turned_hi(0)
            hi(1, of=WeightsA)
            act.wait_ge(lam_sum, 1)
            act.activation(lame[:, :], lame[:, :], ACT.Exp).then_inc(lam_exp, 1)
            hi(2, 3, of=WeightsA)
            def project(kinds, used, at, c_act, c_dve, t_ps, t_ready, sq, v, gate, turned_to, i, h0=0,
                        of=WeightsB):
                j = 0
                n_v = n_g = 0
                act.wait_ge(rs_ready, i + 1)
                pend = None

                def copy_turned(jj, dst, gain):
                    for t in range(TT):
                        act.wait_ge(t_ps, 2 * jj + t + 1)
                        src, to = cols(banks[4 + t][:, :], 4), dst[:, :, P * t:P * t + P]
                        if gain is None:
                            act.activation(to, src, ACT.Copy).then_inc(t_ready, 1)
                        else:
                            act.activation(to, src, ACT.Identity, scale=gain).then_inc(t_ready, 1)

                for c, kind in enumerate(kinds):
                    hi(h0 + 2 * c + 4, of=of)
                    act.wait_ge(used, at + 2 * c + 2)
                    for t in range(TT):
                        bank = banks[2 * (c % 2) + t]
                        if kind == "qk":
                            if j >= 1 and t == 0:
                                act.wait_ge(c_dve, 2 * j)
                            act.activation(sq[:, t, :], bank[:, :], ACT.Square, scale=rs[:, i, t:t + 1])\
                               .then_inc(c_act, 1)
                        elif kind == "v":
                            act.activation(v[:, t, 512 * n_v:512 * n_v + 512], bank[:, :], ACT.Identity,
                                           scale=rs[:, i, t:t + 1]).then_inc(c_act, 1)
                        else:
                            act.activation(gate[:, t, 512 * n_g:512 * n_g + 512], bank[:, :], ACT.Silu,
                                           scale=rs[:, i, t:t + 1])\
                               .then_inc(c_act, 1)
                    n_v += kind == "v"
                    n_g += kind == "gate"
                    hi(h0 + 2 * c + 5, of=of)
                    if pend is not None:
                        copy_turned(*pend)
                        pend = None
                    if kind == "qk":
                        pend = (j, *turned_to[j])
                        j += 1
                if pend is not None:
                    copy_turned(*pend)

            act.wait_ge(gains_ready, 3)
            project(["qk", "qk", "v", "qk", "qk", "v"], used_a, 0, proj_act, proj_dve, qkT_ps, qkT_ready,
                    sq_a, v_a, None, [(qT_a[:, 0:4, :], gq[:, 0:1]), (kT_a[:, 0:4, :], None),
                                      (qT_a[:, 4:8, :], gq[:, 1:2]), (kT_a[:, 4:8, :], None)], 0, of=WeightsA)

            def exps(u):
                for m in maps_of(u):
                    act.wait_ge(nmax_ready, m + 1)
                    if m >= 4:
                        act.wait_ge(wT_ps, unit_of(m - 4) + 1)
                    bank = banks[LOGIT_BANKS[m % 4]]
                    act.activation(probs[:, m % 4, 0:128], bank[:, 0:128], ACT.Exp, bias=nmax[:, m, 0:1],
                                   accum_out=psum_[:, m, 0:1])
                    act.activation(probs[:, m % 4, 128:384], bank[:, 128:384], ACT.Exp, bias=nmax[:, m, 1:2],
                                   accum_out=psum_[:, m, 1:2]).then_inc(probs_ready, 1)

            exps(0)
            for u in range(UNITS + 1):
                if u + 1 < UNITS:
                    exps(u + 1)
                if u < UNITS:
                    act.wait_ge(wT_ps, u + 1)
                    if u >= 2:
                        act.wait_ge(pv_ps, u - 1)
                    act.activation(wT[:, u % 2, :], banks[3 + u % 2][:, 0:384], ACT.Copy).then_inc(wT_ready, 1)
                if 1 <= u <= DIFF_HEADS:
                    act.wait_ge(pv_ps, u)
                    for t in range(TT):
                        ins = act.activation(sq_a[:, t, 128 * (u - 1):128 * u], banks[5 + (u - 1) % 2][:, 128 * t:128 * t + 128],
                                             ACT.Square, accum_out=ssd[:, u - 1, t:t + 1])
                    ins.then_inc(sqd_ready, 1)

            turned_hi(1)
            squares(1)
            act.wait_ge(gsub_ready, 1)
            act.activation(gex, gex, ACT.Exp).then_inc(gexp_ready, 1)
            act.wait_ge(edif_ready, 1)
            act.activation(m2, m2, ACT.Exp).then_inc(eexp_ready, 1)

            act.wait_ge(npass_ready, 1)
            npass = act.value_load(counts_i[0:1, 0:1], min_val=1, max_val=S // SLOTS)
            act.sem_inc(h_ready, 4)
            act.sem_inc(dn0_ready, 1)
            with act.Fori(0, npass) as r:
                for n in range(4):
                    act.wait_ge(selT_ps, r * 4 + (n + 1))
                    if n == 0:
                        act.wait_ge(selq_ready, r * QUADS + 1)
                    t, half = n // 2, n % 2
                    act.activation(selwT[:, 4 * half:4 * half + 4, P * t:P * t + P],
                                   cols(banks[6 + n % 2][:, :], 4), ACT.Copy).then_inc(selT_ready, 1)
                with act.Fori(0, QUADS) as g:
                    q = r * QUADS + g
                    for e in range(QUAD):
                        act.wait_ge(used_e, q * RING + (2 * e + 2))
                        act.wait_ge(fold_ps, q * QUAD + (e + 3))
                        act.activation(hpre[:, e % 2, :], banks[6 + e % 2][:, :], ACT.Copy).then_inc(h_ready, 1)
                        if e >= 1:
                            act.wait_ge(fold_ps, q * QUAD + (e + QUAD))
                            act.activation(sg[:, e - 1, :], banks[4 + (e - 1) % 2][:, 0:64], ACT.Silu)\
                               .then_inc(silu_ready, 1)
                    act.wait_ge(fold_ps, q * QUAD + 2 * QUAD)
                    act.activation(sg[:, 3, :], banks[5][:, 0:64], ACT.Silu).then_inc(silu_ready, 1)
                    act.wait_ge(dn0_ps, q + 1)
                    act.wait_ge(scatter_ps, q + 1)
                    act.activation(dn[:, 0:512], banks[6][:, :], ACT.Copy).then_inc(dn0_ready, 1)

            squares(2, (0,))
            hi(0)
            squares(2, (1,))
            hi(1)
            turned_hi(3)
            hi(2, 3)
            act.activation(negA, headp[:, 1, :], ACT.Exp).then_inc(a_ready, 1)
            act.wait_ge(dta_ready, 1)
            act.activation(dtu, dta, ACT.Exp, scale=-1.0).then_inc(dtu_ready, 1)
            act.wait_ge(dtw_ready, 1)
            act.activation(dtl, dtw, ACT.Ln).then_inc(dtl_ready, 1)

            def xc_silu(ci):
                act.wait_ge(conv_done, ci + 1)
                c = XBC_ORDER[ci]
                v = xc[:, 4 * c:4 * c + 4, :]
                act.activation(v, v, ACT.Silu).then_inc(xc_ready, 1)

            def z_silu(c):
                act.wait_ge(used_b, AT_Z + 2 * c + 2)
                for t in range(TT):
                    act.activation(z[:, t, 512 * c:512 * c + 512], banks[(6 if c else 0) + t][:, :], ACT.Silu)\
                       .then_inc(z_ready, 1)

            for ci, c in enumerate(XBC_ORDER):
                act.wait_ge(used_b, 2 * ci + 2)
                for k in range(4):
                    tile = 4 * c + k
                    ins = act.activation(xc[:, tile, :],
                                         banks[2 * (ci % 2) + k // 2][:, 256 * (k % 2):256 * (k % 2) + 256],
                                         ACT.Identity, bias=gcol[:, 64 + tile:65 + tile],
                                         scale=ccol[:, 24 * 3 + tile:24 * 3 + tile + 1])
                ins.then_inc(tap_ready, 1)
                hi(2 * ci + 4, 2 * ci + 5)
                if ci >= 1:
                    xc_silu(ci - 1)
            xc_silu(5)
            hi(16, 17)
            z_silu(0)
            act.wait_ge(acum_ready, 1)
            link(act.activation(toend, toend, ACT.Exp))
            act.activation(ea, acum[:, 1, :], ACT.Exp).then_inc(decay_ready, 1)
            act.wait_ge(bt_ps, 1)
            act.activation(btok, banks[4][:, :], ACT.Copy).then_inc(bt_ready, 1)
            for c in range(TT):
                act.wait_ge(cb_ps, c + 1)
                act.activation(cb[:, c, :], banks[6 + c][:, :], ACT.Copy).then_inc(cb_ready, 1)

            def mamba_tail(i):
                k = YZ_ORDER[i]
                c, g = k // 4, k % 4
                act.wait_ge(yz_ready, i + 1)
                if i >= 1:
                    act.wait_ge(ssy_ready, i)
                act.activation(btok, ym[:, c, 512 * g:512 * g + 512], ACT.Square,
                               accum_out=ssy[:, k:k + 1]).then_inc(ssy_ready, 1)

            def state_copy(k):
                act.wait_ge(intra_ps, k + 1)
                act.activation(state[:, 512 * k:512 * k + 512], banks[5][:, :], ACT.Copy).then_inc(state_ready, 1)

            for k in range(8):
                c, g = k // 4, k % 4
                act.wait_ge(xT_ps, k + 1)
                act.activation(ym[:, c, 512 * g:512 * g + 512], banks[k % 2][:, :], ACT.Copy)\
                   .then_inc(xt_ready, 1)
                for b in range(2):
                    act.wait_ge(seg_ready, 2 * k + b + 1)
                    v = seg[:, k % 2, 512 * b:512 * b + 512]
                    act.activation(v, v, ACT.Exp).then_inc(dec_ready, 1)
                if 1 <= k <= 4:
                    state_copy(k - 1)
                if k in (2, 4, 6):
                    z_silu(k // 2)
                if 1 <= k <= 6:
                    hi(17 + k)
                if k >= 4:
                    mamba_tail(k - 4)
            for i in range(4, 8):
                mamba_tail(i)
            act.wait_ge(yz_ready, 8)
            for j, k in enumerate(TAIL_ORDER):
                at = (slice(None), slice(4 * (k % 4), 4 * (k % 4) + 4), slice(P * (k // 4), P * (k // 4) + P))
                act.wait_ge(yT_ready, j + 1)
                act.activation(yT_hi[at], yT[at], ACT.Copy).then_inc(yT_hi_ready, 1)
            hi(*range(H_MOUT + 4, H_MOUT + 8))

            def embed(i):
                act.wait_ge(pT_ps, i + 1)
                act.activation(pT, cols(banks[6][:, :], 2), ACT.Copy).then_inc(pT_ready, 1)

            def sigmoids(i, at, c):
                act.wait_ge(rs_ready, 4 + 2 * i)
                act.wait_ge(used_b, at + 3 + 2 * c)
                for t in range(TT):
                    if c == 1:
                        act.wait_ge(x_ready, 12 + 8 * i + t + 1)
                    act.activation(sig[:, t, :], banks[2 * c + t][:, :], ACT.Sigmoid,
                                   scale=rs[:, 3 + 2 * i, t:t + 1]).then_inc(sig_ready, 1)

            embed(0)
            act.dma_start(pbuf[:, :, :], d["p_2"][1, 0].rearrange("(t p) n -> p t n", p=P)).then_inc(p_loaded, 16)
            squares(3, (0,))
            hi(H_PLE0)
            turned_hi(4, (0,))
            hi(H_PLE0 + 1, H_PLE0 + 2)
            squares(3, (1,))
            turned_hi(4, (1,))
            hi(H_PLE0 + 3, H_KV)
            sigmoids(0, AT_PLE0, 0)

            squares(4, (0,))
            hi(H_KV + 1)
            turned_hi(5, (0,))
            hi(H_KV + 2)
            sigmoids(0, AT_PLE0, 1)
            squares(4, (1,))
            turned_hi(5, (1,))
            hi(H_KV + 3)
            for n in range(4):
                half, t = n // 2, n % 2
                at = (slice(None), slice(4 * half, 4 * half + 4), slice(P * t, P * t + P))
                act.wait_ge(turned2, n + 1)
                act.activation(hT2_hi[at], hT2[at], ACT.Copy).then_inc(hi_turned2, 1)
            project(["qk", "qk", "v", "v", "qk", "qk", "gate", "gate"], used_b, AT_KV, projb_act, projb_dve,
                    qkTb_ps, qkTb_ready, sq_b, v_b, gate_b,
                    [(kT_b[:, 0:4, :], None), (kT_b[:, 4:8, :], None),
                     (qT_b[:, 0:4, :], gq[:, 2:3]), (qT_b[:, 4:8, :], gq[:, 2:3])], 4, H_KV)
            act.preload_act_table_set("natural_log_exp_and_others")

            def weights(h):
                act.wait_ge(wm_ready, h + 1)
                act.activation(wz[:, h % 2, :], wz[:, h % 2, :], ACT.Exp).then_inc(we_ready, 1)

            for h in range(SB_HEADS):
                act.wait_ge(zz_ps, h + 1)
                link(act.activation(absz[:, h % 2, :], banks[h % 4][:, 0:384], ACT.Abs))
                if h >= 2:
                    act.wait_ge(sp_ready, h - 1)
                link(act.activation(expz[:, h % 2, :], absz[:, h % 2, :], ACT.Exp, scale=-1.0))
                act.activation(lnz[:, h % 2, :], expz[:, h % 2, :], ACT.Ln, bias=1.0).then_inc(ln_ready, 1)
                if h >= 2:
                    weights(h - 2)
                if h == 14:
                    turned_hi(6, (0,))
            weights(SB_HEADS - 2)
            weights(SB_HEADS - 1)
            turned_hi(6, (1,))
            hi(H_PLE1)
            embed(1)
            squares(5, (0,))
            hi(H_PLE1 + 1)
            turned_hi(7, (0,))
            hi(H_PLE1 + 2)
            squares(5, (1,))
            turned_hi(7, (1,))
            hi(H_PLE1 + 3)
            sigmoids(1, AT_PLE1, 0)
            sigmoids(1, AT_PLE1, 1)

        @block.gpsimd
        def _(pool):
            def y_z(k):
                c, g = k // 4, k % 4
                y = ym[:, c, 512 * g:512 * g + 512]
                pool.wait_ge(ysum_ready, k + 1)
                pool.wait_ge(z_ready, 2 * g + 2)
                pool.tensor_tensor(y, y, z[:, c, 512 * g:512 * g + 512], ALU.mult).then_inc(yz_ready, 1)

            chain = [0]

            def link(ins):
                chain[0] += 1
                ins.then_inc(pool_step, 1)
                pool.wait_ge(pool_step, chain[0])

            def rsqrt(dst, src, eps, ready, step, done):
                pool.wait_ge(ready, step)
                link(pool.tensor_scalar(dst, src, eps, None, ALU.add))
                pool.tensor_tensor(dst, dst, C("neghalf")[:, 0:src.shape[1]], ALU.pow).then_inc(done, 1)

            def norm(i):
                pool.wait_ge(ss_ready, 4 * i + 4)
                link(pool.tensor_tensor(rs[:, i, :], ss[:, i, 0, :], ss[:, i, 1, :], ALU.add))
                link(pool.tensor_scalar(rs[:, i, :], rs[:, i, :], 1.0 / D, EPS, ALU.mult, ALU.add))
                pool.tensor_tensor(rs[:, i, :], rs[:, i, :], C("neghalf")[:, 0:TT], ALU.pow).then_inc(rs_ready, 1)
                pool.wait_ge(rs_ready, i + 1)

            def project(i, hs, hr, hsum, hroot):
                for j in range(4):
                    for t in range(TT):
                        v = hr[:, t, :]
                        pool.wait_ge(hsum, 2 * j + t + 1)
                        link(pool.tensor_scalar(v, hs[:, t, :], EPS * HD, None, ALU.add))
                        link(pool.tensor_tensor(v, v, C("neghalf"), ALU.pow))
                        pool.tensor_scalar(v, v, rs[:, i, t:t + 1], None, ALU.mult).then_inc(hroot, 1)

            pool.wait_ge(const_loaded, 16)
            norm(0)
            project(0, hss, hrs, hss_ready, hrs_ready)
            for u in range(DIFF_HEADS):
                rsqrt(rsd[:, u, :], ssd[:, u, :], EPS * 128, sqd_ready, u + 1, rsd_ready)
            norm(1)
            norm(2)
            for k in range(8):
                c, g = k // 4, k % 4
                y = ym[:, c, 512 * g:512 * g + 512]
                pool.wait_ge(xt_ready, k + 1)
                if k == 0:
                    pool.wait_ge(small_loaded, 16 * SMALL_LOADS)
                    pool.wait_ge(cb_ready, 2)
                    pool.wait_ge(decay_ready, 1)
                if c == 0:
                    pool.wait_ge(xdt_ready, k + 1)
                    if k >= 1:
                        pool.wait_ge(intra_ps, k)
                    pool.tensor_tensor(cols(xdte, 8), cols(xdt[:, k % 2, :], 8),
                                       over(toend[:, 8 * g:8 * g + 8], HD), ALU.mult).then_inc(xdte_ready, 1)
                for b in range(2):
                    pool.wait_ge(dec_ready, 2 * k + b + 1)
                    v = cols(seg[:, k % 2, 512 * b:512 * b + 512], 4)
                    pool.tensor_tensor(v, v, repeat(cb[:, c, P * g:P * g + P], 4), ALU.mult).then_inc(m_ready, 1)
                pool.tensor_tensor(cols(y, 8), cols(y, 8), over(headp[:, 2, 8 * g:8 * g + 8], HD), ALU.mult)\
                    .then_inc(xd_ready, 1)
                for j in {2: [0], 3: [1], 5: [2], 6: [4], 7: [3, 5]}.get(k, []):
                    y_z(j)
            for j in (6, 7):
                y_z(j)
            rsqrt(rsy[:, 0:4], ssy[:, 0:4], EPS * 512, ssy_ready, 5, rsy_ready)
            rsqrt(rsy[:, 4:8], ssy[:, 4:8], EPS * 512, ssy_ready, 8, rsy_ready)
            norm(3)
            norm(4)
            project(4, hss_b, hrs_b, hssb_ready, hrsb_ready)
            norm(5)

        @block.vector
        def _(dve):
            chain = [0]

            def link(ins):
                chain[0] += 1
                ins.then_inc(dve_step, 1)
                dve.wait_ge(dve_step, chain[0])

            dve.memset(tab[BUCKETS:BUCKETS + 1, :], 1.0).then_inc(ones_set, 1)
            for i, (dst, n) in enumerate(((gcol, 95), (ccol, 96))):
                dve.wait_ge(gains_ps, i + 1)
                dve.tensor_copy(dst[:, 0:n], banks[4 + i][:, 0:n]).then_inc(gains_ready, 1)

            def norm(i, permuted=False):
                for t in range(TT):
                    dve.wait_ge(rs_ready, i + 1)
                    src, dst = x[:, t, :], hn[:, t, :]
                    if permuted:
                        src, dst = src.rearrange("p (j k) -> p k j", k=KT), cols(dst, KT)
                    dve.tensor_scalar(dst, src, rs[:, i, t:t + 1], None, ALU.mult)\
                       .then_inc(hn_ready, 1)

            def lo(*hs, of=WeightsB):
                for h in hs:
                    slot = of.slot(of.split[h])
                    dve.wait_ge(of.hi_ready, h + 1)
                    dve.tensor_tensor(ring_r[:, slot, :], ring[:, slot, :], w_hi(h).bitcast(F32), ALU.subtract)\
                       .then_inc(of.lo_ready, 1)

            def part(n):
                return slice(None), slice(4 * (n // 2), 4 * (n // 2) + 4), slice(P * (n % 2), P * (n % 2) + P)

            def low(i, n):
                dve.wait_ge(hi_turned, 4 * SPLIT_TURNS.index(i) + n + 1)
                dve.tensor_tensor(hT_lo[part(n)], hT[part(n)], hT_hi[part(n)].bitcast(F32), ALU.subtract)\
                   .then_inc(lo_turned, 1)

            def turn(i, gain, second=None, split=False, bank0=6, halves=(0, 1)):
                for n in range(2 * halves[0], 2 * halves[-1] + 2):
                    half = n // 2
                    dve.wait_ge(turn_ps, 4 * i + n + 1)
                    src = cols(banks[bank0 + n % 2][:, :], 4)
                    dve.tensor_tensor(hT[part(n)], src, over(gain[:, 4 * half:4 * half + 4], P), ALU.mult)\
                       .then_inc(turned, 1)
                    if split and n % 2:
                        low(i, n - 1)
                        low(i, n)
                if second is not None:
                    for n in range(2 * halves[0], 2 * halves[-1] + 2):
                        half = n // 2
                        dve.tensor_tensor(hT2[part(n)], cols(banks[bank0 + n % 2][:, :], 4),
                                          over(second[:, 4 * half:4 * half + 4], P), ALU.mult).then_inc(turned2, 1)

            def G(name, n=KT):
                return gcol[:, GAIN[name]:GAIN[name] + n]

            dve.wait_ge(gains_ready, 2)
            lo(0, of=WeightsA)
            turn(0, G("norm1"), split=True)
            lo(1, of=WeightsA)
            for i, a in enumerate(("dq", "mq", "sq")):
                at = GAIN[a]
                link(dve.tensor_scalar(gq[:, i:i + 1], gcol[:, at:at + 1], gcol[:, at + 1:at + 2], 8.0,
                                       ALU.mult, ALU.mult))
            link(dve.memset(ga[:, :], 1.0))
            dve.tensor_scalar(ga[:, 0:4], G("sub", 1).to_broadcast([P, 4]), 1.0 - LAMBDA_INIT, None, ALU.mult)\
               .then_inc(gains_ready, 1)
            dve.wait_ge(gains_ready, 3)
            dve.wait_ge(lam_loaded, 16 * 4)
            for i in range(2):
                link(dve.tensor_tensor(lamv[:, 2 * i, :], lamv[:, 2 * i, :], lamv[:, 2 * i + 1, :], ALU.mult))
                ins = dve.tensor_reduce(lame[:, i:i + 1], lamv[:, 2 * i, :], AX.X, ALU.add)
                if i == 0:
                    link(ins)
            ins.then_inc(lam_sum, 1)
            dve.wait_ge(lam_exp, 1)
            link(dve.tensor_scalar(nlam[:, :], lame[:, 1:2], lame[:, 0:1], -LAMBDA_INIT, ALU.subtract, ALU.add))
            dve.wait_ge(u_ps, 1)
            dve.tensor_copy(u_sb[0:UNITS, :], banks[7][0:UNITS, 0:384]).then_inc(u_ready, 1)
            lo(2, 3, of=WeightsA)

            def project(kinds, c_act, c_dve, t_ps, sq, qk, hs, hr, hsum, hroot, h0=0, of=WeightsB):
                j = 0
                for c, kind in enumerate(kinds):
                    lo(*([h0 + 2 * c + 3] if c else []), h0 + 2 * c + 4, of=of)
                    if kind != "qk":
                        continue
                    if j >= 2:
                        dve.wait_ge(t_ps, 2 * (j - 1))
                    for t in range(TT):
                        dve.wait_ge(c_act, 2 * c + t + 1)
                        dve.tensor_reduce(hs[:, t, :], cols(sq[:, t, :], 8), AX.X, ALU.add).then_inc(hsum, 1)
                    for t in range(TT):
                        dve.wait_ge(hroot, 2 * j + t + 1)
                        dve.tensor_tensor(cols(qk[:, j % 2, t, :], 8), cols(banks[2 * (c % 2) + t][:, :], 8),
                                          over(hr[:, t, :], HD), ALU.mult).then_inc(c_dve, 1)
                    j += 1
                lo(h0 + 2 * len(kinds) + 3, of=of)

            project(["qk", "qk", "v", "qk", "qk", "v"], proj_act, proj_dve, qkT_ps,
                    sq_a, qk_a, hss, hrs, hss_ready, hrs_ready, of=WeightsA)

            def maxima(u):
                for m in maps_of(u):
                    dve.wait_ge(logits_ps, m + 1)
                    bank = banks[LOGIT_BANKS[m % 4]]
                    dve.tensor_reduce(nmax[:, m, 0:1], bank[:, 0:128], AX.X, ALU.max, negate=True)
                    dve.tensor_reduce(nmax[:, m, 1:2], bank[:, 128:384], AX.X, ALU.max, negate=True)\
                       .then_inc(nmax_ready, 1)

            def combine(u):
                ms = maps_of(u)
                dve.wait_ge(probs_ready, ms[-1] + 1)
                for m in ms[:-1]:
                    link(dve.reciprocal(prec[:, m, :], psum_[:, m, :]))
                last = dve.reciprocal(prec[:, ms[-1], :], psum_[:, ms[-1], :])
                if u >= DIFF_HEADS:
                    last.then_inc(w_ready, 1)
                    return
                link(last)
                a, b = ms
                link(dve.tensor_scalar(prec[:, b, :], prec[:, b, :], nlam[:, 0:1], None, ALU.mult))
                parts = ((0, 128), (128, 384))
                for t, (lo, hi) in enumerate(parts):
                    ins = dve.tensor_scalar(probs[:, b % 4, lo:hi], probs[:, b % 4, lo:hi],
                                            prec[:, b, t:t + 1], None, ALU.mult)
                link(ins)
                for t, (lo, hi) in enumerate(parts):
                    pa = probs[:, a % 4, lo:hi]
                    ins = dve.scalar_tensor_tensor(pa, pa, prec[:, a, t:t + 1], probs[:, b % 4, lo:hi],
                                                   ALU.mult, ALU.add)
                ins.then_inc(w_ready, 1)

            def outputs(u):
                bank = banks[5 + u % 2]
                if u < DIFF_HEADS:
                    dve.wait_ge(rsd_ready, u + 1)
                    for t in range(TT):
                        ins = dve.tensor_scalar(y_a[:, t, 128 * u:128 * u + 128], bank[:, 128 * t:128 * t + 128],
                                                rsd[:, u, t:t + 1], math.sqrt(128.0), ALU.mult, ALU.mult)
                else:
                    dve.wait_ge(pv_ps, u + 1)
                    dve.wait_ge(w_ready, u + 1)
                    h, m = u - DIFF_HEADS, u + DIFF_HEADS
                    for t in range(TT):
                        ins = dve.tensor_scalar(y_a[:, t, 512 + HD * h:512 + HD * h + HD],
                                                bank[:, 128 * t:128 * t + HD], prec[:, m, t:t + 1], None, ALU.mult)
                ins.then_inc(y_ready, 1)

            maxima(0)
            for u in range(UNITS + 2):
                if u + 1 < UNITS:
                    maxima(u + 1)
                if u < UNITS:
                    combine(u)
                if u >= 2:
                    outputs(u - 2)
            turn(1, ga, split=True, bank0=3)

            def add_product(c, bank0, used, at):
                dve.wait_ge(used, at)
                for t in range(TT):
                    xv = x[:, t, 512 * c:512 * c + 512]
                    dve.tensor_tensor(xv, banks[bank0 + t][:, :], xv, ALU.add).then_inc(x_ready, 1)

            for c in range(2):
                add_product(c, 2 * c, used_a, 12 + 2 * c + 2)
            dve.wait_ge(x_ready, 4)
            norm(1, permuted=True)
            turn(2, g2)

            dve.wait_ge(router_ps, 1)
            link(dve.tensor_copy(rl, cols(banks[4][:, 0:72], 2)))
            iota32 = C("iota")
            gl = rl[:, :, 0:GROUPS]
            link(dve.tensor_reduce(gmx, gl, AX.X, ALU.max))
            link(dve.tensor_tensor(geq, gl, over(gmx, 4), ALU.is_equal))
            dve.tensor_tensor(gex, gl, over(gmx, 4), ALU.subtract).then_inc(gsub_ready, 1)
            link(dve.tensor_tensor(gc, geq, repeat(C("iota_low")[:, 0:4], TT), ALU.mult))
            link(dve.tensor_reduce(gidx, gc, AX.X, ALU.min))
            link(dve.tensor_tensor(geq, repeat(C("iota_low")[:, 0:4], TT), over(gidx, 4), ALU.is_equal))
            link(dve.tensor_scalar(gc, geq, -NEG, NEG, ALU.mult, ALU.add))
            for t in range(TT):
                ins = dve.tensor_tensor(cols(el[:, t, :], GROUPS), cols(rl[:, t, GROUPS:36], GROUPS),
                                        over(gc[:, t, :], PER_GROUP), ALU.add)
            link(ins)

            def pick(vals, mx, oh):
                link(dve.tensor_reduce(mx, vals, AX.X, ALU.max))
                link(dve.tensor_tensor(eq, vals, over(mx, EXPERTS), ALU.is_equal))
                link(dve.tensor_tensor(cand, eq, repeat(C("iota_low"), TT), ALU.mult))
                link(dve.tensor_reduce(i1, cand, AX.X, ALU.min))
                link(dve.tensor_tensor(oh, repeat(C("iota_low"), TT), over(i1, EXPERTS), ALU.is_equal))

            pick(el, m1, oh1)
            link(dve.scalar_tensor_tensor(el2, oh1, 2 * NEG, el, ALU.mult, ALU.add))
            pick(el2, m2, oh2)
            dve.tensor_tensor(m2, m2, m1, ALU.subtract).then_inc(edif_ready, 1)
            dve.wait_ge(edif_ready, 1)
            dve.tensor_tensor(msel, oh1, oh2, ALU.add).then_inc(msel_ready, 1)
            dve.wait_ge(gexp_ready, 1)
            link(dve.tensor_reduce(gsum, gex, AX.X, ALU.add))
            dve.wait_ge(eexp_ready, 1)
            link(dve.tensor_scalar(w1, m2, 1.0, None, ALU.add))
            link(dve.tensor_tensor(w1, w1, gsum, ALU.mult))
            link(dve.reciprocal(w1, w1))
            link(dve.tensor_tensor(w2, w1, m2, ALU.mult))
            link(dve.tensor_tensor(oh1, oh1, over(w1, EXPERTS), ALU.mult))
            link(dve.tensor_tensor(oh2, oh2, over(w2, EXPERTS), ALU.mult))
            link(dve.tensor_tensor(wsel, oh1, oh2, ALU.add))
            dve.wait_ge(rank_ps, 1)
            link(dve.scalar_tensor_tensor(rk, cols(banks[5][:, 0:64], 2), 1.0, msel, ALU.add, ALU.mult))
            link(dve.tensor_scalar(rk, rk, -1.0, None, ALU.add))
            link(dve.tensor_reduce(cmax, banks[5][:, 64:96], AX.X, ALU.max))
            link(dve.tensor_scalar(cpass, C("passes"), cmax[:, 0:1], None, ALU.is_lt))
            link(dve.tensor_reduce(cmax, cpass, AX.X, ALU.add))
            link(dve.tensor_scalar(cpass[:, 0:1], cmax, float(QUADS * RING), 1.0 - RING, ALU.mult, ALU.add))
            dve.tensor_copy(counts_i[:, 0:1], cmax)
            dve.tensor_copy(counts_i[:, 1:2], cpass[:, 0:1]).then_inc(npass_ready, 1)
            dve.wait_ge(npass_ready, 1)
            npass = dve.value_load(counts_i[0:1, 0:1], min_val=1, max_val=S // SLOTS)

            dve.sem_inc(xg_ready, 2)
            dve.sem_inc(hid_ready, 4)
            dve.sem_inc(dn1_ready, 1)
            dve.sem_inc(selq_ready, 1)
            with dve.Fori(0, npass) as r:
                dve.wait_ge(scatter_ps, r * QUADS + 1)
                for t in range(TT):
                    ins = dve.tensor_tensor(cols(sel[:, t, :], EXPERTS), repeat(iota32, EXPERTS),
                                            over(rk[:, t, :], SLOTS), ALU.is_equal)
                ins.then_inc(pass_step, 1)
                dve.wait_ge(pass_step, r * 2 + 1)
                dve.tensor_scalar(rk, rk, -float(SLOTS), None, ALU.add).then_inc(pass_step, 1)
                dve.wait_ge(pass_step, r * 2 + 2)
                for t in range(TT):
                    dve.tensor_tensor(cols(selw[:, t, :], EXPERTS), cols(sel[:, t, :], EXPERTS),
                                      over(wsel[:, t, :], SLOTS), ALU.mult).then_inc(sel_ready, 1)
                with dve.Fori(0, QUADS) as g:
                    q = r * QUADS + g
                    for b in range(2):
                        dve.wait_ge(gather_ps, q * 2 + (b + 1))
                        dve.tensor_tensor(xg[:, 4 * b:4 * b + 4, :], cols(banks[4 + b][:, :], 4),
                                          over(g2[:, 4 * b:4 * b + 4], P), ALU.mult).then_inc(xg_ready, 1)
                    dve.wait_ge(selT_ready, r * 4 + 4)
                    dve.wait_ge(scatter_ps, q + 1)
                    dve.tensor_copy(selwT_q, selwT[:, bass.ds(g, 1), :].rearrange("p a b -> p (a b)"))\
                       .then_inc(selq_ready, 1)
                    for e in range(QUAD):
                        dve.wait_ge(silu_ready, q * QUAD + (e + 1))
                        dve.tensor_tensor(hid[:, e, :], banks[4 + e % 2][:, 64:128], sg[:, e, :], ALU.mult)\
                           .then_inc(hid_ready, 1)
                    dve.wait_ge(used_e, q * RING + RING)
                    dve.tensor_copy(dn[:, 512:1024], banks[7][:, :]).then_inc(dn1_ready, 1)
            dve.wait_ge(scatter_ps, npass * QUADS + 1)
            for half in range(2):
                for t in range(TT):
                    dve.tensor_copy(x[:, t, 512 * half:512 * half + 512], banks[2 * t + half][:, :])\
                       .then_inc(x_ready, 1)
            dve.wait_ge(x_ready, 8)

            def turned_y(j):
                c, g = TAIL_ORDER[j] // 4, TAIL_ORDER[j] % 4
                dve.wait_ge(yT_ps, j + 1)
                dve.tensor_tensor(yT[:, 4 * g:4 * g + 4, P * c:P * c + P], cols(banks[6 + j % 2][:, :], 4),
                                  over(gcol[:, 48 + 4 * g:52 + 4 * g], P), ALU.mult).then_inc(yT_ready, 1)

            def low_y(j):
                c, g = TAIL_ORDER[j] // 4, TAIL_ORDER[j] % 4
                at = (slice(None), slice(4 * g, 4 * g + 4), slice(P * c, P * c + P))
                dve.wait_ge(yT_hi_ready, j + 1)
                dve.tensor_tensor(yT_lo[at], yT[at], yT_hi[at].bitcast(F32), ALU.subtract).then_inc(yT_lo_ready, 1)

            norm(2)
            lo(0)
            turn(3, G("m_norm"), split=True)
            lo(1, 2, 3)
            dve.wait_ge(dt_ps, 1)
            link(dve.tensor_tensor(dtb, cols(banks[4][:, 0:64], 2), repeat(headp[:, 0, :], TT), ALU.add))
            dve.scalar_tensor_tensor(dta, dtb, -1.0, dtb, ALU.mult, ALU.max).then_inc(dta_ready, 1)
            dve.wait_ge(dtu_ready, 1)
            dve.tensor_scalar(dtw, dtu, 1.0, None, ALU.add).then_inc(dtw_ready, 1)
            dve.wait_ge(dtw_ready, 1)
            link(dve.tensor_scalar(dtv, dtw, -1.0, None, ALU.add))
            link(dve.tensor_scalar(dtq, dtv, 0.0, None, ALU.is_equal))
            link(dve.tensor_tensor(dtv, dtv, dtq, ALU.add))
            link(dve.reciprocal(dtv, dtv))
            link(dve.tensor_tensor(dtv, dtv, dtu, ALU.mult))
            link(dve.tensor_tensor(dtq, dtq, dtu, ALU.mult))
            dve.wait_ge(dtl_ready, 1)
            link(dve.tensor_tensor(dtv, dtv, dtl, ALU.mult))
            link(dve.tensor_tensor(dtv, dtv, dtq, ALU.add))
            link(dve.scalar_tensor_tensor(dtb, dtb, 0.0, dtv, ALU.max, ALU.add))
            dve.wait_ge(a_ready, 1)
            dve.scalar_tensor_tensor(dtA, dtb, -1.0, repeat(negA, TT), ALU.mult, ALU.mult).then_inc(dtA_ready, 1)

            def conv(ci):
                dve.wait_ge(tap_ready, ci + 1)
                c = XBC_ORDER[ci]
                for tap in range(CONV_K - 2, -1, -1):
                    lag = CONV_K - 1 - tap
                    for k in range(4):
                        tile = 4 * c + k
                        src = banks[2 * (ci % 2) + k // 2][:, 256 * (k % 2):256 * (k % 2) + 256 - lag]
                        w = ccol[:, 24 * tap + tile:24 * tap + tile + 1]
                        v = xc[:, tile, lag:]
                        ins = dve.scalar_tensor_tensor(v, src, w, v, ALU.mult, ALU.add)
                    if tap:
                        link(ins)
                ins.then_inc(conv_done, 1)
                lo(2 * ci + 4, 2 * ci + 5)

            conv(0)
            conv(1)
            dve.wait_ge(cum_ps, 1)
            link(dve.tensor_copy(acum, cols(banks[5][:, 0:64], 2)))
            dve.tensor_tensor(toend, banks[5][:, 64:96], acum[:, 0, :], ALU.subtract).then_inc(acum_ready, 1)
            for ci in range(2, 6):
                conv(ci)
            lo(16)

            def y_out(k):
                c, g = k // 4, k % 4
                y = ym[:, c, 512 * g:512 * g + 512]
                dve.wait_ge(intra_ps, k + 1)
                dve.wait_ge(xd_ready, k + 1)
                if c == 0:
                    dve.tensor_tensor(y, banks[4][:, :], y, ALU.add).then_inc(ysum_ready, 1)
                    return
                link(dve.tensor_tensor(y, banks[4][:, :], y, ALU.add))
                link(dve.tensor_tensor(cols(xdte, 8), cols(banks[5][:, :], 8),
                                       over(ea[:, 8 * g:8 * g + 8], HD), ALU.mult))
                dve.tensor_tensor(y, y, xdte, ALU.add).then_inc(ysum_ready, 1)

            for k in range(8):
                c, g = k // 4, k % 4
                dve.wait_ge(xT_ps, k + 1)
                dve.wait_ge(xt_ready, k + 1)
                if k >= 2:
                    dve.wait_ge(intra_ps, k - 1)
                    if c == 0 or k - 2 < 4:
                        dve.wait_ge(xdte_ready, min(k - 1, 4))
                dve.tensor_tensor(cols(xdt[:, k % 2, :], 8), cols(banks[k % 2][:, :], 8),
                                  over(dtb[:, c, 8 * g:8 * g + 8], HD), ALU.mult).then_inc(xdt_ready, 1)
                for b in range(2):
                    dve.wait_ge(rows_ps, 2 * k + b + 1)
                    for i in range(4):
                        h = 8 * g + 4 * b + i
                        ins = dve.scalar_tensor_tensor(
                            seg[:, k % 2, 512 * b + P * i:512 * b + P * i + P], banks[2 + b][:, P * i:P * i + P],
                            acum[:, c, h:h + 1], C("segmask"), ALU.subtract, ALU.add)
                    ins.then_inc(seg_ready, 1)
                if k >= 1:
                    y_out(k - 1)
                    lo(16 + k)
            y_out(7)
            for j, k in enumerate(TAIL_ORDER):
                c, g = k // 4, k % 4
                y = ym[:, c, 512 * g:512 * g + 512]
                dve.wait_ge(rsy_ready, 2 if c else 1)
                dve.tensor_scalar(y, y, rsy[:, k:k + 1], math.sqrt(512.0), ALU.mult, ALU.mult).then_inc(yn_ready, 1)
                if j >= 1:
                    turned_y(j - 1)
                if j >= 2:
                    low_y(j - 2)
            turned_y(7)
            low_y(6)
            low_y(7)
            lo(*range(H_MOUT + 4, H_MOUT + 7))
            add_product(0, 0, used_b, AT_MOUT + 4)
            lo(H_MOUT + 7, H_PLE0)

            def gated(i, c):
                for t in range(TT):
                    dve.wait_ge(sig_ready, 4 * i + 2 * c + t + 1)
                    link(dve.tensor_tensor(pret[:, t, :], banks[4 + 2 * c + t][:, :], sig[:, t, :], ALU.mult))
                    xv = x[:, t, 512 * c:512 * c + 512]
                    dve.tensor_tensor(xv, xv, pret[:, t, :], ALU.add).then_inc(x_ready, 1)

            turn(4, G("ple0"), split=True, halves=(0,))
            lo(H_PLE0 + 1, H_PLE0 + 2)
            add_product(1, 2, used_b, AT_MOUT + 8)
            turn(4, G("ple0"), split=True, halves=(1,))
            lo(H_PLE0 + 3, H_KV)
            gated(0, 0)

            lo(H_KV + 1)
            turn(5, G("kv"), second=G("s_norm"), split=True, bank0=4, halves=(0,))
            lo(H_KV + 2)
            gated(0, 1)
            turn(5, G("kv"), second=G("s_norm"), split=True, bank0=4, halves=(1,))
            lo(H_KV + 3)
            for n in range(4):
                half, t = n // 2, n % 2
                at = (slice(None), slice(4 * half, 4 * half + 4), slice(P * t, P * t + P))
                dve.wait_ge(hi_turned2, n + 1)
                dve.tensor_tensor(hT2_lo[at], hT2[at], hT2_hi[at].bitcast(F32), ALU.subtract).then_inc(lo_turned2, 1)
            project(["qk", "qk", "v", "v", "qk", "qk", "gate", "gate"], projb_act, projb_dve,
                    qkTb_ps, sq_b, qk_b, hss_b, hrs_b, hssb_ready, hrsb_ready, H_KV)

            def softplus(h):
                dve.wait_ge(ln_ready, h + 1)
                if h >= 2:
                    dve.wait_ge(suf_ps, h - 1)
                link(dve.scalar_tensor_tensor(spz[:, h % 2, :], banks[h % 4][:, 0:384], 0.0, lnz[:, h % 2, :],
                                              ALU.max, ALU.add))
                v = spz[:, h % 2, :].rearrange("p (a b) -> p a b", a=3)[:, 0:3:2, :]
                dve.tensor_tensor(v, v, repeat(C("tri_lt"), 2), ALU.mult).then_inc(sp_ready, 1)

            def mask(h):
                dve.wait_ge(suf_ps, h + 1)
                if h >= 2:
                    dve.wait_ge(ob_ps, h - 1)
                dve.tensor_tensor(wz[:, h % 2, :], banks[h % 4][:, 0:384], mask3, ALU.add).then_inc(wm_ready, 1)

            def take(h):
                dve.wait_ge(ob_ps, h + 1)
                dve.wait_ge(projb_act, 16)
                for t in range(TT):
                    ins = dve.tensor_tensor(o_b[:, t, HD * h:HD * h + HD], banks[4 + h % 2][:, HD * t:HD * t + HD],
                                            gate_b[:, t, HD * h:HD * h + HD], ALU.mult)
                ins.then_inc(o_ready, 1)

            link(dve.memset(ga[:, 0:4], 1.0))
            link(dve.memset(mask3, 0.0))
            for at in (0, 256):
                link(dve.tensor_copy(mask3[:, at:at + P], C("strictmask")))
            for h in range(SB_HEADS):
                softplus(h)
                if h >= 1:
                    mask(h - 1)
                if h >= 3:
                    take(h - 3)
                if h == 13:
                    turn(6, ga, split=False, halves=(0,))
                if h == 15:
                    low(6, 0)
                    low(6, 1)
            mask(SB_HEADS - 1)
            take(SB_HEADS - 3)
            take(SB_HEADS - 2)
            take(SB_HEADS - 1)
            turn(6, ga, split=True, halves=(1,))
            lo(H_PLE1)
            add_product(0, 0, used_b, AT_SOUT + 2)
            lo(H_PLE1 + 1)
            turn(7, G("ple1"), split=True, halves=(0,))
            lo(H_PLE1 + 2)
            add_product(1, 2, used_b, AT_SOUT + 4)
            turn(7, G("ple1"), split=True, halves=(1,))
            lo(H_PLE1 + 3)
            gated(1, 0)
            gated(1, 1)

        @block.tensor
        def _(pe):
            ident = C("ident")

            def turn(i, wait, src=hn, bank0=6, halves=(0, 1)):
                for n in range(2 * halves[0], 2 * halves[-1] + 2):
                    half, t = n // 2, n % 2
                    pe.wait_ge(*wait(n))
                    if n >= 2 or i >= 1:
                        pe.wait_ge(turned, 4 * i + n - 1)
                    if i == 5 and n >= 2:
                        pe.wait_ge(turned2, n - 1)
                    for k in range(4):
                        kt = 4 * half + k
                        ins = pe.transpose(banks[bank0 + n % 2][:, P * k:P * k + P],
                                           src[:, t, P * kt:P * kt + P], ident)
                    ins.then_inc(turn_ps, 1)

            def product(hi, low, bank0, u0, n_units, ready=None, n_kt=None, kt0=0, of=WeightsB,
                        middle=None):
                n_kt = n_kt or 4 * n_units
                for i in range(n_units):
                    h = of.split.index(u0 + i)
                    pe.wait_ge(of.lo_ready, h + 1)
                    if ready is not None:
                        pe.wait_ge(ready[0], ready[1] + 2 * i + 2)
                    wh, wl = cols(w_hi(h), 4), cols(ring_r[:, of.slot(u0 + i), :], 4)
                    for t in range(TT):
                        if t == 1 and middle is not None:
                            middle()
                        for k in range(4):
                            kt = kt0 + 4 * i + k
                            a, b = hi[:, kt, P * t:P * t + P], low[:, kt, P * t:P * t + P]
                            pe.matmul(banks[bank0 + t][:, :], a, wh[:, k, :], start=kt == 0, stop=False)
                            pe.matmul(banks[bank0 + t][:, :], a, wl[:, k, :], start=False, stop=False)
                            ins = pe.matmul(banks[bank0 + t][:, :], b, wh[:, k, :], start=False,
                                            stop=kt == n_kt - 1)
                    ins.then_inc(of.used, 1)

            pe.wait_ge(const_loaded, 16)
            pe.wait_ge(rows_loaded, 16 * ROW_LOADS)
            pe.transpose(banks[4][:, 0:95], rows_a[0:95, :], ident[0:95, 0:95]).then_inc(gains_ps, 1)
            pe.transpose(banks[5][:, 0:96], rows_c[0:96, :], ident[0:96, 0:96]).then_inc(gains_ps, 1)
            turn(0, lambda n: (x_loaded, 16 * TT), src=x, halves=(0,))

            def bias_rows():
                pe.wait_ge(tab_loaded, 32)
                pe.wait_ge(ones_set, 1)
                pe.wait_ge(turned, 4)
                pe.matmul(banks[7][0:UNITS, 0:384], tab[0:BUCKETS + 1, :], onehot[0:BUCKETS + 1, :],
                          start=True, stop=True).then_inc(u_ps, 1)


            def project(kinds, multiply, c_act, c_dve, t_ps, t_ready, qk):
                j = 0
                pend = None
                n_qk = [sum(k == "qk" for k in kinds[:c + 1]) for c in range(len(kinds))]

                def turn_qk(jj):
                    for t in range(TT):
                        pe.wait_ge(c_dve, 2 * jj + t + 1)
                        if jj >= 1:
                            pe.wait_ge(t_ready, 2 * (jj - 1) + t + 1)
                        for p in range(4):
                            ins = pe.transpose(banks[4 + t][:, P * p:P * p + P], qk[:, jj % 2, t, P * p:P * p + P],
                                               ident)
                        ins.then_inc(t_ps, 1)

                for c, kind in enumerate(kinds):
                    if c >= 2:
                        pe.wait_ge(c_act, 2 * (c - 1))
                        if n_qk[c - 2]:
                            pe.wait_ge(c_dve, 2 * n_qk[c - 2])
                    multiply(c, 2 * (c % 2))
                    if pend is not None:
                        turn_qk(pend)
                        pend = None
                    if kind == "qk":
                        pend = j
                        j += 1
                if pend is not None:
                    turn_qk(pend)

            def multiply_a(c, bank0):
                if c == 0:
                    product(hT_hi, hT_lo, bank0, 0, 1, ready=(lo_turned, 0), n_kt=KT, of=WeightsA,
                            middle=lambda: turn(0, lambda n: (x_loaded, 16 * TT), src=x, halves=(1,)))
                    product(hT_hi, hT_lo, bank0, 1, 1, ready=(lo_turned, 2), n_kt=KT, kt0=4, of=WeightsA,
                            middle=bias_rows)
                else:
                    product(hT_hi, hT_lo, bank0, 2 * c, 2, of=WeightsA)

            project(["qk", "qk", "v", "qk", "qk", "v"], multiply_a,
                    proj_act, proj_dve, qkT_ps, qkT_ready, qk_a)

            pe.wait_ge(hank_loaded, 16)
            pe.wait_ge(proj_act, 12)
            pe.wait_ge(proj_dve, 8)
            pe.wait_ge(qkT_ready, 8)

            def logits(u):
                for m in maps_of(u):
                    if m >= 4:
                        pe.wait_ge(probs_ready, m - 3)
                    r0, pair, bank = HD * (m % 2), m // 2, banks[LOGIT_BANKS[m % 4]]
                    for t, lo, hi in ((0, 0, 128), (1, 128, 384)):
                        n = hi - lo
                        pe.matmul(bank[:, lo:hi], qT_a[r0:r0 + HD, pair, P * t:P * t + P],
                                  kT_a[r0:r0 + HD, pair, 0:n], start=True, stop=False)
                        ins = pe.matmul(bank[:, lo:hi], C("flip"), hank[:, u, 256 - n:256], start=False, stop=True)
                    ins.then_inc(logits_ps, 1)

            logits(0)
            logits(1)
            for u in range(UNITS + 1):
                if u < UNITS:
                    pe.wait_ge(w_ready, u + 1)
                    pe.wait_ge(probs_ready, maps_of(u)[0] + 1)
                    if u >= 2:
                        pe.wait_ge(wT_ready, u - 1)
                    m, bank = maps_of(u)[0], banks[3 + u % 2]
                    for i in range(3):
                        ins = pe.transpose(bank[:, P * i:P * i + P], probs[:, m % 4, P * i:P * i + P], ident)
                    ins.then_inc(wT_ps, 1)
                if u + 2 < UNITS:
                    logits(u + 2)
                if u >= 1:
                    v = u - 1
                    pe.wait_ge(wT_ready, v + 1)
                    if v >= 2:
                        pe.wait_ge(y_ready, v - 1)
                    bank, w = banks[5 + v % 2], wT[:, v % 2, :]
                    at, n = (128 * v, 128) if v < DIFF_HEADS else (512 + HD * (v - DIFF_HEADS), HD)
                    pe.matmul(bank[:, 0:n], w[:, 0:128], v_a[:, 0, at:at + n], start=True, stop=True)
                    pe.matmul(bank[:, 128:128 + n], w[:, 128:256], v_a[:, 0, at:at + n], start=True, stop=False)
                    pe.matmul(bank[:, 128:128 + n], w[:, 256:384], v_a[:, 1, at:at + n], start=False, stop=True)\
                      .then_inc(pv_ps, 1)
            turn(1, lambda n: (y_ready, DIFF_HEADS), bank0=3, halves=(0,))
            product(hT_hi, hT_lo, 0, 12, 1, ready=(lo_turned, 4), n_kt=KT, of=WeightsA,
                    middle=lambda: turn(1, lambda n: (y_ready, UNITS), bank0=3, halves=(1,)))
            product(hT_hi, hT_lo, 0, 13, 1, ready=(lo_turned, 6), n_kt=KT, kt0=4, of=WeightsA)
            product(hT_hi, hT_lo, 2, 14, 2, of=WeightsA)

            pe.wait_ge(x_ready, 4)
            for t in range(TT):
                for half in range(2):
                    pe.matmul(banks[2 * t + half][:, :], ident, x[:, t, 512 * half:512 * half + 512],
                              start=True, stop=True)
            turn(2, lambda n: (hn_ready, n % 2 + 1))
            pe.wait_ge(turned, 12)
            pe.wait_ge(small_loaded, 16 * SMALL_LOADS)
            for t in range(TT):
                for kt in range(KT):
                    ins = pe.matmul(banks[4][:, 36 * t:36 * t + 36], hT[:, kt, P * t:P * t + P], wr[:, kt, :],
                                    start=kt == 0, stop=kt == KT - 1)
            ins.then_inc(router_ps, 1)
            pe.wait_ge(msel_ready, 1)
            b = banks[5]
            pe.matmul(b[:, 0:32], C("tri_lt"), msel[:, 0, :], start=True, stop=True)
            pe.matmul(b[:, 32:64], C("ones"), msel[:, 0, :], start=True, stop=False)
            pe.matmul(b[:, 32:64], C("tri_lt"), msel[:, 1, :], start=False, stop=True)
            pe.matmul(b[:, 64:96], C("ones"), msel[:, 0, :], start=True, stop=False)
            pe.matmul(b[:, 64:96], C("ones"), msel[:, 1, :], start=False, stop=True).then_inc(rank_ps, 1)

            pe.wait_ge(npass_ready, 1)
            npass = pe.value_load(counts_i[0:1, 0:1], min_val=1, max_val=S // SLOTS)
            pe.sem_inc(fold_ps, 4)
            pe.sem_inc(scatter_ps, 1)
            with pe.Fori(0, npass) as r:
                for n in range(4):
                    t, half = n // 2, n % 2
                    if n < 2:
                        pe.wait_ge(sel_ready, r * 2 + (2 if n else 1))
                    if n == 0:
                        pe.wait_ge(sel_ready, r * 2 + 2)
                    if n >= 2:
                        pe.wait_ge(selT_ready, r * 4 + (n - 1))
                    for k in range(4):
                        qd = 4 * half + k
                        ins = pe.transpose(banks[6 + n % 2][:, P * k:P * k + P], selw[:, t, P * qd:P * qd + P], ident)
                    ins.then_inc(selT_ps, 1)
                with pe.Fori(0, QUADS) as g:
                    q = r * QUADS + g
                    pe.wait_ge(hid_ready, q * QUAD + 4)
                    for b in range(2):
                        for k in range(4):
                            kt = 4 * b + k
                            for t in range(TT):
                                ins = pe.matmul(banks[4 + b][:, P * k:P * k + P], hn[:, t, P * kt:P * kt + P],
                                                sel[:, t, bass.ds(g * P, P)], start=t == 0, stop=t == 1)
                        ins.then_inc(gather_ps, 1)
                    pe.wait_ge(xg_ready, q * 2 + 4)
                    pe.wait_ge(selT_ready, r * 4 + 4)
                    pe.wait_ge(dn0_ready, q + 1)
                    pe.wait_ge(dn1_ready, q + 1)

                    def fold(e):
                        pe.wait_ge(h_ready, q * QUAD + (e + 5))
                        if e >= 2:
                            pe.wait_ge(hid_ready, q * QUAD + (e + 3))
                        for i in range(4):
                            at = 256 * (i // 2) + i % 2
                            ins = pe.matmul(banks[4 + e % 2][:, SLOTS * i:SLOTS * i + SLOTS],
                                            hpre[:, e % 2, at:256 * (i // 2) + 256:2], C("fold"),
                                            start=True, stop=True)
                        ins.then_inc(fold_ps, 1)

                    for e in range(QUAD):
                        if e >= 2:
                            pe.wait_ge(h_ready, q * QUAD + (e + 3))
                        for i in range(2):
                            slot = e_slot(2 * e + i)
                            pe.wait_ge(full_a[slot], q * 16 + e_full(slot))
                            w = cols(ring[:, slot, :], KT)
                            for kt in range(KT):
                                c0 = SLOTS * (kt % 4)
                                ins = pe.matmul(banks[6 + e % 2][c0:c0 + SLOTS, 256 * i:256 * i + 256],
                                                xg[:, kt, SLOTS * e:SLOTS * e + SLOTS], w[:, kt, :],
                                                start=kt < 4, stop=kt >= 4)
                            ins.then_inc(used_e, 1)
                        if e >= 1:
                            fold(e - 1)
                    fold(3)
                    for e in range(QUAD):
                        pe.wait_ge(full_a[e_slot(8 + e)], q * 16 + e_full(e_slot(8 + e)))
                    pe.wait_ge(hid_ready, q * QUAD + 8)
                    for half in range(2):
                        for f in range(2):
                            for e in range(QUAD):
                                w = cols(ring[:, e_slot(8 + e), :], 2)
                                ins = pe.matmul(banks[6 + half][SLOTS * e:SLOTS * e + SLOTS, :],
                                                hid[:, e, SLOTS * f:SLOTS * f + SLOTS],
                                                w[:, f, 512 * half:512 * half + 512],
                                                start=f == 0, stop=f == 1)
                                if half == 1 and f == 1:
                                    ins.then_inc(used_e, 1)
                                elif half == 0 and f == 1 and e == 3:
                                    ins.then_inc(dn0_ps, 1)
                    pe.wait_ge(selq_ready, q + 2)
                    for half in range(2):
                        pe.wait_ge((dn0_ready, dn1_ready)[half], q + 2)
                        for t in range(TT):
                            ins = pe.matmul(banks[2 * t + half][:, :], selwT_q[:, P * t:P * t + P],
                                            dn[:, 512 * half:512 * half + 512], start=False, stop=False,
                                            skip_group_check=True)
                    ins.then_inc(scatter_ps, 1)

            turn(3, lambda n: (hn_ready, n % 2 + 3))
            pe.wait_ge(lo_turned, 12)
            for t in range(TT):
                for kt in range(KT):
                    for i, part in enumerate((hT_hi, hT_lo)):
                        ins = pe.matmul(banks[4][:, 32 * t:32 * t + 32], part[:, kt, P * t:P * t + P].bitcast(F32),
                                        wdt[:, kt, :], start=kt == 0 and i == 0, stop=kt == KT - 1 and i == 1)
            ins.then_inc(dt_ps, 1)
            for ci in range(6):
                if ci >= 2:
                    pe.wait_ge(conv_done, ci - 1)
                pe.wait_ge(lo_w, 2 * ci + 2)
                for k in range(4):
                    bank = banks[2 * (ci % 2) + k // 2][:, 256 * (k % 2):256 * (k % 2) + 256]
                    for kt in range(KT):
                        u = 2 * ci + kt // 4
                        wh = cols(w_hi(u), 4)[:, kt % 4, P * k:P * k + P]
                        wl = cols(ring_r[:, b_slot(u), :], 4)[:, kt % 4, P * k:P * k + P]
                        pe.matmul(bank, wh, hT_hi[:, kt, :], start=kt == 0, stop=False)
                        pe.matmul(bank, wh, hT_lo[:, kt, :], start=False, stop=False)
                        ins = pe.matmul(bank, wl, hT_hi[:, kt, :], start=False, stop=kt == KT - 1)
                ins.then_inc(used_b, 2)
                if ci == 1:
                    pe.wait_ge(dtA_ready, 1)
                    b = banks[5]
                    for c in range(TT):
                        pe.matmul(b[:, 32 * c:32 * c + 32], C("tri_le"), dtA[:, c, :], start=True, stop=True)
                    pe.matmul(b[:, 64:96], C("ones"), dtA[:, 0, :], start=True, stop=True).then_inc(cum_ps, 1)
            pe.wait_ge(conv_done, 5)
            product(hT_hi, hT_lo, 0, AT_Z, 2)
            pe.wait_ge(xc_ready, 6)
            for g in range(4):
                ins = pe.transpose(banks[4][:, P * g:P * g + P], xc[:, 16 + g, 0:P], ident)
            ins.then_inc(bt_ps, 1)
            for c in range(TT):
                for g in range(4):
                    ins = pe.matmul(banks[6 + c][:, P * g:P * g + P], xc[:, 16 + g, P * c:P * c + P],
                                    xc[:, 20 + g, P * c:P * c + P], start=True, stop=True)
                ins.then_inc(cb_ps, 1)
            pe.wait_ge(z_ready, 2)
            pe.wait_ge(acum_ready, 1)
            pe.wait_ge(cb_ready, 2)

            def step_in(k):
                c, g = k // 4, k % 4
                if k >= 2:
                    pe.wait_ge(xdt_ready, k - 1)
                    pe.wait_ge(xt_ready, k - 1)
                for i in range(4):
                    ins = pe.transpose(banks[k % 2][:, P * i:P * i + P], xc[:, 4 * g + i, P * c:P * c + P], ident)
                ins.then_inc(xT_ps, 1)
                for b in range(2):
                    if k >= 1:
                        pe.wait_ge(seg_ready, 2 * k - 1 + b)
                    for i in range(4):
                        h = 8 * g + 4 * b + i
                        ins = pe.matmul(banks[2 + b][:, P * i:P * i + P], dtA[:, c, h:h + 1].to_broadcast([P, P]),
                                        C("tri_le"), start=True, stop=True)
                    ins.then_inc(rows_ps, 1)

            def step_out(k):
                c, g = k // 4, k % 4
                pe.wait_ge(xdt_ready, k + 1)
                pe.wait_ge(m_ready, 2 * k + 2)
                if k == 0:
                    pe.wait_ge(bt_ready, 1)
                if k >= 1:
                    pe.wait_ge(ysum_ready, k)
                    pe.wait_ge(state_ready, min(k, 4))
                if c == 0:
                    pe.wait_ge(xdte_ready, k + 1)
                    pe.matmul(banks[5][:, :], btok[:, P * g:P * g + P], xdte, start=True, stop=True)
                else:
                    pe.matmul(banks[5][:, :], xc[:, 20 + g, P:2 * P], state[:, 512 * g:512 * g + 512],
                              start=True, stop=True)
                for i in range(8):
                    ins = pe.matmul(banks[4][:, HD * i:HD * i + HD], seg[:, k % 2, P * i:P * i + P],
                                    xdt[:, k % 2, HD * i:HD * i + HD], start=True, stop=True)
                ins.then_inc(intra_ps, 1)

            step_in(0)
            for k in range(8):
                if k + 1 < 8:
                    step_in(k + 1)
                if k < 6:
                    c, half = 1 + k // 2, k % 2
                    if half == 0 and c >= 2:
                        pe.wait_ge(z_ready, 2 * c)
                    product(hT_hi, hT_lo, 6, AT_Z + 2 * c + half, 1, n_kt=KT, kt0=4 * half)
                step_out(k)
            pe.wait_ge(z_ready, 8)
            pe.wait_ge(seg_ready, 16)
            pe.wait_ge(xt_ready, 8)
            pe.wait_ge(xdt_ready, 8)
            for j, k in enumerate(TAIL_ORDER):
                c, g = k // 4, k % 4
                if j in (4, 6):
                    product(yT_hi, yT_lo, 0, AT_MOUT + j // 2 - 2, 1, ready=(yT_lo_ready, j - 4),
                            n_kt=16, kt0=2 * j - 8)
                pe.wait_ge(yn_ready, j + 1)
                if j >= 2:
                    pe.wait_ge(yT_ready, j - 1)
                for i in range(4):
                    ins = pe.transpose(banks[6 + j % 2][:, P * i:P * i + P],
                                       ym[:, c, 512 * g + P * i:512 * g + P * i + P], ident)
                ins.then_inc(yT_ps, 1)
            for i in (2, 3):
                product(yT_hi, yT_lo, 0, AT_MOUT + i, 1, ready=(yT_lo_ready, 2 * i), n_kt=16, kt0=4 * i)

            def turn_p(i):
                pe.wait_ge(p_loaded, 16 * (i + 1))
                for kp in range(2):
                    for t in range(TT):
                        ins = pe.transpose(banks[6][:, 256 * kp + P * t:256 * kp + P * t + P],
                                           pbuf[:, t, P * kp:P * kp + P], ident)
                ins.then_inc(pT_ps, 1)

            def embedding(i, at, x_from):
                base = 12 + 12 * i
                product(hT_hi, hT_lo, 0, at, 1, ready=(lo_turned, base), n_kt=KT,
                        middle=lambda: turn(4 + 3 * i, lambda n: (x_ready, x_from + n + 1), src=x, halves=(1,)))
                pe.wait_ge(*b_full(at + 1))
                w = cols(ring[:, b_slot(at + 1), :], 2)
                for c in range(2):
                    if c == 1:
                        pe.wait_ge(turned, 20 + 12 * i)
                    for t in range(TT):
                        for kp in range(2):
                            ins = pe.matmul(banks[4 + 2 * c + t][:, :], pT[:, kp, P * t:P * t + P],
                                            w[:, kp, 512 * c:512 * c + 512], start=kp == 0, stop=kp == 1)
                ins.then_inc(used_b, 1)
                product(hT_hi, hT_lo, 0, at + 2, 1, ready=(lo_turned, base + 2), n_kt=KT, kt0=4)

            pe.wait_ge(yT_ready, 8)
            turn_p(0)
            product(yT_hi, yT_lo, 2, AT_MOUT + 4, 2, n_kt=16)
            pe.wait_ge(pT_ready, 1)
            turn(4, lambda n: (x_ready, 8 + n + 1), src=x, halves=(0,))
            product(yT_hi, yT_lo, 2, AT_MOUT + 6, 2, n_kt=16, kt0=8)
            embedding(0, AT_PLE0, 8)
            product(hT_hi, hT_lo, 2, AT_PLE0 + 3, 1, n_kt=KT)
            turn(5, lambda n: (x_ready, 12 + n + 1), src=x, bank0=4, halves=(0,))
            product(hT_hi, hT_lo, 2, AT_PLE0 + 4, 1, n_kt=KT, kt0=4)

            def multiply(c, bank0):
                if c == 0:
                    product(hT_hi, hT_lo, bank0, AT_KV, 1, ready=(lo_turned, 16), n_kt=KT,
                            middle=lambda: turn(5, lambda n: (x_ready, 12 + n + 1), src=x, bank0=4, halves=(1,)))
                    product(hT_hi, hT_lo, bank0, AT_KV + 1, 1, ready=(lo_turned, 18), n_kt=KT, kt0=4)
                elif c < 4:
                    product(hT_hi, hT_lo, bank0, AT_KV + 2 * c, 2, ready=(lo_turned, 16))
                else:
                    product(hT2_hi, hT2_lo, bank0, AT_KV + 2 * c, 2, ready=(lo_turned2, 0))

            project(["qk", "qk", "v", "v", "qk", "qk", "gate", "gate"], multiply,
                    projb_act, projb_dve, qkTb_ps, qkTb_ready, qk_b)
            pe.wait_ge(projb_act, 16)
            pe.wait_ge(qkTb_ready, 8)

            def scores(h):
                if h >= 4:
                    pe.wait_ge(wm_ready, h - 3)
                r0, pair, bank = HD * (h % 2), h // 2, banks[h % 4]
                pe.matmul(bank[:, 0:256], kT_b[r0:r0 + HD, pair, 0:P], qT_b[r0:r0 + HD, pair, :],
                          start=True, stop=False, skip_group_check=True)
                pe.matmul(bank[:, 256:384], kT_b[r0:r0 + HD, pair, P:2 * P], qT_b[r0:r0 + HD, pair, P:2 * P],
                          start=False, stop=False, skip_group_check=True).then_inc(zz_ps, 1)

            def suffix(h):
                pe.wait_ge(sp_ready, h + 1)
                bank, sp_ = banks[h % 4], spz[:, h % 2, :]
                pe.matmul(bank[:, 128:256], C("negones"), sp_[:, 256:384], start=False, stop=False,
                          skip_group_check=True)
                pe.matmul(bank[:, 0:384], C("sufneg"), sp_, start=False, stop=True, skip_group_check=True)\
                  .then_inc(suf_ps, 1)

            def outputs(h):
                pe.wait_ge(we_ready, h + 1)
                if h >= 2:
                    pe.wait_ge(o_ready, h - 1)
                bank, w, at = banks[4 + h % 2], wz[:, h % 2, :], HD * h
                pe.matmul(bank[:, 0:HD], w[:, 0:128], v_b[:, 0, at:at + HD], start=True, stop=True)
                pe.matmul(bank[:, HD:2 * HD], w[:, 128:256], v_b[:, 0, at:at + HD], start=True, stop=False)
                pe.matmul(bank[:, HD:2 * HD], w[:, 256:384], v_b[:, 1, at:at + HD], start=False, stop=True)\
                  .then_inc(ob_ps, 1)

            scores(0)
            scores(1)
            for h in range(SB_HEADS):
                if h + 2 < SB_HEADS:
                    scores(h + 2)
                suffix(h)
                if h >= 2:
                    outputs(h - 2)
                if h == 12:
                    turn(6, lambda n: (o_ready, SB_HEADS // 2), halves=(0,))
            outputs(SB_HEADS - 2)
            outputs(SB_HEADS - 1)
            product(hT_hi, hT_lo, 0, AT_SOUT, 1, ready=(lo_turned, 20), n_kt=KT,
                    middle=lambda: turn(6, lambda n: (o_ready, SB_HEADS), halves=(1,)))
            product(hT_hi, hT_lo, 0, AT_SOUT + 1, 1, ready=(lo_turned, 22), n_kt=KT, kt0=4)
            pe.wait_ge(turned, 28)
            turn_p(1)
            product(hT_hi, hT_lo, 2, AT_SOUT + 2, 1, n_kt=KT)
            pe.wait_ge(pT_ready, 2)
            turn(7, lambda n: (x_ready, 16 + n + 1), src=x, halves=(0,))
            product(hT_hi, hT_lo, 2, AT_SOUT + 3, 1, n_kt=KT, kt0=4)
            embedding(1, AT_PLE1, 16)
            product(hT_hi, hT_lo, 2, AT_PLE1 + 3, 2)


INPUTS = ["x", "norm1_g", "w_in", "diff_q_g", "diff_k_g", "lambda_q1", "lambda_k1", "lambda_q2", "lambda_k2",
          "diff_sub_g", "moba_q_g", "moba_k_g", "rel_bias", "w_out", "norm2_g", "router_group",
          "router_expert", "w_gate", "w_up", "w_down", "p_2", "m_norm_2", "m_in_2", "m_conv_w_2",
          "m_conv_b_2", "m_dt_bias_2", "m_A_log_2", "m_D_2", "m_ynorm_2", "m_out_2", "kv_norm_2",
          "w_kv_2", "k_norm_2", "s_norm_2", "s_in_2", "q_norm_2", "s_out_2", "ple_norm_2",
          "ple_gate_2", "ple_proj_2"]


def kernel(**inputs):
    import concourse.bacc as bacc
    from concourse.bass_utils import run_bass_kernel_spmd

    nc = bacc.Bacc("TRN2", target_bir_lowering=False, num_devices=1)
    arrays = {f"in_{n}": np.ascontiguousarray(inputs[n]) for n in INPUTS}
    arrays["in_consts"] = constants()[0]
    arrays["in_onehot"] = bucket_onehot()
    d = {n[3:]: nc.dram_tensor(n, a.shape, F32, kind="ExternalInput").ap() for n, a in arrays.items()}
    out = nc.dram_tensor("out_dram", (1, S, D), F32, kind="ExternalOutput").ap()
    two_blocks(nc, d, out)
    r = run_bass_kernel_spmd(nc, [arrays], core_ids=[0])
    return r.results[0]["out_dram"]
```

```python
import math
from contextlib import ExitStack

import numpy as np

import concourse.bass as bass
from concourse import mybir

F32 = mybir.dt.float32
R32 = mybir.dt.float32r
I32 = mybir.dt.int32
ALU = mybir.AluOpType
ACT = mybir.ActivationFunctionType
AX = mybir.AxisListType

P = 128
D = 1024
S = 256
TT = S // P
KT = D // P
HD = 64
DIFF_HEADS, MOBA_HEADS = 4, 8
UNITS = DIFF_HEADS + MOBA_HEADS
MAPS = 2 * DIFF_HEADS + MOBA_HEADS
BUCKETS, MAX_DISTANCE = 32, 2048
EXPERTS, GROUPS, PER_GROUP, HIDDEN = 32, 4, 8, 256
SLOTS = 32
QUAD = 4
QUADS = EXPERTS // QUAD
D_INNER, SSM_HEADS, CONV_K = 2048, 32, 4
CONV_TILES = 24
SB_HEADS = 16
EPS = 1e-6
NEG = -1e30
LAMBDA_INIT = 0.8 - 0.6 * math.exp(-0.3 * 0)

RING = 12
UNIT = 2048
UNITS_A = 16
UNITS_B = 58
SHORT = 7
HI_SLOTS = (11, 0, 1, 2)
HT_HI_SLOT = 3
ARENA = 19776


def bucket_onehot():
    out = np.zeros((BUCKETS + 1, 384), np.float32)
    exact = BUCKETS // 2
    for i in range(384):
        n = S - 1 - i
        if n < 0:
            out[BUCKETS, i] = NEG
            continue
        b = n if n < exact else min(BUCKETS - 1, exact + int(
            math.log(n / exact) / math.log(MAX_DISTANCE / exact) * (BUCKETS - exact)))
        out[b, i] = 1.0
    return out


CONSTS = ["ident", "tri_le", "tri_lt", "flip", "sufneg", "negones", "ones", "segmask", "strictmask", "fold", "iota", "iota_low", "passes", "neghalf"]


def constants():
    a, b = np.arange(P)[:, None], np.arange(P)[None, :]
    parts = {
        "ident": a == b, "tri_le": a <= b, "tri_lt": a < b, "flip": a + b == P - 1,
        "sufneg": -1.0 * (a >= b), "negones": -np.ones((P, P)), "ones": np.ones((P, P)),
        "segmask": np.where(a <= b, 0.0, NEG),
        "strictmask": np.where(a < b, 0.0, NEG),
        "fold": (a % SLOTS) == np.arange(SLOTS)[None, :],
        "iota": np.broadcast_to(np.arange(32.0), (P, 32)),
        "iota_low": np.broadcast_to(np.arange(32.0) - 99.0, (P, 32)),
        "passes": np.broadcast_to(SLOTS * np.arange(8.0), (P, 8)),
        "neghalf": np.full((P, 8), -0.5),
    }
    at, col = {}, 0
    for name in CONSTS:
        at[name] = (col, parts[name].shape[1])
        col += parts[name].shape[1]
    return np.concatenate([np.asarray(parts[n], np.float32) for n in CONSTS], 1), at


def two_blocks(nc, d, out):
    _, const_at = constants()
    n_const = sum(w for _, w in const_at.values())
    ctx = ExitStack()
    with ctx:
        def sb(name, shape, dt=F32):
            return ctx.enter_context(nc.sbuf_tensor(name, shape, dt))

        def sem(name):
            return ctx.enter_context(nc.semaphore(name))

        base = -(-nc.sbuf_base // 64) * 64
        sb("slab", [P, 16 + RING * UNIT + ARENA + KT * S])

        def twin(name, shape, at):
            return (nc.alloc_sbuf_tensor_at(name, shape, F32, offset=base + 4 * at),
                    nc.alloc_sbuf_tensor_at(name + "_r", shape, R32, offset=base + 4 * at))

        ring, ring_r = twin("ring", [P, RING, UNIT], 0)
        arena, arena_r = twin("arena", [P, ARENA], RING * UNIT)
        hT, hT_lo = twin("hT", [P, KT, S], RING * UNIT + ARENA)
        hT_hi = ring_r[:, HT_HI_SLOT, :].rearrange("p (a b) -> p a b", a=KT)
        consts = sb("consts", [P, n_const])
        x = sb("x_residual", [P, TT, D])
        hn = sb("hn", [P, TT, D])
        gcol = sb("gcol", [P, 104])
        ccol = sb("ccol", [P, 96])
        g2 = sb("g2", [P, KT])
        gq = sb("gq", [P, 3])
        ga = sb("ga", [P, KT])
        headp = sb("headp", [P, 3, SSM_HEADS])
        nlam = sb("nlam", [P, 1])
        ss = sb("ss", [P, 6, 2, TT])
        rs = sb("rs", [P, 6, TT])
        pbuf = sb("pbuf", [P, TT, 256])
        counts_i = sb("counts_i", [P, 2], I32)
        banks = [ctx.enter_context(nc.psum_tensor(f"bank{i}", [P, 512], F32)) for i in range(8)]

        def C(name):
            at, n = const_at[name]
            return consts[:, at:at + n]

        class Arena:
            def __init__(self):
                self.at = 0

            def __call__(self, *dims):
                return self.twin(*dims)[0]

            def twin(self, *dims):
                n = math.prod(dims)
                self.at += n
                assert self.at <= ARENA
                return [self.view(a[:, self.at - n:self.at], dims) for a in (arena, arena_r)]

            @staticmethod
            def view(v, dims):
                if len(dims) == 2:
                    v = v.rearrange("p (a b) -> p a b", a=dims[0])
                if len(dims) == 3:
                    v = v.rearrange("p (a b c) -> p a b c", a=dims[0], b=dims[1])
                return v

        def over(ap, *dims):
            n = ap.shape[1]
            return ap.unsqueeze(2).to_broadcast([P, n, dims[0]])

        def repeat(ap, n):
            return ap.unsqueeze(1).to_broadcast([P, n, ap.shape[1]])

        def cols(ap, n):
            return ap.rearrange("p (a b) -> p a b", a=n)

        GAIN = {"norm1": 0, "m_norm": 8, "kv": 16, "s_norm": 24, "ple0": 32, "ple1": 40,
                "ynorm": 48, "conv_b": 64, "dq": 88, "dk": 89, "mq": 90, "mk": 91, "sq": 92,
                "sk": 93, "sub": 94, "norm2": 95}

        A = Arena()
        qk_a = A(2, TT, 512)
        sq_a = A(TT, 512)
        v_a = A(TT, D)
        qT_a, kT_a = A(KT, S), A(KT, S)
        hank, hank_lo = A.twin(UNITS, 256)
        _, hank_hi = A.twin(UNITS, 256)
        _, flip_r = A.twin(P)
        probs = A(4, 384)
        wT = A(2, 384)
        nmax, psum_, prec = A(MAPS, TT), A(MAPS, TT), A(MAPS, TT)
        ssd, rsd = A(UNITS, TT), A(UNITS, TT)
        hss, hrs = A(TT, 8), A(TT, 8)
        lamv = A(4, 64)
        lame = A(2)
        rows_a, rows_c = A(P), A(P)
        u_sb, tab, onehot = A(384), A(UNITS), A(384)
        y_a = hn
        xT = arena[:, 0:KT * S].rearrange("p (a b) -> p a b", a=KT)

        M = Arena()
        sel = M(TT, EXPERTS * SLOTS)
        selw_q = M(TT, P)
        xg = M(KT, P)
        selwT_q = M(S)
        hpre = M(2, 512)
        sg = M(QUAD, 64)
        hid = M(QUAD, 64)
        dn = M(D)
        rl = M(TT, 36)
        gmx, gex, gsum, gidx = M(TT), M(TT, GROUPS), M(TT), M(TT)
        geq, gc = M(TT, GROUPS), M(TT, GROUPS)
        el, el2, eq, cand = (M(TT, EXPERTS) for _ in range(4))
        oh1, oh2, wsel, msel, rk = (M(TT, EXPERTS) for _ in range(5))
        m1, m2, i1, w1, w2 = (M(TT) for _ in range(5))
        cmax, cpass = M(1), M(8)
        EXTRA = 7
        assert M.at + (EXTRA - 1) * UNIT <= ARENA
        extra = [arena[:, ARENA - (i + 1) * UNIT:ARENA - i * UNIT] for i in range(EXTRA - 1)]
        extra.append(hT.rearrange("p a b -> p (a b)"))

        B = Arena()
        xc, xc_r = B.twin(CONV_TILES, S)
        z, z_r = B.twin(TT, D_INNER)
        ym = B(TT, D_INNER)
        seg = B(2, 1024)
        xdt = B(2, 512)
        xdte = B(512)
        cb = B(TT, 512)
        btok = B(512)
        dtb, dtA = B(TT, SSM_HEADS), B(TT, SSM_HEADS)
        dta, dtu, dtw, dtl, dtq, dtv = (cols(seg[:, 0, 64 * i:64 * i + 64], TT) for i in range(6))
        acum, toend, ea = B(TT, SSM_HEADS), B(SSM_HEADS), B(SSM_HEADS)
        negA = B(SSM_HEADS)
        ssy, rsy = B(8), B(8)
        state = hn[:, :, :].rearrange("p a b -> p (a b)")
        yT, yT_lo = xc[:, 0:16, :], xc_r[:, 0:16, :]
        yT_hi = z_r.rearrange("p a b -> p (a b)").rearrange("p (a b) -> p a b", a=16)

        E_ = Arena()
        E_.at = 16896
        pT = E_(TT, S)
        sig = E_(2, 512)
        pret = E_(2, 512)

        K = Arena()
        qk_b = K(2, TT, 512)
        sq_b = K(TT, 512)
        v_b = K(TT, D)
        gate_b = K(TT, D)
        qT_b, kT_b = K(KT, S), K(KT, S)
        hT2, hT2_lo = K.twin(KT, S)
        _, hT2_hi = K.twin(KT, S)
        mask3 = K(384)
        absz, expz, lnz, spz, wz = (K(2, 384) for _ in range(5))
        hss_b, hrs_b = K(TT, 8), K(TT, 8)
        o_b = hn

        wr = sb("wr", [P, KT, 36])
        wdt = sb("wdt", [P, KT, SSM_HEADS])

        bias_dram = nc.dram_tensor("bias_rows", (UNITS, 384), F32, kind="Internal").ap()

        hi_a, lo_a, hi_w, lo_w, hi_turned, lo_turned, turned2, hi_turned2, lo_turned2, yT_hi_ready, yT_lo_ready, tap_ready = map(
            sem, ("hi_a", "lo_a", "hi_w", "lo_w", "hi_turned", "lo_turned", "turned2", "hi_turned2", "lo_turned2",
                  "yT_hi_ready", "yT_lo_ready", "tap_ready"))
        hank_hi_ready, hank_lo_ready = map(sem, ("hank_hi_ready", "hank_lo_ready"))
        x_loaded, const_loaded, rows_loaded, small_loaded, lam_loaded = map(sem, (
            "x_loaded", "const_loaded", "rows_loaded", "small_loaded", "lam_loaded"))
        tab_loaded, ones_set, u_ps, u_ready, bias_moved = map(sem, (
            "tab_loaded", "ones_set", "u_ps", "u_ready", "bias_moved"))
        full_a = [sem(f"full_a{i}") for i in range(RING)]
        full_x = [sem(f"full_x{i}") for i in range(EXTRA)]
        full_b = [sem(f"full_b{i}") for i in range(SHORT)]
        used_a, used_e, used_b = map(sem, ("used_a", "used_e", "used_b"))
        act_step, dve_step, pool_step = map(sem, ("act_step", "dve_step", "pool_step"))
        gains_ps, gains_ready, lam_sum, lam_exp = map(sem, (
            "gains_ps", "gains_ready", "lam_sum", "lam_exp"))
        ss_ready, hn_ready, turn_ps, turned, x_ready = map(sem, (
            "ss_ready", "hn_ready", "turn_ps", "turned", "x_ready"))
        proj_act, proj_dve, qkT_ps, qkT_ready = map(sem, ("proj_act", "proj_dve", "qkT_ps", "qkT_ready"))
        logits_ps, nmax_ready, probs_ready, w_ready, wT_ps, wT_ready, pv_ps, sqd_ready, y_ready = map(
            sem, ("logits_ps", "nmax_ready", "probs_ready", "w_ready", "wT_ps", "wT_ready", "pv_ps",
                  "sqd_ready", "y_ready"))
        router_ps, exp_in, exp_out, msel_ready, rank_ps, npass_ready = map(
            sem, ("router_ps", "exp_in", "exp_out", "msel_ready", "rank_ps", "npass_ready"))
        pass_step, sel0_ready, selw_ready, selT_ps = map(sem, (
            "pass_step", "sel0_ready", "selw_ready", "selT_ps"))
        gather_ps, xg_ready, h_ready, fold_ps, silu_ready, hid_ready, dn0_ps = map(sem, (
            "gather_ps", "xg_ready", "h_ready", "fold_ps", "silu_ready", "hid_ready", "dn0_ps"))
        dn0_ready, dn1_ready, selq_ready, scatter_ps = map(sem, (
            "dn0_ready", "dn1_ready", "selq_ready", "scatter_ps"))
        dt_ps, softplus_in, softplus_out, a_ready, dtA_ready, cum_ps = map(sem, (
            "dt_ps", "softplus_in", "softplus_out", "a_ready", "dtA_ready", "cum_ps"))
        acum_ready, decay_ready, conv_done, xc_ready, z_ready = map(sem, (
            "acum_ready", "decay_ready", "conv_done", "xc_ready", "z_ready"))
        bt_ps, bt_ready, cb_ps, cb_ready, xT_ps, xt_ready, xdt_ready, xdte_ready = map(sem, (
            "bt_ps", "bt_ready", "cb_ps", "cb_ready", "xT_ps", "xt_ready", "xdt_ready", "xdte_ready"))
        rows_ps, seg_ready, dec_ready, m_ready, intra_ps, state_ready, ysum_ready, yz_ready = map(sem, (
            "rows_ps", "seg_ready", "dec_ready", "m_ready", "intra_ps", "state_ready", "ysum_ready",
            "yz_ready"))
        ssy_ready, yn_ready, yT_ps, yT_ready, xd_ready = map(sem, (
            "ssy_ready", "yn_ready", "yT_ps", "yT_ready", "xd_ready"))
        p_loaded, pT_ps, pT_ready, sig_ready = map(sem, ("p_loaded", "pT_ps", "pT_ready", "sig_ready"))
        projb_act, projb_dve, qkTb_ps, qkTb_ready = map(sem, (
            "projb_act", "projb_dve", "qkTb_ps", "qkTb_ready"))
        zz_ps, ln_ready, sp_ready, suf_ps, we_ready, wm_ready, ob_ps, o_ready = map(sem, (
            "zz_ps", "ln_ready", "sp_ready", "suf_ps", "we_ready", "wm_ready", "ob_ps",
            "o_ready"))
        out_stored = sem("out_stored")
        rs_ready, hss_ready, hrs_ready, hssb_ready, hrsb_ready, rsd_ready, rsy_ready = map(sem, (
            "rs_ready", "hss_ready", "hrs_ready", "hssb_ready", "hrsb_ready", "rsd_ready", "rsy_ready"))

        def wide(w, c, half):
            return w[512 * half:512 * half + 512, 512 * c:512 * c + 512].rearrange("(k p) n -> p k n", p=P)

        w_in, w_out = d["w_in"][0], d["w_out"][0]
        units_a = [wide(w_in, c, h) for c in range(6) for h in range(2)]
        units_a += [wide(w_out, c, h) for c in range(2) for h in range(2)]
        m_in, m_out = d["m_in_2"][0], d["m_out_2"][0]
        XBC_ORDER = [4, 5, 0, 1, 2, 3]
        m_xbc = m_in[:, D_INNER:]
        units_b = [wide(m_xbc, c, h) for c in XBC_ORDER for h in range(2)]
        units_b += [wide(m_in, c, h) for c in range(4) for h in range(2)]
        units_b += [wide(m_out, c, h) for c in range(2) for h in range(4)]
        ple = [[wide(d["ple_gate_2"][i], c, h) for c in range(2) for h in range(2)] for i in range(2)]
        for i in range(2):
            ple[i].insert(1, d["ple_proj_2"][i].rearrange("(k p) n -> p k n", p=P))
        AT_Z, AT_MOUT, AT_PLE0 = 12, 20, 28
        units_b += ple[0]
        AT_KV = len(units_b)
        units_b += [wide(d["w_kv_2"], c, h) for c in range(4) for h in range(2)]
        units_b += [wide(d["s_in_2"][0], c, h) for c in range(4) for h in range(2)]
        AT_SOUT = len(units_b)
        units_b += [wide(d["s_out_2"][0], c, h) for c in range(2) for h in range(2)]
        AT_PLE1 = len(units_b)
        units_b += ple[1]
        assert len(units_a) == UNITS_A and len(units_b) == UNITS_B

        gate_v = d["w_gate"][0].rearrange("e (p k) n -> e p (k n)", k=KT)
        up_v = d["w_up"][0].rearrange("e (p k) n -> e p (k n)", k=KT)
        down_v = d["w_down"][0].rearrange("e (p f) n -> e p (f n)", f=2)
        QUAD_UNITS = [(v, e) for e in range(QUAD) for v in (gate_v, up_v)] + [(down_v, e) for e in range(QUAD)]

        def e_slot(j):
            return (UNITS_A + j) % RING

        def e_full(slot):
            return 16 * (1 + sum(a_slot(n) == slot for n in range(UNITS_A)))

        def e_view(j, odd):
            return extra[j] if odd and j < EXTRA else ring[:, e_slot(j), :]

        def a_slot(n):
            return 4 + (n % SHORT - UNITS_A % SHORT) % SHORT

        def b_slot(n):
            return (UNITS_A + n % SHORT) % RING

        def b_full(n):
            return full_b[n % SHORT], 16 * (n // SHORT + 1)

        SPLIT = [n for n in range(UNITS_B) if n not in (AT_PLE0 + 1, AT_PLE1 + 1)]
        H_KV, H_MOUT = SPLIT.index(AT_KV), SPLIT.index(AT_MOUT)
        H_PLE0, H_SOUT, H_PLE1 = SPLIT.index(AT_PLE0), SPLIT.index(AT_SOUT), SPLIT.index(AT_PLE1)

        class WeightsA:
            split, slot, used, hi_ready, lo_ready = range(UNITS_A), a_slot, used_a, hi_a, lo_a

            def full(n):
                return full_a[a_slot(n)], 16 * (n // SHORT + 1)

        class WeightsB:
            split, slot, used, hi_ready, lo_ready, full = SPLIT, b_slot, used_b, hi_w, lo_w, b_full

        def w_hi(h):
            return ring_r[:, HI_SLOTS[h % 4], :]

        def maps_of(u):
            return [2 * u, 2 * u + 1] if u < DIFF_HEADS else [u + DIFF_HEADS]

        def unit_of(m):
            return m // 2 if m < 2 * DIFF_HEADS else m - DIFF_HEADS

        SMALL_LOADS = 10
        ROW_LOADS = 16

        SPLIT_TURNS = [0, 1, 3, 4, 5, 6, 7]

        LOGIT_BANKS = [0, 1, 2, 7]

        block = ctx.enter_context(nc.Block())

        @block.sync
        def _(sp):
            xin = d["x"][0].rearrange("(t p) n -> t p n", p=P)
            for t in range(TT):
                sp.dma_start(x[:, t, :], xin[t]).then_inc(x_loaded, 16)
            sp.dma_start(cols(ring[:, a_slot(0), :], 4), units_a[0]).then_inc(full_a[a_slot(0)], 16)
            sp.dma_start(consts[:, :], d["consts"]).then_inc(const_loaded, 16)
            for name, n in (("dq", "diff_q_g"), ("dk", "diff_k_g"), ("mq", "moba_q_g"), ("mk", "moba_k_g"),
                            ("sq", "q_norm_2"), ("sk", "k_norm_2")):
                at = GAIN[name]
                sp.dma_start(cols(rows_a[at:at + 1, :], 2), bass.AP(d[n].tensor, 0, [[HD, 1], [0, 2], [1, HD]]))\
                  .then_inc(rows_loaded, 16)
            sp.dma_start(rows_a[GAIN["sub"]:GAIN["sub"] + 1, :], d["diff_sub_g"]).then_inc(rows_loaded, 16)
            for n in range(1, UNITS_A):
                if n == 2:
                    sp.dma_start(tab[0:BUCKETS, :], d["rel_bias"]).then_inc(tab_loaded, 16)
                    sp.dma_start(onehot[0:BUCKETS + 1, :], d["onehot"]).then_inc(tab_loaded, 16)
                    for i, m in enumerate(("lambda_q1", "lambda_k1", "lambda_q2", "lambda_k2")):
                        sp.dma_start(lamv[:, i, :], d[m].to_broadcast([P, HD])).then_inc(lam_loaded, 16)
                    sp.wait_ge(rows_loaded, 16 * ROW_LOADS)
                if n == 6:
                    sp.dma_start(pbuf[:, :, :], d["p_2"][0, 0].rearrange("(t p) n -> p t n", p=P)).then_inc(p_loaded, 16)
                    for i, m in enumerate(("m_dt_bias_2", "m_A_log_2", "m_D_2")):
                        sp.dma_start(headp[:, i, :], d[m].to_broadcast([P, SSM_HEADS])).then_inc(small_loaded, 16)
                    sp.dma_start(g2[:, :], d["norm2_g"].rearrange("o (p k) -> (o p) k", k=KT))\
                      .then_inc(small_loaded, 16)
                    sp.dma_start(wr[:, :, 0:GROUPS], d["router_group"][0].rearrange("(k p) n -> p k n", p=P))\
                      .then_inc(small_loaded, 16)
                    for g in range(GROUPS):
                        sp.dma_start(wr[:, :, GROUPS + PER_GROUP * g:GROUPS + PER_GROUP * (g + 1)],
                                     d["router_expert"][0, g].rearrange("(k p) n -> p k n", p=P))\
                          .then_inc(small_loaded, 16)
                    sp.dma_start(wdt[:, :, :], d["m_in_2"][0][:, 5120:5152].rearrange("(k p) n -> p k n", p=P))\
                      .then_inc(small_loaded, 16)
                if n == 8:
                    sp.wait_ge(u_ready, 1)
                    sp.dma_start(bias_dram, u_sb[0:UNITS, :]).then_inc(bias_moved, 16)
                if n == 10:
                    sp.wait_ge(bias_moved, 16)
                    sp.dma_start(hank, bass.AP(bias_dram.tensor, 0, [[1, P], [384, UNITS], [1, 256]]))\
                      .then_inc(bias_moved, 16)
                if n >= SHORT:
                    sp.wait_ge(used_a, n - SHORT + 1)
                sp.dma_start(cols(ring[:, a_slot(n), :], 4), units_a[n]).then_inc(full_a[a_slot(n)], 16)
            for j, (v, e) in enumerate(QUAD_UNITS):
                sp.wait_ge(used_a, UNITS_A - SHORT + j + 1 if j < SHORT else min(UNITS_A, UNITS_A - 4 + j - SHORT + 1))
                sp.dma_start(ring[:, e_slot(j), :], v[e]).then_inc(full_a[e_slot(j)], 16)
            for j, (v, e) in enumerate(QUAD_UNITS):
                if j == 0:
                    sp.wait_ge(x_ready, 2)
                if j == EXTRA - 1:
                    sp.wait_ge(used_a, UNITS_A)
                if j >= EXTRA:
                    sp.wait_ge(used_e, j + 1)
                sp.dma_start(e_view(j, 1), v[QUAD + e])\
                  .then_inc(full_x[j] if j < EXTRA else full_a[e_slot(j)], 16)
            sp.wait_ge(npass_ready, 1)
            npass = sp.value_load(counts_i[0:1, 0:1], min_val=1, max_val=S // SLOTS)
            first_free = sp.value_load(counts_i[0:1, 1:2], min_val=QUADS * RING - RING + 1,
                                       max_val=S // SLOTS * QUADS * RING)
            with sp.Fori(1, npass * (QUADS // 2)) as pair:
                for odd in range(2):
                    for j, (v, e) in enumerate(QUAD_UNITS):
                        ago = 2 if j < EXTRA else 1
                        sp.wait_ge(used_e, pair * (2 * RING) + ((odd - ago) * RING + j + 1))
                        src = v[bass.ds((pair % (QUADS // 2)) * (2 * QUAD) + (odd * QUAD + e), 1)]
                        sp.dma_start(e_view(j, odd), src.rearrange("e p n -> (e p) n"))\
                          .then_inc(full_x[j] if odd and j < EXTRA else full_a[e_slot(j)], 16)
            for n in range(UNITS_B):
                if n < SHORT:
                    sp.wait_ge(used_e, first_free + n)
                else:
                    sp.wait_ge(used_b, n - SHORT + 1)
                dst = cols(ring[:, b_slot(n), :], 2 if n in (AT_PLE0 + 1, AT_PLE1 + 1) else 4)
                sp.dma_start(dst, units_b[n]).then_inc(full_b[n % SHORT], 16)
            out_v = out[0].rearrange("(t p) n -> p t n", p=P)
            sp.wait_ge(x_ready, 22)
            sp.dma_start(out_v[:, :, 0:512], x[:, :, 0:512]).then_inc(out_stored, 16)
            for t in range(TT):
                sp.wait_ge(x_ready, 23 + t)
                sp.dma_start(out_v[:, t, 512:D], x[:, t, 512:D]).then_inc(out_stored, 16)
            sp.wait_ge(out_stored, 48)

        @block.scalar
        def _(act):
            chain = [0]

            def link(ins):
                chain[0] += 1
                ins.then_inc(act_step, 1)
                act.wait_ge(act_step, chain[0])

            for name, n in (("norm1", "norm1_g"), ("m_norm", "m_norm_2"), ("s_norm", "s_norm_2"),
                            ("ynorm", "m_ynorm_2"), ("conv_b", "m_conv_b_2"), ("ple0", "ple_norm_2"),
                            ("norm2", "norm2_g")):
                v = d[n].rearrange("o (k p) -> (o k) p", p=P)
                act.dma_start(rows_a[GAIN[name]:GAIN[name] + v.shape[0], :], v).then_inc(rows_loaded, 16)
            act.dma_start(rows_a[GAIN["kv"]:GAIN["kv"] + KT, :], d["kv_norm_2"].rearrange("(k p) -> k p", p=P))\
               .then_inc(rows_loaded, 16)
            act.dma_start(rows_c[0:96, :], d["m_conv_w_2"].rearrange("o j (k p) -> (o j k) p", p=P))\
               .then_inc(rows_loaded, 16)

            def squares(i, halves=(0, 1)):
                for half in halves:
                    for t in range(TT):
                        if i == 0:
                            act.wait_ge(x_loaded, 16 * TT)
                        else:
                            act.wait_ge(x_ready, 4 * i - 4 + 2 * half + t + 1)
                        at = (slice(None), t, slice(512 * half, 512 * half + 512))
                        act.activation(hn[at], x[at], ACT.Square, accum_out=ss[:, i, half, t:t + 1])\
                           .then_inc(ss_ready, 1)

            def hi(*hs, of=WeightsB):
                for h in hs:
                    act.wait_ge(*of.full(of.split[h]))
                    if h >= 4:
                        act.wait_ge(of.used, of.split[h - 4] + 1)
                    act.activation(w_hi(h), ring[:, of.slot(of.split[h]), :], ACT.Copy).then_inc(of.hi_ready, 1)

            def turned_hi(i, halves=(0, 1)):
                for n in range(2 * halves[0], 2 * halves[-1] + 2):
                    half, t = n // 2, n % 2
                    at = (slice(None), slice(4 * half, 4 * half + 4), slice(P * t, P * t + P))
                    act.wait_ge(turned, 4 * i + n + 1)
                    act.activation(hT_hi[at], hT[at], ACT.Copy).then_inc(hi_turned, 1)

            hi(0, of=WeightsA)
            squares(0)
            turned_hi(0)
            hi(1, of=WeightsA)
            hi(2, of=WeightsA)
            act.wait_ge(lam_sum, 1)
            act.activation(lame[:, :], lame[:, :], ACT.Exp).then_inc(lam_exp, 1)
            hi(3, of=WeightsA)
            def project(kinds, used, at, c_act, c_dve, t_ps, t_ready, sq, v, gate, turned_to, i, h0=0,
                        of=WeightsB):
                j = 0
                n_v = n_g = 0
                act.wait_ge(rs_ready, i + 1)
                pend = None

                def copy_turned(jj, dst, gain):
                    for t in range(TT):
                        act.wait_ge(t_ps, 2 * jj + t + 1)
                        src, to = cols(banks[4 + t][:, :], 4), dst[:, :, P * t:P * t + P]
                        if gain is None:
                            act.activation(to, src, ACT.Copy).then_inc(t_ready, 1)
                        else:
                            act.activation(to, src, ACT.Identity, scale=gain).then_inc(t_ready, 1)

                for c, kind in enumerate(kinds):
                    hi(h0 + 2 * c + 4, of=of)
                    act.wait_ge(used, at + 2 * c + 2)
                    for t in range(TT):
                        bank = banks[2 * (c % 2) + t]
                        if kind == "qk":
                            if j >= 1 and t == 0:
                                act.wait_ge(c_dve, 2 * j)
                            act.activation(sq[:, t, :], bank[:, :], ACT.Square, scale=rs[:, i, t:t + 1])\
                               .then_inc(c_act, 1)
                        elif kind == "v":
                            act.activation(v[:, t, 512 * n_v:512 * n_v + 512], bank[:, :], ACT.Identity,
                                           scale=rs[:, i, t:t + 1]).then_inc(c_act, 1)
                        else:
                            act.activation(gate[:, t, 512 * n_g:512 * n_g + 512], bank[:, :], ACT.Silu,
                                           scale=rs[:, i, t:t + 1])\
                               .then_inc(c_act, 1)
                    n_v += kind == "v"
                    n_g += kind == "gate"
                    if pend is not None:
                        copy_turned(*pend)
                        pend = None
                    if i == 0 or c < len(kinds) - 1:
                        hi(h0 + 2 * c + 5, of=of)
                    if i == 0 and c == 2:
                        act.wait_ge(bias_moved, 32)
                        act.activation(flip_r, C("flip"), ACT.Copy)
                        act.activation(hank_hi, hank, ACT.Copy).then_inc(hank_hi_ready, 1)
                    if kind == "qk":
                        pend = (j, *turned_to[j])
                        j += 1
                if pend is not None:
                    copy_turned(*pend)

            act.wait_ge(gains_ready, 3)
            project(["qk", "qk", "v", "qk", "qk", "v"], used_a, 0, proj_act, proj_dve, qkT_ps, qkT_ready,
                    sq_a, v_a, None, [(qT_a[:, 0:4, :], gq[:, 0:1]), (kT_a[:, 0:4, :], None),
                                      (qT_a[:, 4:8, :], gq[:, 1:2]), (kT_a[:, 4:8, :], None)], 0, of=WeightsA)

            def exps(u):
                for m in maps_of(u):
                    act.wait_ge(nmax_ready, m + 1)
                    if m >= 4:
                        act.wait_ge(wT_ps, unit_of(m - 4) + 1)
                    bank = banks[LOGIT_BANKS[m % 4]]
                    act.activation(probs[:, m % 4, 0:128], bank[:, 0:128], ACT.Exp, bias=nmax[:, m, 0:1],
                                   accum_out=psum_[:, m, 0:1])
                    act.activation(probs[:, m % 4, 128:384], bank[:, 128:384], ACT.Exp, bias=nmax[:, m, 1:2],
                                   accum_out=psum_[:, m, 1:2]).then_inc(probs_ready, 1)

            exps(0)
            for u in range(UNITS + 1):
                if u + 1 < UNITS:
                    exps(u + 1)
                if u < UNITS:
                    act.wait_ge(wT_ps, u + 1)
                    if u >= 2:
                        act.wait_ge(pv_ps, u - 1)
                    act.activation(wT[:, u % 2, :], banks[3 + u % 2][:, 0:384], ACT.Copy).then_inc(wT_ready, 1)
                if 1 <= u <= DIFF_HEADS:
                    act.wait_ge(pv_ps, u)
                    for t in range(TT):
                        ins = act.activation(sq_a[:, t, 128 * (u - 1):128 * u], banks[5 + (u - 1) % 2][:, 128 * t:128 * t + 128],
                                             ACT.Square, accum_out=ssd[:, u - 1, t:t + 1])
                    ins.then_inc(sqd_ready, 1)

            turned_hi(1)
            squares(1)
            act.wait_ge(exp_in, 1)
            act.activation(gex, gex, ACT.Exp).then_inc(exp_out, 1)
            act.wait_ge(exp_in, 2)
            act.activation(m2, m2, ACT.Exp).then_inc(exp_out, 1)

            act.wait_ge(npass_ready, 1)
            npass = act.value_load(counts_i[0:1, 0:1], min_val=1, max_val=S // SLOTS)
            act.sem_inc(h_ready, 4)
            act.sem_inc(dn0_ready, 1)
            with act.Fori(0, npass) as r:
                with act.Fori(0, QUADS) as g:
                    q = r * QUADS + g
                    for e in range(QUAD):
                        act.wait_ge(used_e, q * RING + (2 * e + 2))
                        act.wait_ge(fold_ps, q * QUAD + (e + 3))
                        act.activation(hpre[:, e % 2, :], banks[6 + e % 2][:, :], ACT.Copy).then_inc(h_ready, 1)
                        if e == 1:
                            act.wait_ge(selT_ps, q + 2)
                            act.wait_ge(scatter_ps, q + 1)
                            act.activation(selwT_q, banks[5][:, 256:512], ACT.Copy).then_inc(selq_ready, 1)
                        if e >= 1:
                            act.wait_ge(fold_ps, q * QUAD + (e + QUAD))
                            act.activation(sg[:, e - 1, :], banks[4 + (e - 1) % 2][:, 0:64], ACT.Silu)\
                               .then_inc(silu_ready, 1)
                    act.wait_ge(fold_ps, q * QUAD + 2 * QUAD)
                    act.activation(sg[:, 3, :], banks[5][:, 0:64], ACT.Silu).then_inc(silu_ready, 1)
                    act.wait_ge(dn0_ps, q + 1)
                    act.wait_ge(scatter_ps, q + 1)
                    act.activation(dn[:, 0:512], banks[6][:, :], ACT.Copy).then_inc(dn0_ready, 1)

            squares(2, (0,))
            hi(0)
            squares(2, (1,))
            hi(1)
            turned_hi(3)
            hi(2, 3)
            act.activation(negA, headp[:, 1, :], ACT.Exp).then_inc(a_ready, 1)
            act.wait_ge(softplus_in, 1)
            act.activation(dtu, dta, ACT.Exp, scale=-1.0).then_inc(softplus_out, 1)
            act.wait_ge(softplus_in, 2)
            act.activation(dtl, dtw, ACT.Ln).then_inc(softplus_out, 1)

            def xc_silu(ci):
                act.wait_ge(conv_done, ci + 1)
                c = XBC_ORDER[ci]
                v = xc[:, 4 * c:4 * c + 4, :]
                act.activation(v, v, ACT.Silu).then_inc(xc_ready, 1)

            def z_silu(c):
                act.wait_ge(used_b, AT_Z + 2 * c + 2)
                for t in range(TT):
                    act.activation(z[:, t, 512 * c:512 * c + 512], banks[(6 if c else 0) + t][:, :], ACT.Silu)\
                       .then_inc(z_ready, 1)

            for ci, c in enumerate(XBC_ORDER):
                act.wait_ge(used_b, 2 * ci + 2)
                for k in range(4):
                    tile = 4 * c + k
                    ins = act.activation(xc[:, tile, :],
                                         banks[2 * (ci % 2) + k // 2][:, 256 * (k % 2):256 * (k % 2) + 256],
                                         ACT.Identity, bias=gcol[:, 64 + tile:65 + tile],
                                         scale=ccol[:, 24 * 3 + tile:24 * 3 + tile + 1])
                ins.then_inc(tap_ready, 1)
                hi(2 * ci + 4, 2 * ci + 5)
                if ci >= 1:
                    xc_silu(ci - 1)
            act.wait_ge(bt_ps, 1)
            act.activation(btok, banks[4][:, :], ACT.Copy).then_inc(bt_ready, 1)
            for c in range(TT):
                act.wait_ge(cb_ps, c + 1)
                act.activation(cb[:, c, :], banks[6 + c][:, :], ACT.Copy).then_inc(cb_ready, 1)
            xc_silu(5)
            hi(16)
            z_silu(0)
            act.wait_ge(acum_ready, 1)
            link(act.activation(toend, toend, ACT.Exp))
            act.activation(ea, acum[:, 1, :], ACT.Exp).then_inc(decay_ready, 1)
            def mamba_tail(k):
                c, g = k // 4, k % 4
                act.wait_ge(yz_ready, k + 1)
                if k >= 1:
                    act.wait_ge(ssy_ready, k)
                act.activation(btok, ym[:, c, 512 * g:512 * g + 512], ACT.Square,
                               accum_out=ssy[:, k:k + 1]).then_inc(ssy_ready, 1)

            def state_copy(k):
                act.wait_ge(intra_ps, k + 1)
                act.activation(state[:, 512 * k:512 * k + 512], banks[5][:, :], ACT.Copy).then_inc(state_ready, 1)

            for k in range(8):
                c, g = k // 4, k % 4
                act.wait_ge(xT_ps, k + 1)
                act.activation(ym[:, c, 512 * g:512 * g + 512], banks[k % 2][:, :], ACT.Copy)\
                   .then_inc(xt_ready, 1)
                for b in range(2):
                    act.wait_ge(seg_ready, 2 * k + b + 1)
                    v = seg[:, k % 2, 512 * b:512 * b + 512]
                    act.activation(v, v, ACT.Exp).then_inc(dec_ready, 1)
                if 1 <= k <= 4:
                    state_copy(k - 1)
                if k in (2, 4, 6):
                    z_silu(k // 2)
                if k <= 6:
                    hi(17 + k)
                if k >= 4:
                    mamba_tail(k - 4)
            for k in range(4, 8):
                mamba_tail(k)
            act.wait_ge(yz_ready, 8)
            for k in range(8):
                at = (slice(None), slice(4 * (k % 4), 4 * (k % 4) + 4), slice(P * (k // 4), P * (k // 4) + P))
                act.wait_ge(yT_ready, k + 1)
                act.activation(yT_hi[at], yT[at], ACT.Copy).then_inc(yT_hi_ready, 1)
            hi(*range(H_MOUT + 4, H_MOUT + 8))

            def embed(i):
                act.wait_ge(pT_ps, i + 1)
                act.activation(pT, cols(banks[6][:, :], 2), ACT.Copy).then_inc(pT_ready, 1)

            def sigmoids(i, at, c):
                act.wait_ge(rs_ready, 4 + 2 * i)
                act.wait_ge(used_b, at + 3 + 2 * c)
                for t in range(TT):
                    if c == 1:
                        act.wait_ge(x_ready, 12 + 8 * i + t + 1)
                    act.activation(sig[:, t, :], banks[2 * c + t][:, :], ACT.Sigmoid,
                                   scale=rs[:, 3 + 2 * i, t:t + 1]).then_inc(sig_ready, 1)

            embed(0)
            act.dma_start(pbuf[:, :, :], d["p_2"][1, 0].rearrange("(t p) n -> p t n", p=P)).then_inc(p_loaded, 16)
            squares(3, (0,))
            hi(H_PLE0)
            turned_hi(4, (0,))
            hi(H_PLE0 + 1, H_PLE0 + 2)
            squares(3, (1,))
            turned_hi(4, (1,))
            hi(H_PLE0 + 3, H_KV)
            sigmoids(0, AT_PLE0, 0)

            squares(4, (0,))
            hi(H_KV + 1)
            turned_hi(5, (0,))
            hi(H_KV + 2)
            sigmoids(0, AT_PLE0, 1)
            squares(4, (1,))
            turned_hi(5, (1,))
            hi(H_KV + 3)
            for n in range(4):
                half, t = n // 2, n % 2
                at = (slice(None), slice(4 * half, 4 * half + 4), slice(P * t, P * t + P))
                act.wait_ge(turned2, n + 1)
                act.activation(hT2_hi[at], hT2[at], ACT.Copy).then_inc(hi_turned2, 1)
            project(["qk", "qk", "v", "v", "qk", "qk", "gate", "gate"], used_b, AT_KV, projb_act, projb_dve,
                    qkTb_ps, qkTb_ready, sq_b, v_b, gate_b,
                    [(kT_b[:, 0:4, :], None), (kT_b[:, 4:8, :], None),
                     (qT_b[:, 0:4, :], gq[:, 2:3]), (qT_b[:, 4:8, :], gq[:, 2:3])], 4, H_KV)
            act.preload_act_table_set("natural_log_exp_and_others")

            def mark(ins):
                chain[0] += 1
                ins.then_inc(act_step, 1)
                return chain[0]

            def absolute(h):
                act.wait_ge(zz_ps, h + 1)
                mark(act.activation(absz[:, h % 2, :], banks[h % 4][:, 0:384], ACT.Abs))

            absolute(0)

            def weights(h):
                act.wait_ge(wm_ready, h + 1)
                act.activation(wz[:, h % 2, :], wz[:, h % 2, :], ACT.Exp).then_inc(we_ready, 1)

            for h in range(SB_HEADS):
                if h >= 2:
                    act.wait_ge(sp_ready, h - 1)
                act.wait_ge(act_step, chain[0])
                exped = mark(act.activation(expz[:, h % 2, :], absz[:, h % 2, :], ACT.Exp, scale=-1.0))
                if h + 1 < SB_HEADS:
                    absolute(h + 1)
                act.wait_ge(act_step, exped)
                act.activation(lnz[:, h % 2, :], expz[:, h % 2, :], ACT.Ln, bias=1.0).then_inc(ln_ready, 1)
                if h >= 2:
                    weights(h - 2)
                if h == 3:
                    hi(H_SOUT + 3)
                if h == 14:
                    turned_hi(6, (0,))
            weights(SB_HEADS - 2)
            weights(SB_HEADS - 1)
            turned_hi(6, (1,))
            hi(H_PLE1)
            embed(1)
            squares(5, (0,))
            hi(H_PLE1 + 1)
            turned_hi(7, (0,))
            hi(H_PLE1 + 2)
            squares(5, (1,))
            turned_hi(7, (1,))
            hi(H_PLE1 + 3)
            sigmoids(1, AT_PLE1, 0)
            sigmoids(1, AT_PLE1, 1)

        @block.gpsimd
        def _(pool):
            def y_z(k):
                c, g = k // 4, k % 4
                y = ym[:, c, 512 * g:512 * g + 512]
                pool.wait_ge(ysum_ready, k + 1)
                pool.wait_ge(z_ready, 2 * g + 2)
                pool.tensor_tensor(y, y, z[:, c, 512 * g:512 * g + 512], ALU.mult).then_inc(yz_ready, 1)

            chain = [0]

            def link(ins):
                chain[0] += 1
                ins.then_inc(pool_step, 1)
                pool.wait_ge(pool_step, chain[0])

            def rsqrt(dst, src, eps, ready, step, done):
                pool.wait_ge(ready, step)
                link(pool.tensor_scalar(dst, src, eps, None, ALU.add))
                pool.tensor_tensor(dst, dst, C("neghalf")[:, 0:src.shape[1]], ALU.pow).then_inc(done, 1)

            def norm(i):
                pool.wait_ge(ss_ready, 4 * i + 4)
                link(pool.tensor_tensor(rs[:, i, :], ss[:, i, 0, :], ss[:, i, 1, :], ALU.add))
                link(pool.tensor_scalar(rs[:, i, :], rs[:, i, :], 1.0 / D, EPS, ALU.mult, ALU.add))
                pool.tensor_tensor(rs[:, i, :], rs[:, i, :], C("neghalf")[:, 0:TT], ALU.pow).then_inc(rs_ready, 1)
                pool.wait_ge(rs_ready, i + 1)

            def project(i, hs, hr, hsum, hroot):
                for j in range(4):
                    for t in range(TT):
                        v = hr[:, t, :]
                        pool.wait_ge(hsum, 2 * j + t + 1)
                        link(pool.tensor_scalar(v, hs[:, t, :], EPS * HD, None, ALU.add))
                        link(pool.tensor_tensor(v, v, C("neghalf"), ALU.pow))
                        pool.tensor_scalar(v, v, rs[:, i, t:t + 1], None, ALU.mult).then_inc(hroot, 1)

            pool.wait_ge(const_loaded, 16)
            norm(0)
            project(0, hss, hrs, hss_ready, hrs_ready)
            for u in range(DIFF_HEADS):
                rsqrt(rsd[:, u, :], ssd[:, u, :], EPS * 128, sqd_ready, u + 1, rsd_ready)
            norm(1)
            norm(2)
            for k in range(8):
                c, g = k // 4, k % 4
                y = ym[:, c, 512 * g:512 * g + 512]
                pool.wait_ge(xt_ready, k + 1)
                if k == 0:
                    pool.wait_ge(small_loaded, 16 * SMALL_LOADS)
                    pool.wait_ge(cb_ready, 2)
                    pool.wait_ge(decay_ready, 1)
                if c == 0:
                    pool.wait_ge(xdt_ready, k + 1)
                    if k >= 1:
                        pool.wait_ge(intra_ps, k)
                    pool.tensor_tensor(cols(xdte, 8), cols(xdt[:, k % 2, :], 8),
                                       over(toend[:, 8 * g:8 * g + 8], HD), ALU.mult).then_inc(xdte_ready, 1)
                for b in range(2):
                    pool.wait_ge(dec_ready, 2 * k + b + 1)
                    v = cols(seg[:, k % 2, 512 * b:512 * b + 512], 4)
                    pool.tensor_tensor(v, v, repeat(cb[:, c, P * g:P * g + P], 4), ALU.mult).then_inc(m_ready, 1)
                pool.tensor_tensor(cols(y, 8), cols(y, 8), over(headp[:, 2, 8 * g:8 * g + 8], HD), ALU.mult)\
                    .then_inc(xd_ready, 1)
                for j in {2: [0], 3: [1], 5: [2], 6: [3], 7: [4, 5]}.get(k, []):
                    y_z(j)
            rsqrt(rsy[:, 0:4], ssy[:, 0:4], EPS * 512, ssy_ready, 4, rsy_ready)
            y_z(6)
            y_z(7)
            rsqrt(rsy[:, 4:8], ssy[:, 4:8], EPS * 512, ssy_ready, 8, rsy_ready)
            norm(3)
            norm(4)
            project(4, hss_b, hrs_b, hssb_ready, hrsb_ready)
            norm(5)

        @block.vector
        def _(dve):
            chain = [0]

            def link(ins):
                chain[0] += 1
                ins.then_inc(dve_step, 1)
                dve.wait_ge(dve_step, chain[0])

            dve.memset(tab[BUCKETS:BUCKETS + 1, :], 1.0).then_inc(ones_set, 1)
            for i, (dst, n) in enumerate(((gcol, 103), (ccol, 96))):
                dve.wait_ge(gains_ps, i + 1)
                dve.tensor_copy(dst[:, 0:n], banks[4 + i][:, 0:n]).then_inc(gains_ready, 1)

            def norm(i, permuted=False):
                for t in range(TT):
                    dve.wait_ge(rs_ready, i + 1)
                    src, dst = x[:, t, :], hn[:, t, :]
                    if permuted:
                        src, dst = src.rearrange("p (j k) -> p k j", k=KT), cols(dst, KT)
                    dve.tensor_scalar(dst, src, rs[:, i, t:t + 1], None, ALU.mult)\
                       .then_inc(hn_ready, 1)

            def lo(*hs, of=WeightsB):
                for h in hs:
                    slot = of.slot(of.split[h])
                    dve.wait_ge(of.hi_ready, h + 1)
                    dve.tensor_tensor(ring_r[:, slot, :], ring[:, slot, :], w_hi(h).bitcast(F32), ALU.subtract)\
                       .then_inc(of.lo_ready, 1)

            def part(n):
                return slice(None), slice(4 * (n // 2), 4 * (n // 2) + 4), slice(P * (n % 2), P * (n % 2) + P)

            def low(i, n):
                dve.wait_ge(hi_turned, 4 * SPLIT_TURNS.index(i) + n + 1)
                dve.tensor_tensor(hT_lo[part(n)], hT[part(n)], hT_hi[part(n)].bitcast(F32), ALU.subtract)\
                   .then_inc(lo_turned, 1)

            def turn(i, gain, second=None, split=False, bank0=6, halves=(0, 1), dst=hT):
                for n in range(2 * halves[0], 2 * halves[-1] + 2):
                    half = n // 2
                    dve.wait_ge(turn_ps, 4 * i + n + 1)
                    src = cols(banks[bank0 + n % 2][:, :], 4)
                    dve.tensor_tensor(dst[part(n)], src, over(gain[:, 4 * half:4 * half + 4], P), ALU.mult)\
                       .then_inc(turned, 1)
                    if split and n % 2:
                        low(i, n - 1)
                        low(i, n)
                if second is not None:
                    for n in range(2 * halves[0], 2 * halves[-1] + 2):
                        half = n // 2
                        dve.tensor_tensor(hT2[part(n)], cols(banks[bank0 + n % 2][:, :], 4),
                                          over(second[:, 4 * half:4 * half + 4], P), ALU.mult).then_inc(turned2, 1)

            def G(name, n=KT):
                return gcol[:, GAIN[name]:GAIN[name] + n]

            dve.wait_ge(gains_ready, 2)
            lo(0, of=WeightsA)
            turn(0, G("norm1"), split=True)
            lo(1, of=WeightsA)
            for i, a in enumerate(("dq", "mq", "sq")):
                at = GAIN[a]
                link(dve.tensor_scalar(gq[:, i:i + 1], gcol[:, at:at + 1], gcol[:, at + 1:at + 2], 8.0,
                                       ALU.mult, ALU.mult))
            link(dve.memset(ga[:, :], 1.0))
            dve.tensor_scalar(ga[:, 0:4], G("sub", 1).to_broadcast([P, 4]), 1.0 - LAMBDA_INIT, None, ALU.mult)\
               .then_inc(gains_ready, 1)
            dve.wait_ge(gains_ready, 3)
            lo(2, of=WeightsA)
            dve.wait_ge(lam_loaded, 16 * 4)
            for i in range(2):
                link(dve.tensor_tensor(lamv[:, 2 * i, :], lamv[:, 2 * i, :], lamv[:, 2 * i + 1, :], ALU.mult))
                ins = dve.tensor_reduce(lame[:, i:i + 1], lamv[:, 2 * i, :], AX.X, ALU.add)
                if i == 0:
                    link(ins)
            ins.then_inc(lam_sum, 1)
            lo(3, of=WeightsA)
            dve.wait_ge(lam_exp, 1)
            link(dve.tensor_scalar(nlam[:, :], lame[:, 1:2], lame[:, 0:1], -LAMBDA_INIT, ALU.subtract, ALU.add))
            dve.wait_ge(u_ps, 1)
            dve.tensor_copy(u_sb[0:UNITS, :], banks[7][0:UNITS, 0:384]).then_inc(u_ready, 1)

            def project(kinds, c_act, c_dve, t_ps, sq, qk, hs, hr, hsum, hroot, h0=0, of=WeightsB):
                j = 0
                for c, kind in enumerate(kinds):
                    lo(*([h0 + 2 * c + 3] if c else []), h0 + 2 * c + 4, of=of)
                    if of is WeightsA and c == 2:
                        dve.wait_ge(hank_hi_ready, 1)
                        dve.tensor_tensor(hank_lo, hank, hank_hi.bitcast(F32), ALU.subtract).then_inc(hank_lo_ready, 1)
                    if kind != "qk":
                        continue
                    if j >= 2:
                        dve.wait_ge(t_ps, 2 * (j - 1))
                    for t in range(TT):
                        dve.wait_ge(c_act, 2 * c + t + 1)
                        dve.tensor_reduce(hs[:, t, :], cols(sq[:, t, :], 8), AX.X, ALU.add).then_inc(hsum, 1)
                    for t in range(TT):
                        dve.wait_ge(hroot, 2 * j + t + 1)
                        dve.tensor_tensor(cols(qk[:, j % 2, t, :], 8), cols(banks[2 * (c % 2) + t][:, :], 8),
                                          over(hr[:, t, :], HD), ALU.mult).then_inc(c_dve, 1)
                    j += 1
                if of is WeightsA:
                    lo(h0 + 2 * len(kinds) + 3, of=of)

            project(["qk", "qk", "v", "qk", "qk", "v"], proj_act, proj_dve, qkT_ps,
                    sq_a, qk_a, hss, hrs, hss_ready, hrs_ready, of=WeightsA)

            def maxima(u):
                for m in maps_of(u):
                    dve.wait_ge(logits_ps, m + 1)
                    bank = banks[LOGIT_BANKS[m % 4]]
                    dve.tensor_reduce(nmax[:, m, 0:1], bank[:, 0:128], AX.X, ALU.max, negate=True)
                    dve.tensor_reduce(nmax[:, m, 1:2], bank[:, 128:384], AX.X, ALU.max, negate=True)\
                       .then_inc(nmax_ready, 1)

            def combine(u):
                ms = maps_of(u)
                dve.wait_ge(probs_ready, ms[-1] + 1)
                for m in ms[:-1]:
                    link(dve.reciprocal(prec[:, m, :], psum_[:, m, :]))
                last = dve.reciprocal(prec[:, ms[-1], :], psum_[:, ms[-1], :])
                if u >= DIFF_HEADS:
                    last.then_inc(w_ready, 1)
                    return
                link(last)
                a, b = ms
                link(dve.tensor_scalar(prec[:, b, :], prec[:, b, :], nlam[:, 0:1], None, ALU.mult))
                parts = ((0, 128), (128, 384))
                for t, (lo, hi) in enumerate(parts):
                    ins = dve.tensor_scalar(probs[:, b % 4, lo:hi], probs[:, b % 4, lo:hi],
                                            prec[:, b, t:t + 1], None, ALU.mult)
                link(ins)
                for t, (lo, hi) in enumerate(parts):
                    pa = probs[:, a % 4, lo:hi]
                    ins = dve.scalar_tensor_tensor(pa, pa, prec[:, a, t:t + 1], probs[:, b % 4, lo:hi],
                                                   ALU.mult, ALU.add)
                ins.then_inc(w_ready, 1)

            def outputs(u):
                bank = banks[5 + u % 2]
                if u < DIFF_HEADS:
                    dve.wait_ge(rsd_ready, u + 1)
                    for t in range(TT):
                        ins = dve.tensor_scalar(y_a[:, t, 128 * u:128 * u + 128], bank[:, 128 * t:128 * t + 128],
                                                rsd[:, u, t:t + 1], math.sqrt(128.0), ALU.mult, ALU.mult)
                else:
                    dve.wait_ge(pv_ps, u + 1)
                    dve.wait_ge(w_ready, u + 1)
                    h, m = u - DIFF_HEADS, u + DIFF_HEADS
                    for t in range(TT):
                        ins = dve.tensor_scalar(y_a[:, t, 512 + HD * h:512 + HD * h + HD],
                                                bank[:, 128 * t:128 * t + HD], prec[:, m, t:t + 1], None, ALU.mult)
                ins.then_inc(y_ready, 1)

            maxima(0)
            for u in range(UNITS + 2):
                if u + 1 < UNITS:
                    maxima(u + 1)
                if u < UNITS:
                    combine(u)
                if u >= 2:
                    outputs(u - 2)
            turn(1, ga, split=True, bank0=3)

            def add_product(c, bank0, used, at):
                dve.wait_ge(used, at)
                for t in range(TT):
                    xv = x[:, t, 512 * c:512 * c + 512]
                    dve.tensor_tensor(xv, banks[bank0 + t][:, :], xv, ALU.add).then_inc(x_ready, 1)

            for c in range(2):
                add_product(c, 2 * c, used_a, 12 + 2 * c + 2)
                turn(2, G("norm2"), halves=(c,), dst=xT)
            norm(1, permuted=True)

            dve.wait_ge(router_ps, 1)
            for t in range(TT):
                ins = dve.tensor_scalar(rl[:, t, :], banks[4 + t][:, 0:36], rs[:, 1, t:t + 1], None, ALU.mult)
            link(ins)
            iota32 = C("iota")
            gl = rl[:, :, 0:GROUPS]
            link(dve.tensor_reduce(gmx, gl, AX.X, ALU.max))
            link(dve.tensor_tensor(geq, gl, over(gmx, 4), ALU.is_equal))
            dve.tensor_tensor(gex, gl, over(gmx, 4), ALU.subtract).then_inc(exp_in, 1)
            link(dve.tensor_tensor(gc, geq, repeat(C("iota_low")[:, 0:4], TT), ALU.mult))
            link(dve.tensor_reduce(gidx, gc, AX.X, ALU.min))
            link(dve.tensor_tensor(geq, repeat(C("iota_low")[:, 0:4], TT), over(gidx, 4), ALU.is_equal))
            link(dve.tensor_scalar(gc, geq, -NEG, NEG, ALU.mult, ALU.add))
            for t in range(TT):
                ins = dve.tensor_tensor(cols(el[:, t, :], GROUPS), cols(rl[:, t, GROUPS:36], GROUPS),
                                        over(gc[:, t, :], PER_GROUP), ALU.add)
            link(ins)

            def pick(vals, mx, oh):
                link(dve.tensor_reduce(mx, vals, AX.X, ALU.max))
                link(dve.tensor_tensor(eq, vals, over(mx, EXPERTS), ALU.is_equal))
                link(dve.tensor_tensor(cand, eq, repeat(C("iota_low"), TT), ALU.mult))
                link(dve.tensor_reduce(i1, cand, AX.X, ALU.min))
                link(dve.tensor_tensor(oh, repeat(C("iota_low"), TT), over(i1, EXPERTS), ALU.is_equal))

            pick(el, m1, oh1)
            link(dve.scalar_tensor_tensor(el2, oh1, 2 * NEG, el, ALU.mult, ALU.add))
            pick(el2, m2, oh2)
            dve.tensor_tensor(m2, m2, m1, ALU.subtract).then_inc(exp_in, 1)
            dve.wait_ge(exp_in, 2)
            dve.tensor_tensor(msel, oh1, oh2, ALU.add).then_inc(msel_ready, 1)
            dve.wait_ge(exp_out, 1)
            link(dve.tensor_reduce(gsum, gex, AX.X, ALU.add))
            dve.wait_ge(exp_out, 2)
            link(dve.tensor_scalar(w1, m2, 1.0, None, ALU.add))
            link(dve.tensor_tensor(w1, w1, gsum, ALU.mult))
            link(dve.reciprocal(w1, w1))
            link(dve.tensor_tensor(w2, w1, m2, ALU.mult))
            link(dve.tensor_tensor(oh1, oh1, over(w1, EXPERTS), ALU.mult))
            link(dve.tensor_tensor(oh2, oh2, over(w2, EXPERTS), ALU.mult))
            link(dve.tensor_tensor(wsel, oh1, oh2, ALU.add))
            dve.wait_ge(rank_ps, 1)
            link(dve.scalar_tensor_tensor(rk, cols(banks[5][:, 0:64], 2), 1.0, msel, ALU.add, ALU.mult))
            link(dve.tensor_scalar(rk, rk, -1.0, None, ALU.add))
            link(dve.tensor_reduce(cmax, banks[5][:, 64:96], AX.X, ALU.max))
            link(dve.tensor_scalar(cpass, C("passes"), cmax[:, 0:1], None, ALU.is_lt))
            link(dve.tensor_reduce(cmax, cpass, AX.X, ALU.add))
            link(dve.tensor_scalar(cpass[:, 0:1], cmax, float(QUADS * RING), 1.0 - RING, ALU.mult, ALU.add))
            dve.tensor_copy(counts_i[:, 0:1], cmax)
            dve.tensor_copy(counts_i[:, 1:2], cpass[:, 0:1]).then_inc(npass_ready, 1)
            dve.wait_ge(npass_ready, 1)
            npass = dve.value_load(counts_i[0:1, 0:1], min_val=1, max_val=S // SLOTS)

            dve.sem_inc(xg_ready, 2)
            dve.sem_inc(hid_ready, 4)
            dve.sem_inc(dn1_ready, 1)
            with dve.Fori(0, npass) as r:
                dve.wait_ge(scatter_ps, r * QUADS + 1)
                for e0, e1 in ((0, QUAD), (QUAD, EXPERTS)):
                    for t in range(TT):
                        ins = dve.tensor_tensor(cols(sel[:, t, SLOTS * e0:SLOTS * e1], e1 - e0),
                                                repeat(iota32, e1 - e0), over(rk[:, t, e0:e1], SLOTS), ALU.is_equal)
                    ins.then_inc(pass_step if e0 else sel0_ready, 1)
                dve.wait_ge(pass_step, r * 2 + 1)
                dve.tensor_scalar(rk, rk, -float(SLOTS), None, ALU.add).then_inc(pass_step, 1)
                with dve.Fori(0, QUADS) as g:
                    q = r * QUADS + g
                    for b in range(2):
                        dve.wait_ge(gather_ps, q * 2 + (b + 1))
                        dve.tensor_tensor(xg[:, 4 * b:4 * b + 4, :], cols(banks[4 + b][:, :], 4),
                                          over(g2[:, 4 * b:4 * b + 4], P), ALU.mult).then_inc(xg_ready, 1)
                    dve.wait_ge(pass_step, r * 2 + 2)
                    dve.wait_ge(selT_ps, q + 1)
                    for t in range(TT):
                        ins = dve.tensor_tensor(cols(selw_q[:, t, :], QUAD), cols(sel[:, t, bass.ds(g * P, P)], QUAD),
                                                over(wsel[:, t, bass.ds(g * QUAD, QUAD)], SLOTS), ALU.mult)
                    ins.then_inc(selw_ready, 1)
                    for e in range(QUAD):
                        dve.wait_ge(silu_ready, q * QUAD + (e + 1))
                        dve.tensor_tensor(hid[:, e, :], banks[4 + e % 2][:, 64:128], sg[:, e, :], ALU.mult)\
                           .then_inc(hid_ready, 1)
                    dve.wait_ge(used_e, q * RING + RING)
                    dve.tensor_copy(dn[:, 512:1024], banks[7][:, :]).then_inc(dn1_ready, 1)
            dve.wait_ge(scatter_ps, npass * QUADS + 1)
            for half in range(2):
                for t in range(TT):
                    dve.tensor_copy(x[:, t, 512 * half:512 * half + 512], banks[2 * t + half][:, :])\
                       .then_inc(x_ready, 1)
            dve.wait_ge(x_ready, 8)

            def normed_y(k):
                c, g = k // 4, k % 4
                y = ym[:, c, 512 * g:512 * g + 512]
                dve.wait_ge(rsy_ready, c + 1)
                dve.tensor_scalar(y, y, rsy[:, k:k + 1], math.sqrt(512.0), ALU.mult, ALU.mult).then_inc(yn_ready, 1)

            def turned_y(j):
                c, g = j // 4, j % 4
                dve.wait_ge(yT_ps, j + 1)
                dve.tensor_tensor(yT[:, 4 * g:4 * g + 4, P * c:P * c + P], cols(banks[6 + j % 2][:, :], 4),
                                  over(gcol[:, 48 + 4 * g:52 + 4 * g], P), ALU.mult).then_inc(yT_ready, 1)

            def low_y(j):
                c, g = j // 4, j % 4
                at = (slice(None), slice(4 * g, 4 * g + 4), slice(P * c, P * c + P))
                dve.wait_ge(yT_hi_ready, j + 1)
                dve.tensor_tensor(yT_lo[at], yT[at], yT_hi[at].bitcast(F32), ALU.subtract).then_inc(yT_lo_ready, 1)

            norm(2)
            lo(0)
            turn(3, G("m_norm"), split=True)
            lo(1, 2, 3)
            dve.wait_ge(dt_ps, 1)
            link(dve.tensor_tensor(dtb, cols(banks[4][:, 0:64], 2), repeat(headp[:, 0, :], TT), ALU.add))
            dve.scalar_tensor_tensor(dta, dtb, -1.0, dtb, ALU.mult, ALU.max).then_inc(softplus_in, 1)
            dve.wait_ge(softplus_out, 1)
            dve.tensor_scalar(dtw, dtu, 1.0, None, ALU.add).then_inc(softplus_in, 1)
            dve.wait_ge(softplus_in, 2)
            link(dve.tensor_scalar(dtv, dtw, -1.0, None, ALU.add))
            link(dve.tensor_scalar(dtq, dtv, 0.0, None, ALU.is_equal))
            link(dve.tensor_tensor(dtv, dtv, dtq, ALU.add))
            link(dve.reciprocal(dtv, dtv))
            link(dve.tensor_tensor(dtv, dtv, dtu, ALU.mult))
            link(dve.tensor_tensor(dtq, dtq, dtu, ALU.mult))
            dve.wait_ge(softplus_out, 2)
            link(dve.tensor_tensor(dtv, dtv, dtl, ALU.mult))
            link(dve.tensor_tensor(dtv, dtv, dtq, ALU.add))
            link(dve.scalar_tensor_tensor(dtb, dtb, 0.0, dtv, ALU.max, ALU.add))
            dve.wait_ge(a_ready, 1)
            dve.scalar_tensor_tensor(dtA, dtb, -1.0, repeat(negA, TT), ALU.mult, ALU.mult).then_inc(dtA_ready, 1)

            def conv(ci):
                dve.wait_ge(tap_ready, ci + 1)
                c = XBC_ORDER[ci]
                for tap in range(CONV_K - 2, -1, -1):
                    lag = CONV_K - 1 - tap
                    for k in range(4):
                        tile = 4 * c + k
                        src = banks[2 * (ci % 2) + k // 2][:, 256 * (k % 2):256 * (k % 2) + 256 - lag]
                        w = ccol[:, 24 * tap + tile:24 * tap + tile + 1]
                        v = xc[:, tile, lag:]
                        ins = dve.scalar_tensor_tensor(v, src, w, v, ALU.mult, ALU.add)
                    if tap:
                        link(ins)
                ins.then_inc(conv_done, 1)
                lo(2 * ci + 4, 2 * ci + 5)

            conv(0)
            conv(1)
            dve.wait_ge(cum_ps, 1)
            link(dve.tensor_copy(acum, cols(banks[5][:, 0:64], 2)))
            dve.tensor_tensor(toend, banks[5][:, 64:96], acum[:, 0, :], ALU.subtract).then_inc(acum_ready, 1)
            for ci in range(2, 6):
                conv(ci)
            lo(16)

            def y_out(k):
                c, g = k // 4, k % 4
                y = ym[:, c, 512 * g:512 * g + 512]
                dve.wait_ge(intra_ps, k + 1)
                dve.wait_ge(xd_ready, k + 1)
                if c == 0:
                    dve.tensor_tensor(y, banks[4][:, :], y, ALU.add).then_inc(ysum_ready, 1)
                    return
                link(dve.tensor_tensor(y, banks[4][:, :], y, ALU.add))
                link(dve.tensor_tensor(cols(xdte, 8), cols(banks[5][:, :], 8),
                                       over(ea[:, 8 * g:8 * g + 8], HD), ALU.mult))
                dve.tensor_tensor(y, y, xdte, ALU.add).then_inc(ysum_ready, 1)

            for k in range(8):
                c, g = k // 4, k % 4
                dve.wait_ge(xT_ps, k + 1)
                dve.wait_ge(xt_ready, k + 1)
                if k >= 2:
                    dve.wait_ge(intra_ps, k - 1)
                    if c == 0 or k - 2 < 4:
                        dve.wait_ge(xdte_ready, min(k - 1, 4))
                dve.tensor_tensor(cols(xdt[:, k % 2, :], 8), cols(banks[k % 2][:, :], 8),
                                  over(dtb[:, c, 8 * g:8 * g + 8], HD), ALU.mult).then_inc(xdt_ready, 1)
                for b in range(2):
                    dve.wait_ge(rows_ps, 2 * k + b + 1)
                    for i in range(4):
                        h = 8 * g + 4 * b + i
                        ins = dve.scalar_tensor_tensor(
                            seg[:, k % 2, 512 * b + P * i:512 * b + P * i + P], banks[2 + b][:, P * i:P * i + P],
                            acum[:, c, h:h + 1], C("segmask"), ALU.subtract, ALU.add)
                    ins.then_inc(seg_ready, 1)
                if k >= 1:
                    y_out(k - 1)
                    lo(16 + k)
            for k in range(4):
                normed_y(k)
            y_out(7)
            for k in range(8):
                if k == 4:
                    for i in range(4, 8):
                        normed_y(i)
                turned_y(k)
                if k >= 1:
                    low_y(k - 1)
            low_y(7)
            lo(*range(H_MOUT + 4, H_MOUT + 7))
            add_product(0, 0, used_b, AT_MOUT + 4)
            lo(H_MOUT + 7, H_PLE0)

            def gated(i, c):
                for t in range(TT):
                    dve.wait_ge(sig_ready, 4 * i + 2 * c + t + 1)
                    link(dve.tensor_tensor(pret[:, t, :], banks[4 + 2 * c + t][:, :], sig[:, t, :], ALU.mult))
                    xv = x[:, t, 512 * c:512 * c + 512]
                    dve.tensor_tensor(xv, xv, pret[:, t, :], ALU.add).then_inc(x_ready, 1)

            turn(4, G("ple0"), split=True, halves=(0,))
            lo(H_PLE0 + 1, H_PLE0 + 2)
            add_product(1, 2, used_b, AT_MOUT + 8)
            turn(4, G("ple0"), split=True, halves=(1,))
            lo(H_PLE0 + 3, H_KV)
            gated(0, 0)

            lo(H_KV + 1)
            turn(5, G("kv"), second=G("s_norm"), split=True, bank0=4, halves=(0,))
            lo(H_KV + 2)
            gated(0, 1)
            turn(5, G("kv"), second=G("s_norm"), split=True, bank0=4, halves=(1,))
            lo(H_KV + 3)
            for n in range(4):
                half, t = n // 2, n % 2
                at = (slice(None), slice(4 * half, 4 * half + 4), slice(P * t, P * t + P))
                dve.wait_ge(hi_turned2, n + 1)
                dve.tensor_tensor(hT2_lo[at], hT2[at], hT2_hi[at].bitcast(F32), ALU.subtract).then_inc(lo_turned2, 1)
            link(dve.memset(ga[:, 0:4], 1.0))
            link(dve.memset(mask3, 0.0))
            for at in (0, 256):
                link(dve.tensor_copy(mask3[:, at:at + P], C("strictmask")))
            project(["qk", "qk", "v", "v", "qk", "qk", "gate", "gate"], projb_act, projb_dve,
                    qkTb_ps, sq_b, qk_b, hss_b, hrs_b, hssb_ready, hrsb_ready, H_KV)

            def softplus(h):
                dve.wait_ge(ln_ready, h + 1)
                if h >= 2:
                    dve.wait_ge(suf_ps, h - 1)
                link(dve.scalar_tensor_tensor(spz[:, h % 2, :], banks[h % 4][:, 0:384], 0.0, lnz[:, h % 2, :],
                                              ALU.max, ALU.add))
                v = spz[:, h % 2, :].rearrange("p (a b) -> p a b", a=3)[:, 0:3:2, :]
                dve.tensor_tensor(v, v, repeat(C("tri_lt"), 2), ALU.mult).then_inc(sp_ready, 1)

            def mask(h):
                dve.wait_ge(suf_ps, h + 1)
                if h >= 2:
                    dve.wait_ge(ob_ps, h - 1)
                dve.tensor_tensor(wz[:, h % 2, :], banks[h % 4][:, 0:384], mask3, ALU.add).then_inc(wm_ready, 1)

            def take(h):
                dve.wait_ge(ob_ps, h + 1)
                dve.wait_ge(projb_act, 16)
                for t in range(TT):
                    ins = dve.tensor_tensor(o_b[:, t, HD * h:HD * h + HD], banks[4 + h % 2][:, HD * t:HD * t + HD],
                                            gate_b[:, t, HD * h:HD * h + HD], ALU.mult)
                ins.then_inc(o_ready, 1)

            for h in range(SB_HEADS):
                softplus(h)
                if h >= 1:
                    mask(h - 1)
                if h >= 3:
                    take(h - 3)
                if h == 4:
                    lo(H_SOUT + 3)
                if h == 13:
                    turn(6, ga, split=False, halves=(0,))
                if h == 15:
                    low(6, 0)
                    low(6, 1)
            mask(SB_HEADS - 1)
            take(SB_HEADS - 3)
            take(SB_HEADS - 2)
            take(SB_HEADS - 1)
            turn(6, ga, split=True, halves=(1,))
            lo(H_PLE1)
            add_product(0, 0, used_b, AT_SOUT + 2)
            lo(H_PLE1 + 1)
            turn(7, G("ple1"), split=True, halves=(0,))
            lo(H_PLE1 + 2)
            add_product(1, 2, used_b, AT_SOUT + 4)
            turn(7, G("ple1"), split=True, halves=(1,))
            lo(H_PLE1 + 3)
            gated(1, 0)
            gated(1, 1)

        @block.tensor
        def _(pe):
            ident = C("ident")

            def turn(i, wait, src=hn, bank0=6, halves=(0, 1)):
                for n in range(2 * halves[0], 2 * halves[-1] + 2):
                    half, t = n // 2, n % 2
                    pe.wait_ge(*wait(n))
                    if n >= 2 or i >= 1:
                        pe.wait_ge(turned, 4 * i + n - 1)
                    if i == 5 and n >= 2:
                        pe.wait_ge(turned2, n - 1)
                    for k in range(4):
                        kt = 4 * half + k
                        ins = pe.transpose(banks[bank0 + n % 2][:, P * k:P * k + P],
                                           src[:, t, P * kt:P * kt + P], ident)
                    ins.then_inc(turn_ps, 1)

            def product(hi, low, bank0, u0, n_units, ready=None, n_kt=None, kt0=0, of=WeightsB,
                        middle=None, tiles=range(TT), done=True):
                n_kt = n_kt or 4 * n_units
                for i in range(n_units):
                    h = of.split.index(u0 + i)
                    pe.wait_ge(of.lo_ready, h + 1)
                    if ready is not None:
                        pe.wait_ge(ready[0], ready[1] + 2 * i + 2)
                    wh, wl = cols(w_hi(h), 4), cols(ring_r[:, of.slot(u0 + i), :], 4)
                    for t in tiles:
                        if t == 1 and middle is not None:
                            middle()
                        for k in range(4):
                            kt = kt0 + 4 * i + k
                            a, b = hi[:, kt, P * t:P * t + P], low[:, kt, P * t:P * t + P]
                            pe.matmul(banks[bank0 + t][:, :], a, wh[:, k, :], start=kt == 0, stop=False)
                            pe.matmul(banks[bank0 + t][:, :], a, wl[:, k, :], start=False, stop=False)
                            ins = pe.matmul(banks[bank0 + t][:, :], b, wh[:, k, :], start=False,
                                            stop=kt == n_kt - 1)
                    if done:
                        ins.then_inc(of.used, 1)

            pe.wait_ge(const_loaded, 16)
            pe.wait_ge(rows_loaded, 16 * ROW_LOADS)
            pe.transpose(banks[4][:, 0:103], rows_a[0:103, :], ident[0:103, 0:103]).then_inc(gains_ps, 1)
            pe.transpose(banks[5][:, 0:96], rows_c[0:96, :], ident[0:96, 0:96]).then_inc(gains_ps, 1)
            turn(0, lambda n: (x_loaded, 16 * TT), src=x, halves=(0,))

            def bias_rows():
                pe.wait_ge(tab_loaded, 32)
                pe.wait_ge(ones_set, 1)
                pe.wait_ge(turned, 4)
                pe.matmul(banks[7][0:UNITS, 0:384], tab[0:BUCKETS + 1, :], onehot[0:BUCKETS + 1, :],
                          start=True, stop=True).then_inc(u_ps, 1)


            def project(kinds, multiply, c_act, c_dve, t_ps, t_ready, qk):
                j = 0
                pend = None
                n_qk = [sum(k == "qk" for k in kinds[:c + 1]) for c in range(len(kinds))]

                def turn_qk(jj):
                    for t in range(TT):
                        pe.wait_ge(c_dve, 2 * jj + t + 1)
                        if jj >= 1:
                            pe.wait_ge(t_ready, 2 * (jj - 1) + t + 1)
                        for p in range(4):
                            ins = pe.transpose(banks[4 + t][:, P * p:P * p + P], qk[:, jj % 2, t, P * p:P * p + P],
                                               ident)
                        ins.then_inc(t_ps, 1)

                for c, kind in enumerate(kinds):
                    if c >= 2:
                        pe.wait_ge(c_act, 2 * (c - 1))
                        if n_qk[c - 2]:
                            pe.wait_ge(c_dve, 2 * n_qk[c - 2])
                    multiply(c, 2 * (c % 2))
                    if pend is not None:
                        turn_qk(pend)
                        pend = None
                    if kind == "qk":
                        pend = j
                        j += 1
                if pend is not None:
                    turn_qk(pend)

            def multiply_a(c, bank0):
                if c == 0:
                    product(hT_hi, hT_lo, bank0, 0, 1, ready=(lo_turned, 0), n_kt=KT, of=WeightsA,
                            middle=lambda: turn(0, lambda n: (x_loaded, 16 * TT), src=x, halves=(1,)))
                    product(hT_hi, hT_lo, bank0, 1, 1, ready=(lo_turned, 2), n_kt=KT, kt0=4, of=WeightsA)
                else:
                    product(hT_hi, hT_lo, bank0, 2 * c, 1, n_kt=KT, of=WeightsA,
                            middle=bias_rows if c == 1 else None)
                    product(hT_hi, hT_lo, bank0, 2 * c + 1, 1, n_kt=KT, kt0=4, of=WeightsA)

            project(["qk", "qk", "v", "qk", "qk", "v"], multiply_a,
                    proj_act, proj_dve, qkT_ps, qkT_ready, qk_a)

            pe.wait_ge(hank_lo_ready, 1)
            pe.wait_ge(proj_act, 12)
            pe.wait_ge(proj_dve, 8)
            pe.wait_ge(qkT_ready, 8)

            def logits(u):
                for m in maps_of(u):
                    if m >= 4:
                        pe.wait_ge(probs_ready, m - 3)
                    r0, pair, bank = HD * (m % 2), m // 2, banks[LOGIT_BANKS[m % 4]]
                    for t, lo, hi in ((0, 0, 128), (1, 128, 384)):
                        n = hi - lo
                        pe.matmul(bank[:, lo:hi], qT_a[r0:r0 + HD, pair, P * t:P * t + P],
                                  kT_a[r0:r0 + HD, pair, 0:n], start=True, stop=False)
                        pe.matmul(bank[:, lo:hi], flip_r, hank_hi[:, u, 256 - n:256], start=False, stop=False)
                        ins = pe.matmul(bank[:, lo:hi], flip_r, hank_lo[:, u, 256 - n:256], start=False, stop=True)
                    ins.then_inc(logits_ps, 1)

            logits(0)
            logits(1)
            for u in range(UNITS + 1):
                if u + 2 < UNITS:
                    logits(u + 2)
                if u < UNITS:
                    pe.wait_ge(w_ready, u + 1)
                    pe.wait_ge(probs_ready, maps_of(u)[0] + 1)
                    if u >= 2:
                        pe.wait_ge(wT_ready, u - 1)
                    m, bank = maps_of(u)[0], banks[3 + u % 2]
                    for i in range(3):
                        ins = pe.transpose(bank[:, P * i:P * i + P], probs[:, m % 4, P * i:P * i + P], ident)
                    ins.then_inc(wT_ps, 1)
                if u >= 1:
                    v = u - 1
                    pe.wait_ge(wT_ready, v + 1)
                    if v >= 2:
                        pe.wait_ge(y_ready, v - 1)
                    bank, w = banks[5 + v % 2], wT[:, v % 2, :]
                    at, n = (128 * v, 128) if v < DIFF_HEADS else (512 + HD * (v - DIFF_HEADS), HD)
                    pe.matmul(bank[:, 0:n], w[:, 0:128], v_a[:, 0, at:at + n], start=True, stop=True)
                    pe.matmul(bank[:, 128:128 + n], w[:, 128:256], v_a[:, 0, at:at + n], start=True, stop=False)
                    pe.matmul(bank[:, 128:128 + n], w[:, 256:384], v_a[:, 1, at:at + n], start=False, stop=True)\
                      .then_inc(pv_ps, 1)
            turn(1, lambda n: (y_ready, DIFF_HEADS), bank0=3, halves=(0,))
            product(hT_hi, hT_lo, 0, 12, 1, ready=(lo_turned, 4), n_kt=KT, of=WeightsA,
                    middle=lambda: turn(1, lambda n: (y_ready, UNITS), bank0=3, halves=(1,)))
            product(hT_hi, hT_lo, 0, 13, 1, ready=(lo_turned, 6), n_kt=KT, kt0=4, of=WeightsA)
            product(hT_hi, hT_lo, 2, 14, 1, n_kt=KT, of=WeightsA)
            turn(2, lambda n: (x_ready, n + 1), src=x, halves=(0,))
            product(hT_hi, hT_lo, 2, 15, 1, n_kt=KT, kt0=4, of=WeightsA)
            pe.wait_ge(small_loaded, 16 * SMALL_LOADS)
            for half in range(2):
                if half == 1:
                    turn(2, lambda n: (x_ready, n + 1), src=x, halves=(1,))
                pe.wait_ge(turned, 10 + 2 * half)
                for t in range(TT):
                    for kt in range(4 * half, 4 * half + 4):
                        ins = pe.matmul(banks[4 + t][:, 0:36], xT[:, kt, P * t:P * t + P], wr[:, kt, :],
                                        start=kt == 0, stop=kt == KT - 1)
            ins.then_inc(router_ps, 1)
            for t in range(TT):
                for half in range(2):
                    pe.matmul(banks[2 * t + half][:, :], ident, x[:, t, 512 * half:512 * half + 512],
                              start=True, stop=True)
            pe.wait_ge(msel_ready, 1)
            b = banks[5]
            pe.matmul(b[:, 0:32], C("tri_lt"), msel[:, 0, :], start=True, stop=True)
            pe.matmul(b[:, 32:64], C("ones"), msel[:, 0, :], start=True, stop=False)
            pe.matmul(b[:, 32:64], C("tri_lt"), msel[:, 1, :], start=False, stop=True)
            pe.matmul(b[:, 64:96], C("ones"), msel[:, 0, :], start=True, stop=False)
            pe.matmul(b[:, 64:96], C("ones"), msel[:, 1, :], start=False, stop=True).then_inc(rank_ps, 1)

            pe.wait_ge(hn_ready, 2)
            pe.wait_ge(npass_ready, 1)
            npass = pe.value_load(counts_i[0:1, 0:1], min_val=1, max_val=S // SLOTS)
            pe.sem_inc(fold_ps, 4)
            pe.sem_inc(scatter_ps, 1)
            pe.sem_inc(selT_ps, 1)
            with pe.Fori(0, npass) as r:
                with pe.Fori(0, QUADS // 2) as pair_i:
                    pair = r * (QUADS // 2) + pair_i
                    for odd in range(2):
                        q = pair * 2 + odd
                        pe.wait_ge(sel0_ready, r + 1)
                        pe.wait_ge(hid_ready, q * QUAD + 4)
                        for b in range(2):
                            for k in range(4):
                                kt = 4 * b + k
                                for t in range(TT):
                                    ins = pe.matmul(banks[4 + b][:, P * k:P * k + P], hn[:, t, P * kt:P * kt + P],
                                                    sel[:, t, bass.ds(pair_i * (2 * P) + odd * P, P)], start=t == 0, stop=t == 1)
                            ins.then_inc(gather_ps, 1)
                        pe.wait_ge(xg_ready, q * 2 + 4)
                        pe.wait_ge(dn0_ready, q + 1)
                        pe.wait_ge(dn1_ready, q + 1)

                        def unit_full(j):
                            if j >= EXTRA:
                                pe.wait_ge(full_a[e_slot(j)], q * 16 + e_full(e_slot(j)))
                            elif odd:
                                pe.wait_ge(full_x[j], pair * 16 + 16)
                            else:
                                pe.wait_ge(full_a[e_slot(j)], pair * 16 + e_full(e_slot(j)))

                        def fold(e):
                            pe.wait_ge(h_ready, q * QUAD + (e + 5))
                            if e >= 2:
                                pe.wait_ge(hid_ready, q * QUAD + (e + 3))
                            for i in range(4):
                                at = 256 * (i // 2) + i % 2
                                ins = pe.matmul(banks[4 + e % 2][:, SLOTS * i:SLOTS * i + SLOTS],
                                                hpre[:, e % 2, at:256 * (i // 2) + 256:2], C("fold"),
                                                start=True, stop=True)
                            ins.then_inc(fold_ps, 1)

                        for e in range(QUAD):
                            if e >= 2:
                                pe.wait_ge(h_ready, q * QUAD + (e + 3))
                            for i in range(2):
                                unit_full(2 * e + i)
                                w = cols(e_view(2 * e + i, odd), KT)
                                for kt in range(KT):
                                    c0 = SLOTS * (kt % 4)
                                    ins = pe.matmul(banks[6 + e % 2][c0:c0 + SLOTS, 256 * i:256 * i + 256],
                                                    xg[:, kt, SLOTS * e:SLOTS * e + SLOTS], w[:, kt, :],
                                                    start=kt < 4, stop=kt >= 4)
                                ins.then_inc(used_e, 1)
                            if e == 1:
                                pe.wait_ge(selw_ready, q + 1)
                                for t in range(TT):
                                    ins = pe.transpose(banks[5][:, 256 + P * t:256 + P * t + P], selw_q[:, t, :], ident)
                                ins.then_inc(selT_ps, 1)
                            if e == 2:
                                pe.wait_ge(selq_ready, q + 1)
                            if e >= 1:
                                fold(e - 1)
                        fold(3)
                        for e in range(QUAD):
                            unit_full(8 + e)
                        pe.wait_ge(hid_ready, q * QUAD + 8)
                        for half in range(2):
                            for f in range(2):
                                for e in range(QUAD):
                                    w = cols(ring[:, e_slot(8 + e), :], 2)
                                    ins = pe.matmul(banks[6 + half][SLOTS * e:SLOTS * e + SLOTS, :],
                                                    hid[:, e, SLOTS * f:SLOTS * f + SLOTS],
                                                    w[:, f, 512 * half:512 * half + 512],
                                                    start=f == 0, stop=f == 1)
                                    if half == 1 and f == 1:
                                        ins.then_inc(used_e, 1)
                                    elif half == 0 and f == 1 and e == 3:
                                        ins.then_inc(dn0_ps, 1)
                        for half in range(2):
                            pe.wait_ge((dn0_ready, dn1_ready)[half], q + 2)
                            for t in range(TT):
                                ins = pe.matmul(banks[2 * t + half][:, :], selwT_q[:, P * t:P * t + P],
                                                dn[:, 512 * half:512 * half + 512], start=False, stop=False,
                                                skip_group_check=True)
                        ins.then_inc(scatter_ps, 1)

            turn(3, lambda n: (hn_ready, n % 2 + 3))
            pe.wait_ge(lo_turned, 12)
            for t in range(TT):
                for kt in range(KT):
                    for i, part in enumerate((hT_hi, hT_lo)):
                        ins = pe.matmul(banks[4][:, 32 * t:32 * t + 32], part[:, kt, P * t:P * t + P].bitcast(F32),
                                        wdt[:, kt, :], start=kt == 0 and i == 0, stop=kt == KT - 1 and i == 1)
            ins.then_inc(dt_ps, 1)
            for ci in range(6):
                if ci >= 2:
                    pe.wait_ge(conv_done, ci - 1)
                pe.wait_ge(lo_w, 2 * ci + 2)
                for k in range(4):
                    bank = banks[2 * (ci % 2) + k // 2][:, 256 * (k % 2):256 * (k % 2) + 256]
                    for kt in range(KT):
                        u = 2 * ci + kt // 4
                        wh = cols(w_hi(u), 4)[:, kt % 4, P * k:P * k + P]
                        wl = cols(ring_r[:, b_slot(u), :], 4)[:, kt % 4, P * k:P * k + P]
                        pe.matmul(bank, wh, hT_hi[:, kt, :], start=kt == 0, stop=False)
                        pe.matmul(bank, wh, hT_lo[:, kt, :], start=False, stop=False)
                        ins = pe.matmul(bank, wl, hT_hi[:, kt, :], start=False, stop=kt == KT - 1)
                ins.then_inc(used_b, 2)
                if ci == 1:
                    pe.wait_ge(dtA_ready, 1)
                    b = banks[5]
                    for c in range(TT):
                        pe.matmul(b[:, 32 * c:32 * c + 32], C("tri_le"), dtA[:, c, :], start=True, stop=True)
                    pe.matmul(b[:, 64:96], C("ones"), dtA[:, 0, :], start=True, stop=True).then_inc(cum_ps, 1)
            pe.wait_ge(xc_ready, 2)
            for g in range(4):
                ins = pe.transpose(banks[4][:, P * g:P * g + P], xc[:, 16 + g, 0:P], ident)
            ins.then_inc(bt_ps, 1)
            for c in range(TT):
                for g in range(4):
                    ins = pe.matmul(banks[6 + c][:, P * g:P * g + P], xc[:, 16 + g, P * c:P * c + P],
                                    xc[:, 20 + g, P * c:P * c + P], start=True, stop=True)
                ins.then_inc(cb_ps, 1)
            pe.wait_ge(conv_done, 5)
            product(hT_hi, hT_lo, 0, AT_Z, 2)
            pe.wait_ge(xc_ready, 6)
            pe.wait_ge(z_ready, 2)
            pe.wait_ge(acum_ready, 1)
            pe.wait_ge(cb_ready, 2)

            def step_in(k):
                c, g = k // 4, k % 4
                if k >= 2:
                    pe.wait_ge(xdt_ready, k - 1)
                    pe.wait_ge(xt_ready, k - 1)
                for i in range(4):
                    ins = pe.transpose(banks[k % 2][:, P * i:P * i + P], xc[:, 4 * g + i, P * c:P * c + P], ident)
                ins.then_inc(xT_ps, 1)
                for b in range(2):
                    if k >= 1:
                        pe.wait_ge(seg_ready, 2 * k - 1 + b)
                    for i in range(4):
                        h = 8 * g + 4 * b + i
                        ins = pe.matmul(banks[2 + b][:, P * i:P * i + P], dtA[:, c, h:h + 1].to_broadcast([P, P]),
                                        C("tri_le"), start=True, stop=True)
                    ins.then_inc(rows_ps, 1)

            def step_out(k):
                c, g = k // 4, k % 4
                pe.wait_ge(xdt_ready, k + 1)
                pe.wait_ge(m_ready, 2 * k + 2)
                if k == 0:
                    pe.wait_ge(bt_ready, 1)
                if k >= 1:
                    pe.wait_ge(ysum_ready, k)
                    pe.wait_ge(state_ready, min(k, 4))
                if c == 0:
                    pe.wait_ge(xdte_ready, k + 1)
                    pe.matmul(banks[5][:, :], btok[:, P * g:P * g + P], xdte, start=True, stop=True)
                else:
                    pe.matmul(banks[5][:, :], xc[:, 20 + g, P:2 * P], state[:, 512 * g:512 * g + 512],
                              start=True, stop=True)
                for i in range(8):
                    ins = pe.matmul(banks[4][:, HD * i:HD * i + HD], seg[:, k % 2, P * i:P * i + P],
                                    xdt[:, k % 2, HD * i:HD * i + HD], start=True, stop=True)
                ins.then_inc(intra_ps, 1)

            step_in(0)
            for k in range(8):
                if k + 1 < 8:
                    step_in(k + 1)
                if k < 6:
                    c, half = 1 + k // 2, k % 2
                    if half == 0 and c >= 2:
                        pe.wait_ge(z_ready, 2 * c)
                    product(hT_hi, hT_lo, 6, AT_Z + 2 * c + half, 1, n_kt=KT, kt0=4 * half)
                step_out(k)
            pe.wait_ge(z_ready, 8)
            pe.wait_ge(seg_ready, 16)
            pe.wait_ge(xt_ready, 8)
            pe.wait_ge(xdt_ready, 8)

            def turn_y(k):
                c, g = k // 4, k % 4
                pe.wait_ge(yn_ready, k + 1)
                if k >= 2:
                    pe.wait_ge(yT_ready, k - 1)
                for i in range(4):
                    ins = pe.transpose(banks[6 + k % 2][:, P * i:P * i + P],
                                       ym[:, c, 512 * g + P * i:512 * g + P * i + P], ident)
                ins.then_inc(yT_ps, 1)

            for k in range(4):
                turn_y(k)
            for g in range(4):
                product(yT_hi, yT_lo, 0, AT_MOUT + g, 1, ready=(yT_lo_ready, g - 1), n_kt=16, kt0=4 * g,
                        tiles=[0], done=False)
                if g in (1, 2):
                    turn_y(2 * g + 2)
                    turn_y(2 * g + 3)
            for g in range(4):
                product(yT_hi, yT_lo, 0, AT_MOUT + g, 1, ready=(yT_lo_ready, 3 + g), n_kt=16, kt0=4 * g, tiles=[1])

            def turn_p(i):
                pe.wait_ge(p_loaded, 16 * (i + 1))
                for kp in range(2):
                    for t in range(TT):
                        ins = pe.transpose(banks[6][:, 256 * kp + P * t:256 * kp + P * t + P],
                                           pbuf[:, t, P * kp:P * kp + P], ident)
                ins.then_inc(pT_ps, 1)

            def embedding(i, at, x_from):
                base = 12 + 12 * i
                product(hT_hi, hT_lo, 0, at, 1, ready=(lo_turned, base), n_kt=KT,
                        middle=lambda: turn(4 + 3 * i, lambda n: (x_ready, x_from + n + 1), src=x, halves=(1,)))
                pe.wait_ge(*b_full(at + 1))
                w = cols(ring[:, b_slot(at + 1), :], 2)
                for c in range(2):
                    if c == 1:
                        pe.wait_ge(turned, 20 + 12 * i)
                    for t in range(TT):
                        for kp in range(2):
                            ins = pe.matmul(banks[4 + 2 * c + t][:, :], pT[:, kp, P * t:P * t + P],
                                            w[:, kp, 512 * c:512 * c + 512], start=kp == 0, stop=kp == 1)
                ins.then_inc(used_b, 1)
                product(hT_hi, hT_lo, 0, at + 2, 1, ready=(lo_turned, base + 2), n_kt=KT, kt0=4)

            pe.wait_ge(yT_ready, 8)
            turn_p(0)
            product(yT_hi, yT_lo, 2, AT_MOUT + 4, 2, n_kt=16)
            pe.wait_ge(pT_ready, 1)
            turn(4, lambda n: (x_ready, 8 + n + 1), src=x, halves=(0,))
            product(yT_hi, yT_lo, 2, AT_MOUT + 6, 2, n_kt=16, kt0=8)
            embedding(0, AT_PLE0, 8)
            product(hT_hi, hT_lo, 2, AT_PLE0 + 3, 1, n_kt=KT)
            turn(5, lambda n: (x_ready, 12 + n + 1), src=x, bank0=4, halves=(0,))
            product(hT_hi, hT_lo, 2, AT_PLE0 + 4, 1, n_kt=KT, kt0=4)

            def multiply(c, bank0):
                if c == 0:
                    product(hT_hi, hT_lo, bank0, AT_KV, 1, ready=(lo_turned, 16), n_kt=KT,
                            middle=lambda: turn(5, lambda n: (x_ready, 12 + n + 1), src=x, bank0=4, halves=(1,)))
                    product(hT_hi, hT_lo, bank0, AT_KV + 1, 1, ready=(lo_turned, 18), n_kt=KT, kt0=4)
                elif c < 4:
                    product(hT_hi, hT_lo, bank0, AT_KV + 2 * c, 2, ready=(lo_turned, 16))
                else:
                    product(hT2_hi, hT2_lo, bank0, AT_KV + 2 * c, 2, ready=(lo_turned2, 0))

            project(["qk", "qk", "v", "v", "qk", "qk", "gate", "gate"], multiply,
                    projb_act, projb_dve, qkTb_ps, qkTb_ready, qk_b)
            pe.wait_ge(projb_act, 16)
            pe.wait_ge(qkTb_ready, 8)

            def scores(h):
                if h >= 4:
                    pe.wait_ge(wm_ready, h - 3)
                r0, pair, bank = HD * (h % 2), h // 2, banks[h % 4]
                pe.matmul(bank[:, 0:256], kT_b[r0:r0 + HD, pair, 0:P], qT_b[r0:r0 + HD, pair, :],
                          start=True, stop=False, skip_group_check=True)
                pe.matmul(bank[:, 256:384], kT_b[r0:r0 + HD, pair, P:2 * P], qT_b[r0:r0 + HD, pair, P:2 * P],
                          start=False, stop=False, skip_group_check=True).then_inc(zz_ps, 1)

            def suffix(h):
                pe.wait_ge(sp_ready, h + 1)
                bank, sp_ = banks[h % 4], spz[:, h % 2, :]
                pe.matmul(bank[:, 128:256], C("negones"), sp_[:, 256:384], start=False, stop=False,
                          skip_group_check=True)
                pe.matmul(bank[:, 0:384], C("sufneg"), sp_, start=False, stop=True, skip_group_check=True)\
                  .then_inc(suf_ps, 1)

            def outputs(h):
                pe.wait_ge(we_ready, h + 1)
                if h >= 2:
                    pe.wait_ge(o_ready, h - 1)
                bank, w, at = banks[4 + h % 2], wz[:, h % 2, :], HD * h
                pe.matmul(bank[:, 0:HD], w[:, 0:128], v_b[:, 0, at:at + HD], start=True, stop=True)
                pe.matmul(bank[:, HD:2 * HD], w[:, 128:256], v_b[:, 0, at:at + HD], start=True, stop=False)
                pe.matmul(bank[:, HD:2 * HD], w[:, 256:384], v_b[:, 1, at:at + HD], start=False, stop=True)\
                  .then_inc(ob_ps, 1)

            scores(0)
            scores(1)
            for h in range(SB_HEADS):
                if h + 2 < SB_HEADS:
                    scores(h + 2)
                suffix(h)
                if h >= 2:
                    outputs(h - 2)
                if h == 12:
                    turn(6, lambda n: (o_ready, SB_HEADS // 2), halves=(0,))
            outputs(SB_HEADS - 2)
            outputs(SB_HEADS - 1)
            product(hT_hi, hT_lo, 0, AT_SOUT, 1, ready=(lo_turned, 20), n_kt=KT,
                    middle=lambda: turn(6, lambda n: (o_ready, SB_HEADS), halves=(1,)))
            product(hT_hi, hT_lo, 0, AT_SOUT + 1, 1, ready=(lo_turned, 22), n_kt=KT, kt0=4)
            pe.wait_ge(turned, 28)
            turn_p(1)
            product(hT_hi, hT_lo, 2, AT_SOUT + 2, 1, n_kt=KT)
            pe.wait_ge(pT_ready, 2)
            turn(7, lambda n: (x_ready, 16 + n + 1), src=x, halves=(0,))
            product(hT_hi, hT_lo, 2, AT_SOUT + 3, 1, n_kt=KT, kt0=4)
            embedding(1, AT_PLE1, 16)
            product(hT_hi, hT_lo, 2, AT_PLE1 + 3, 2)


INPUTS = ["x", "norm1_g", "w_in", "diff_q_g", "diff_k_g", "lambda_q1", "lambda_k1", "lambda_q2", "lambda_k2",
          "diff_sub_g", "moba_q_g", "moba_k_g", "rel_bias", "w_out", "norm2_g", "router_group",
          "router_expert", "w_gate", "w_up", "w_down", "p_2", "m_norm_2", "m_in_2", "m_conv_w_2",
          "m_conv_b_2", "m_dt_bias_2", "m_A_log_2", "m_D_2", "m_ynorm_2", "m_out_2", "kv_norm_2",
          "w_kv_2", "k_norm_2", "s_norm_2", "s_in_2", "q_norm_2", "s_out_2", "ple_norm_2",
          "ple_gate_2", "ple_proj_2"]


def kernel(**inputs):
    import concourse.bacc as bacc
    from concourse.bass_utils import run_bass_kernel_spmd

    nc = bacc.Bacc("TRN2", target_bir_lowering=False, num_devices=1)
    arrays = {f"in_{n}": np.ascontiguousarray(inputs[n]) for n in INPUTS}
    arrays["in_consts"] = constants()[0]
    arrays["in_onehot"] = bucket_onehot()
    d = {n[3:]: nc.dram_tensor(n, a.shape, F32, kind="ExternalInput").ap() for n, a in arrays.items()}
    out = nc.dram_tensor("out_dram", (1, S, D), F32, kind="ExternalOutput").ap()
    two_blocks(nc, d, out)
    r = run_bass_kernel_spmd(nc, [arrays], core_ids=[0])
    return r.results[0]["out_dram"]
```
